# Optimizing a Trainium2 kernel written in Bass

```python
import jax
import jax.numpy as jnp
from jax import lax
import numpy as np

D_MODEL = 1024
BATCH = 1
SEQ = 256
DEPTH = 2
DEC_BATCH = 8
DEC_SEQ = 1
PAST_LEN = 256
PAGE_SIZE = 128

D_POOL = D_MODEL // 2
POOL_WINDOWS = (2, 4, 8, 16)
POOL_GROUP = D_POOL // len(POOL_WINDOWS)
POOL_HIST = max(POOL_WINDOWS) - 1
D_CONV = D_MODEL // 2
CONV_WIDTH = 3
HEAD_DIM = 64
N_HEADS = D_MODEL // HEAD_DIM
N_KV = 4
GROUP = N_HEADS // N_KV
D_ATTN = N_HEADS * HEAD_DIM
D_KV = N_KV * HEAD_DIM
ROT_DIM = HEAD_DIM // 4
ROPE_THETA = 500000.0
CMP_LEN = 32
CMP_STRIDE = 16
SEL_LEN = 64
N_SEL = 8
WINDOW = 512
Q_BLOCK = 64
FORCE_SCORE = 1.0e4
LN_EPS = 1e-5
ALPHA = (2 * DEPTH) ** 0.25
BETA = (8 * DEPTH) ** -0.25
IN_SIZES = (D_POOL, D_POOL,
            D_CONV, D_CONV, D_CONV, D_CONV,
            D_ATTN, D_KV, D_KV, D_KV, D_KV, D_KV, D_KV, 3 * N_HEADS, D_ATTN,
            3 * D_MODEL)
D_IN = sum(IN_SIZES)

kernel_name = 'nsa_pool_conv_gated_hybrid_step'

def layer_norm(x, g, b):
    xf = x.astype(jnp.float32)
    mu = jnp.mean(xf, axis=-1, keepdims=True)
    var = jnp.mean(jnp.square(xf - mu), axis=-1, keepdims=True)
    return ((xf - mu) * lax.rsqrt(var + LN_EPS) * g + b).astype(x.dtype)

def masked_softmax(s, mask):
    s = jnp.where(mask, s.astype(jnp.float32), -jnp.inf)
    m = jnp.max(s, axis=-1, keepdims=True)
    m = jnp.where(jnp.isfinite(m), m, 0.0)
    e = jnp.where(mask, jnp.exp(s - m), 0.0)
    return e / jnp.maximum(jnp.sum(e, axis=-1, keepdims=True), 1e-30)

def partial_rope(x, pos):
    half = ROT_DIM // 2
    inv_freq = 1.0 / (ROPE_THETA ** (np.arange(0, ROT_DIM, 2, dtype=np.float32) / ROT_DIM))
    ang = jnp.asarray(pos, jnp.float32)[:, None] * jnp.asarray(inv_freq, jnp.float32)[None, :]
    cos = jnp.cos(ang)[:, None, :]
    sin = jnp.sin(ang)[:, None, :]
    xr = x[..., :ROT_DIM].astype(jnp.float32)
    x1, x2 = xr[..., :half], xr[..., half:]
    rot = jnp.concatenate([x1 * cos - x2 * sin, x2 * cos + x1 * sin], axis=-1)
    return jnp.concatenate([rot.astype(x.dtype), x[..., ROT_DIM:]], axis=-1)

def pool_mixer(u, hist, pos0, w_grp, scale):
    bn, t, _ = u.shape
    ext = jnp.concatenate([hist, u], axis=1).astype(jnp.float32)
    cs = jnp.cumsum(ext, axis=1)
    cs = jnp.concatenate([jnp.zeros_like(cs[:, :1]), cs], axis=1)
    upto = cs[:, POOL_HIST + 1:]
    pos = pos0 + np.arange(t, dtype=np.int32)
    means = []
    for g, w in enumerate(POOL_WINDOWS):
        ch = slice(g * POOL_GROUP, (g + 1) * POOL_GROUP)
        start = cs[:, POOL_HIST + 1 - w: POOL_HIST + 1 - w + t, ch]
        count = jnp.asarray(np.minimum(w, pos + 1), jnp.float32)[None, :, None]
        means.append((upto[..., ch] - start) / count)
    pooled = (jnp.concatenate(means, axis=-1) - ext[:, POOL_HIST:]).astype(u.dtype)
    pooled = pooled.reshape(bn, t, len(POOL_WINDOWS), POOL_GROUP)
    mixed = jnp.einsum('btgc,gcd->btgd', pooled, w_grp).reshape(bn, t, D_POOL)
    return mixed * scale

def short_conv(h, hist, w):
    t = h.shape[1]
    ext = jnp.concatenate([hist, h], axis=1)
    return sum(ext[:, j:j + t] * w[j] for j in range(CONV_WIDTH))

def compress(k, pe, wc):
    bn, total = k.shape[:2]
    reps = CMP_LEN // CMP_STRIDE
    n_cmp = (total - CMP_LEN) // CMP_STRIDE + 1
    n_chunk = total // CMP_STRIDE
    chunks = k[:, :n_chunk * CMP_STRIDE].reshape(bn, n_chunk, CMP_STRIDE, N_KV, HEAD_DIM)
    pe_r = pe.reshape(reps, CMP_STRIDE, 1, HEAD_DIM)
    w_r = wc.reshape(reps, CMP_STRIDE, HEAD_DIM, HEAD_DIM)
    return sum(jnp.einsum('bcsgh,she->bcge', chunks[:, r:r + n_cmp] + pe_r[r], w_r[r])
               for r in range(reps))

def cover_matrix(n_cmp, n_blk):
    c0 = np.arange(n_cmp)[:, None] * CMP_STRIDE
    s0 = np.arange(n_blk)[None, :] * SEL_LEN
    return ((c0 < s0 + SEL_LEN) & (c0 + CMP_LEN > s0)).astype(np.float32)

def nsa_block(blk, kc, vc, kc_end, ksb, vsb, cover):
    q, qpos, kw, vw, kwpos, gates = blk
    bn, qb = q.shape[:2]
    scale = HEAD_DIM ** -0.5
    qg = q.reshape(bn, qb, N_KV, GROUP, HEAD_DIM)
    s_c = jnp.einsum('bqgrh,bcgh->bqgrc', qg, kc) * scale
    vis_c = kc_end[None, :] <= qpos[:, None]
    p_c = masked_softmax(s_c, vis_c[None, :, None, None, :])
    o_c = jnp.einsum('bqgrc,bcgh->bqgrh', p_c.astype(vc.dtype), vc)
    imp = jnp.einsum('bqgrc,cj->bqgj', p_c, cover)
    n_blk = cover.shape[1]
    n_pick = min(N_SEL, n_blk)
    bidx = jnp.arange(n_blk)
    cur = qpos // SEL_LEN
    eligible = bidx[None, :] * SEL_LEN <= qpos[:, None]
    forced = (bidx[None, :] == 0) | (bidx[None, :] == cur[:, None]) | (bidx[None, :] == cur[:, None] - 1)
    score = jnp.where(forced[None, :, None, :], FORCE_SCORE,
                      jnp.where(eligible[None, :, None, :], imp, -jnp.inf))
    top_val, top_idx = lax.top_k(score, n_pick)
    valid = jnp.isfinite(top_val)
    gidx = jnp.transpose(top_idx, (0, 2, 1, 3)).reshape(bn, N_KV, qb * n_pick)
    b_ix = jnp.arange(bn)[:, None, None]
    g_ix = jnp.arange(N_KV)[None, :, None]
    ks = ksb[b_ix, g_ix, gidx].reshape(bn, N_KV, qb, n_pick * SEL_LEN, HEAD_DIM)
    vs = vsb[b_ix, g_ix, gidx].reshape(bn, N_KV, qb, n_pick * SEL_LEN, HEAD_DIM)
    kpos = (top_idx[..., None] * SEL_LEN + jnp.arange(SEL_LEN)).reshape(bn, qb, N_KV, n_pick * SEL_LEN)
    m_s = jnp.repeat(valid, SEL_LEN, axis=-1) & (kpos <= qpos[None, :, None, None])
    s_s = jnp.einsum('bqgrh,bgqkh->bqgrk', qg, ks) * scale
    p_s = masked_softmax(s_s, m_s[:, :, :, None, :])
    o_s = jnp.einsum('bqgrk,bgqkh->bqgrh', p_s.astype(vs.dtype), vs)
    m_w = (kwpos[None, :] <= qpos[:, None]) & (qpos[:, None] - kwpos[None, :] < WINDOW)
    s_w = jnp.einsum('bqgrh,bkgh->bqgrk', qg, kw) * scale
    p_w = masked_softmax(s_w, m_w[None, :, None, None, :])
    o_w = jnp.einsum('bqgrk,bkgh->bqgrh', p_w.astype(vw.dtype), vw)
    g = gates.reshape(bn, qb, N_KV, GROUP, 3)
    o = g[..., 0:1] * o_c + g[..., 1:2] * o_s + g[..., 2:3] * o_w
    return o.reshape(bn, qb, D_ATTN)

def nsa_mixer(q, kc_new, vc_new, ks_new, vs_new, kw_new, vw_new, gates, past, pos0, cmp_pe, cmp_w):
    kc_past, vc_past, ks_past, vs_past, kw_buf, vw_buf = past
    bn, t = q.shape[:2]
    total = pos0 + t
    qpos = pos0 + np.arange(t, dtype=np.int32)
    q = partial_rope(q, qpos)
    ks_new = partial_rope(ks_new, qpos)
    kw_new = partial_rope(kw_new, qpos)
    k_cmp_all = jnp.concatenate([kc_past, kc_new], axis=1)
    v_cmp_all = jnp.concatenate([vc_past, vc_new], axis=1)
    k_sel_all = jnp.concatenate([ks_past, ks_new], axis=1)
    v_sel_all = jnp.concatenate([vs_past, vs_new], axis=1)
    kc = compress(k_cmp_all, cmp_pe[0], cmp_w[0])
    vc = compress(v_cmp_all, cmp_pe[1], cmp_w[1])
    n_cmp = kc.shape[1]
    kc_end = np.arange(n_cmp, dtype=np.int32) * CMP_STRIDE + CMP_LEN - 1
    kc = partial_rope(kc, kc_end)
    n_blk = -(-total // SEL_LEN)
    pad = n_blk * SEL_LEN - total

    def to_blocks(a):
        a = jnp.pad(a, ((0, 0), (0, pad), (0, 0), (0, 0)))
        return a.reshape(bn, n_blk, SEL_LEN, N_KV, HEAD_DIM).transpose(0, 3, 1, 2, 4)

    ksb, vsb = to_blocks(k_sel_all), to_blocks(v_sel_all)
    cover = jnp.asarray(cover_matrix(n_cmp, n_blk))
    wb = kw_buf.shape[1]
    zpad = jnp.zeros((bn, WINDOW, N_KV, HEAD_DIM), kw_new.dtype)
    kw_all = jnp.concatenate([zpad, kw_buf, kw_new], axis=1)
    vw_all = jnp.concatenate([zpad.astype(vw_new.dtype), vw_buf, vw_new], axis=1)
    kw_pos = np.concatenate([np.full((WINDOW,), -WINDOW, np.int32),
                             pos0 - wb + np.arange(wb + t, dtype=np.int32)])
    qb = Q_BLOCK if t % Q_BLOCK == 0 else t
    nqb = t // qb
    band = np.arange(nqb)[:, None] * qb + wb + np.arange(WINDOW + qb)[None, :]

    def q_blocks(a):
        return jnp.moveaxis(a.reshape(bn, nqb, qb, *a.shape[2:]), 1, 0)

    xs = (q_blocks(q), jnp.asarray(qpos.reshape(nqb, qb)),
          jnp.moveaxis(kw_all[:, band], 1, 0), jnp.moveaxis(vw_all[:, band], 1, 0),
          jnp.asarray(kw_pos[band]), q_blocks(gates))
    kc_end_j = jnp.asarray(kc_end)
    o = lax.map(lambda blk: nsa_block(blk, kc, vc, kc_end_j, ksb, vsb, cover), xs)
    o = jnp.moveaxis(o, 0, 1).reshape(bn, t, D_ATTN)
    keep = min(WINDOW, total)
    new_state = (kc_new, vc_new, ks_new, vs_new, kw_all[:, -keep:], vw_all[:, -keep:])
    return o, new_state

def trunk_layer(x, pos0, hist, w_in, pool_w, pool_scale, conv_w, cmp_pe, cmp_w,
                proj_a, proj_b, proj_c, w_out, ln_g, ln_b):
    kc_past, vc_past, ks_past, vs_past, kw_buf, vw_buf, pool_hist, conv_hist = hist
    bn, t, _ = x.shape
    h = jnp.einsum('btd,de->bte', x, w_in)
    offs = np.cumsum(IN_SIZES)[:-1].tolist()
    (pu, pz, cb, cc, cx, cz, q, kc, vc, ks, vs, kw, vw, ng, az, mg) = jnp.split(h, offs, axis=-1)
    y_a = pool_mixer(pu, pool_hist, pos0, pool_w, pool_scale) * jax.nn.silu(pz)
    hc = cc * cx
    y_b = cb * short_conv(hc, conv_hist, conv_w) * jax.nn.silu(cz)
    kvh = lambda a: a.reshape(bn, t, N_KV, HEAD_DIM)
    gates = jax.nn.sigmoid(ng).reshape(bn, t, N_HEADS, 3)
    y_c, nsa_state = nsa_mixer(q.reshape(bn, t, N_HEADS, HEAD_DIM), kvh(kc), kvh(vc), kvh(ks), kvh(vs),
                               kvh(kw), kvh(vw), gates,
                               (kc_past, vc_past, ks_past, vs_past, kw_buf, vw_buf), pos0, cmp_pe, cmp_w)
    y_c = y_c * jax.nn.silu(az)
    g_a, g_b, g_c = jnp.split(jax.nn.sigmoid(mg), 3, axis=-1)
    merged = (g_a * jnp.einsum('btc,cd->btd', y_a, proj_a)
              + g_b * jnp.einsum('btc,cd->btd', y_b, proj_b)
              + g_c * jnp.einsum('btc,cd->btd', y_c, proj_c))
    y = jnp.einsum('btd,de->bte', merged, w_out)
    out = layer_norm(ALPHA * x + y, ln_g, ln_b)
    pool_new = jnp.concatenate([pool_hist, pu], axis=1)[:, -POOL_HIST:]
    conv_new = jnp.concatenate([conv_hist, hc], axis=1)[:, -(CONV_WIDTH - 1):]
    return out, nsa_state + (pool_new, conv_new)

def gather_pages(pool, page_table, past_len):
    return pool[page_table].reshape(page_table.shape[0], past_len, N_KV, HEAD_DIM)

def setup_inputs(seed: int = 0) -> dict:
    key = jax.random.key(seed)
    k = jax.random.split(key, 24)
    n_pages = PAST_LEN // PAGE_SIZE
    n_used = DEC_BATCH * n_pages
    n_pool = n_used + (n_used + 3) // 4
    win_rows = min(WINDOW, PAST_LEN)
    nrm = lambda kk, shape, s=1.0: s * jax.random.normal(kk, shape, jnp.float32)
    cache_shape = (DEPTH, n_pool, PAGE_SIZE, N_KV, HEAD_DIM)
    win_shape = (DEPTH, DEC_BATCH, win_rows, N_KV, HEAD_DIM)
    page_table = jax.random.permutation(k[6], n_pool)[:n_used].reshape(DEC_BATCH, n_pages).astype(jnp.int32)
    return {
        'x_prompt': nrm(k[0], (BATCH, SEQ, D_MODEL)),
        'x_sample': nrm(k[1], (DEC_BATCH, DEC_SEQ, D_MODEL)),
        'cache_k_cmp': nrm(k[2], cache_shape),
        'cache_v_cmp': nrm(k[3], cache_shape),
        'cache_k_sel': nrm(k[4], cache_shape),
        'cache_v_sel': nrm(k[5], cache_shape),
        'page_table': page_table,
        'state_k_win': nrm(k[7], win_shape),
        'state_v_win': nrm(k[8], win_shape),
        'state_pool': nrm(k[9], (DEPTH, DEC_BATCH, POOL_HIST, D_POOL)),
        'state_conv': nrm(k[10], (DEPTH, DEC_BATCH, CONV_WIDTH - 1, D_CONV)),
        'w_in': nrm(k[11], (DEPTH, D_MODEL, D_IN), D_MODEL ** -0.5),
        'pool_w': nrm(k[12], (DEPTH, len(POOL_WINDOWS), POOL_GROUP, POOL_GROUP), POOL_GROUP ** -0.5),
        'pool_scale': 1.0 + nrm(k[13], (DEPTH, D_POOL), 0.1),
        'conv_w': nrm(k[14], (DEPTH, CONV_WIDTH, D_CONV), CONV_WIDTH ** -0.5),
        'cmp_pe': nrm(k[15], (DEPTH, 2, CMP_LEN, HEAD_DIM), 0.1),
        'cmp_w': nrm(k[16], (DEPTH, 2, CMP_LEN * HEAD_DIM, HEAD_DIM), (CMP_LEN * HEAD_DIM) ** -0.5),
        'proj_a': nrm(k[17], (DEPTH, D_POOL, D_MODEL), BETA * D_POOL ** -0.5),
        'proj_b': nrm(k[18], (DEPTH, D_CONV, D_MODEL), BETA * D_CONV ** -0.5),
        'proj_c': nrm(k[19], (DEPTH, D_ATTN, D_MODEL), BETA * D_ATTN ** -0.5),
        'w_out': nrm(k[20], (DEPTH, D_MODEL, D_MODEL), BETA * D_MODEL ** -0.5),
        'ln_g': 1.0 + nrm(k[21], (DEPTH, D_MODEL), 0.02),
        'ln_b': nrm(k[22], (DEPTH, D_MODEL), 0.02),
    }

def reference(x_prompt, x_sample, cache_k_cmp, cache_v_cmp, cache_k_sel, cache_v_sel, page_table,
              state_k_win, state_v_win, state_pool, state_conv, w_in, pool_w, pool_scale, conv_w,
              cmp_pe, cmp_w, proj_a, proj_b, proj_c, w_out, ln_g, ln_b):
    bp = x_prompt.shape[0]
    past_len = page_table.shape[1] * cache_k_cmp.shape[2]
    dt = x_prompt.dtype
    empty_kv = jnp.zeros((bp, 0, N_KV, HEAD_DIM), dt)
    hist_prompt = (empty_kv, empty_kv, empty_kv, empty_kv, empty_kv, empty_kv,
                   jnp.zeros((bp, POOL_HIST, D_POOL), dt), jnp.zeros((bp, CONV_WIDTH - 1, D_CONV), dt))
    y_p, y_s = x_prompt, x_sample
    st_p, st_s = [], []
    for l in range(DEPTH):
        weights = (w_in[l], pool_w[l], pool_scale[l], conv_w[l], cmp_pe[l], cmp_w[l],
                   proj_a[l], proj_b[l], proj_c[l], w_out[l], ln_g[l], ln_b[l])
        y_p, new_p = trunk_layer(y_p, 0, hist_prompt, *weights)
        hist_sample = (gather_pages(cache_k_cmp[l], page_table, past_len),
                       gather_pages(cache_v_cmp[l], page_table, past_len),
                       gather_pages(cache_k_sel[l], page_table, past_len),
                       gather_pages(cache_v_sel[l], page_table, past_len),
                       state_k_win[l], state_v_win[l], state_pool[l], state_conv[l])
        y_s, new_s = trunk_layer(y_s, past_len, hist_sample, *weights)
        st_p.append(new_p)
        st_s.append(new_s)

    def stacked(states, i):
        return jnp.stack([s[i] for s in states], axis=0)

    p_k_cmp, p_v_cmp, p_k_sel, p_v_sel = stacked(st_p, 0), stacked(st_p, 1), stacked(st_p, 2), stacked(st_p, 3)
    p_k_win, p_v_win, p_pool, p_conv = stacked(st_p, 4), stacked(st_p, 5), stacked(st_p, 6), stacked(st_p, 7)
    s_k_cmp, s_v_cmp, s_k_sel, s_v_sel = stacked(st_s, 0), stacked(st_s, 1), stacked(st_s, 2), stacked(st_s, 3)
    s_k_win, s_v_win, s_pool, s_conv = stacked(st_s, 4), stacked(st_s, 5), stacked(st_s, 6), stacked(st_s, 7)
    return (y_p, y_s, p_k_cmp, p_v_cmp, p_k_sel, p_v_sel, p_k_win, p_v_win, p_pool, p_conv,
            s_k_cmp, s_v_cmp, s_k_sel, s_v_sel, s_k_win, s_v_win, s_pool, s_conv)


_drawn_inputs = setup_inputs


def setup_inputs(seed=0):
    import zlib

    import numpy as np

    out = dict(_drawn_inputs(seed))
    spreads = {}
    factors = {'cache_k_cmp': 4.573,
     'cache_v_cmp': 3.59,
     'cache_k_sel': 8.0,
     'cache_v_sel': 8.0,
     'pool_scale': 7.35,
     'cmp_pe': 8.0}
    for name, (base, spread) in spreads.items():
        noise = np.random.default_rng([zlib.crc32(name.encode()), seed]).standard_normal(out[name].shape)
        drawn = base * np.exp(spread * noise) if base else spread * noise
        out[name] = jnp.asarray(drawn.astype(out[name].dtype))
    for name, factor in factors.items():
        out[name] = (out[name] * factor).astype(out[name].dtype)
    return out
```

```python
from contextlib import ExitStack

import numpy as np

import concourse.bass as bass
from concourse import mybir

F32 = mybir.dt.float32
BF16 = mybir.dt.bfloat16
I32 = mybir.dt.int32
ALU = mybir.AluOpType
ACT = mybir.ActivationFunctionType
AX_X = mybir.AxisListType.X

P = 128
DEPTH = 2
D_MODEL = 1024
SEQ = 256
NB = 8
T = SEQ + NB
PAST = 256
KEYS = PAST + 1
HD = 64
HEADS = 16
GP = 2
R = 4
CT = 16
TAPS = 32
NC = 15
KT8 = D_MODEL // P
ALPHA = (2 * DEPTH) ** 0.25
EPS = 1e-5
QK = HD ** -0.5
MASKED = -1.0e30
FLOOR = -1.0e29
WINDOWS = (2, 4, 8, 16)
HIST = 15

KC, VC, KS, KW, VS, VW, Q, NG, PU, PZ, CB, CC, CX, CZ, AZ = 0, 2, 4, 6, 8, 10, 12, 20, 21, 25, 29, 33, 37, 41, 45
KEPT = 53
ROPED = [KS, KS + 1, KW, KW + 1] + list(range(Q, Q + 8))

RING = 5
SLOT_CK = 21
SLOT_CV = SLOT_CK + 4
SLOT_B = SLOT_CV + 4
SLOT_MERGE = SLOT_B + KEPT - 21
SLOT_OUT = SLOT_MERGE + 5 * KT8
SLOTS = SLOT_OUT + KT8

PRM = {}
_at = 0
for _name, _n in (("pool_scale", 4), ("conv_w", 12), ("ln_g", 8), ("ln_b", 8), ("pe_k", TAPS), ("pe_v", TAPS),
                  ("pool_hist", 4 * NB * HIST), ("conv_hist", 4 * 2 * NB), ("pool_w", 4 * P)):
    PRM[_name] = (_at, _n)
    _at += _n
N_PRM = _at
CST = {}
_at = 0
for _name, _n in (("rope_c", T), ("rope_s", T), ("cmp_c", CT), ("cmp_s", CT), ("ident", P), ("perm", P),
                  ("causal", P), ("cmp_mask", 2 * CT), ("own_row", NB), ("own_head", 4 * P),
                  ("inv_count", 4 * CT), ("gate_head", HEADS), ("gate_type", 3)):
    CST[_name] = (_at, _n)
    _at += _n
N_CST = _at
ST_PP, ST_PS, ST_CP, ST_CS, N_ST = 0, 60, 540, 548, 612


def make_order():
    order = []
    for n in range(21):
        order.append(("dense", n))
        if n - 1 in ROPED:
            order.append(("rope", n - 1))
        if n == 13:
            order += [("v_rows", 0), ("v_rows", 1)]
        if n == 14:
            order.append(("v_new", 0))
    order += [("cmp_k", 0), ("gates", 0), ("cmp_v", 0), ("cmp_rope", 0), ("dense", 21), ("cmp_vrows", 0),
              ("cmp_scores", 0), ("dense", 22), ("dense", 23), ("cmp_turn", 0), ("dense", 24)]
    nxt = 25
    for u in range(HEADS):
        order += [("scores", u), ("dense", nxt)]
        nxt += 1
        if u > 0:
            order.append(("pv", u - 1))
        order.append(("turn", u))
        if u == 3:
            order.append(("pool", 0))
    order += [("one_cmp_scores", 0), ("one_scores", 0), ("dense", nxt), ("pv", HEADS - 1),
              ("one_turn", 0), ("dense", nxt + 1), ("dense", nxt + 2), ("conv", 0), ("one_pv", 0),
              ("one_scores", 1), ("dense", nxt + 3), ("dense", nxt + 4), ("one_turn", 1), ("one_cmp_turn", 0)]
    nxt += 5
    while nxt < KEPT:
        order.append(("dense", nxt))
        nxt += 1
    order += [("one_pv", 1), ("silu", 0)]
    order += [("mix", g) for g in range(4)]
    order += [("merge", i) for i in range(KT8)]
    for i in range(KT8):
        order.append(("out", i))
        if i:
            order.append(("mean", i - 1))
    order += [("mean", KT8 - 1), ("norm", 0)]
    return order


ORDER = make_order()
D0, D1, SA, SB, PT0, PT1, OT, MI = range(8)


def banks_of(step, i):
    if step == "dense":
        return [i % 2]
    if step == "merge":
        gates = [(KEPT + 3 * i + j) % 2 for j in range(3)]
        return gates + ([SA, SB, PT0] if i % 2 == 0 else [PT1, OT, MI])
    if step == "out":
        return [(KEPT + 3 * KT8 + i) % 2]
    if step == "turn":
        return [PT0, PT1]
    if step == "scores":
        return [SA, SB]
    if step == "pv":
        return [OT] if i % 2 else []
    if step == "mix":
        return [(SA, SB, PT0, PT1)[i]]
    if step == "v_rows":
        return [(PT0, PT1)[i]]
    if step == "one_scores":
        return [(SA, PT0)[i]]
    if step == "one_turn":
        return [(PT1, SB)[i]]
    if step == "one_pv":
        return [OT] if i else []
    return {"rope": [MI], "v_new": [MI], "cmp_k": [PT0], "gates": [MI], "cmp_v": [PT1], "cmp_rope": [MI],
            "cmp_vrows": [MI], "cmp_scores": [SA], "cmp_turn": [PT0], "one_cmp_scores": [SB],
            "one_cmp_turn": [MI]}.get(step, [])


def plan_fills():
    fill, total = {}, [0] * 8
    for step, i in ORDER:
        for j, b in enumerate(banks_of(step, i)):
            total[b] += 1
            fill[step, i, j] = (b, total[b])
    return fill, total


FILL, FILLS = plan_fills()
BY_SLOT = {"dense", "cmp_k", "cmp_v", "merge", "out"}
FILLED = [sum(1 for (s, i, j), (b, k) in FILL.items() if b == bank and s not in BY_SLOT) for bank in range(8)]


def filled_count(step, i, j):
    bank, k = FILL[step, i, j]
    return bank, sum(1 for (s, a, c), (b, m) in FILL.items() if b == bank and m <= k and s not in BY_SLOT)


SLOT_OF = {("dense", n): (n if n < 21 else SLOT_B + n - 21) for n in range(KEPT)}
SLOT_OF.update({("cmp_k", 0): SLOT_CK + 3, ("cmp_v", 0): SLOT_CV + 3})
SLOT_OF.update({("out", i): SLOT_OUT + i for i in range(KT8)})
SLOTS_IN = [sum(1 for i in range(SLOTS) if i % RING == s) for s in range(RING)]
VECTOR_STEPS = 148


def trunk(nc, x_in, weights, params, consts, pages, kcmp, vcmp, ksel, vsel, kwin, vwin,
          y_out, kv_out, state_out, kwin_out, vwin_out):
    n_pool = kcmp.shape[1]
    with ExitStack() as ctx:
        def sb(name, shape, dt=F32):
            return ctx.enter_context(nc.sbuf_tensor(name, shape, dt))

        def sem(name):
            return ctx.enter_context(nc.semaphore(name))

        bank = [ctx.enter_context(nc.psum_tensor(f"bank{b}", [P, 512], F32)) for b in range(8)]

        x = sb("x", [P, KT8, T])
        z = sb("z", [P, KT8, T])
        m = sb("m", [P, KT8, T])
        h = sb("h", [P, KEPT, T])
        ring = sb("ring", [P, RING, KT8, P])
        cache_a = sb("cache_a", [P, 10 * GP * PAST])
        cache_b = sb("cache_b", [P, 10 * GP * PAST])
        prm = sb("prm", [P, N_PRM])
        cst = sb("cst", [P, N_CST])
        page = sb("page", [1, NB * 2], I32)
        causal_b = sb("causal_b", [P, P], BF16)
        ident_b = sb("ident_b", [P, P], BF16)
        ones = sb("ones", [P, P])
        eps = sb("eps", [P, 1])
        v_rows = sb("v_rows", [P, 2, 4 * P])
        v_new_c = sb("v_new_c", [P, GP, 2, NB])
        v_new = sb("v_new", [2 * NB, GP * P])
        gate = sb("gate", [P, 99])
        gate_d = sb("gate_d", [P, HEADS, NB])
        kc_all = sb("kc_all", [P, GP, NB + 1, CT])
        vc_all = sb("vc_all", [P, GP, NB + 1, CT])
        vc_rep = sb("vc_rep", [P, GP, 8, CT])
        kc_bd = sb("kc_bd", [P, GP, 2, CT])
        vc_bd = sb("vc_bd", [P, GP, R, P])
        vc_one = sb("vc_one", [P, GP, P])
        bias = sb("bias", [P, 2])
        tmp = sb("tmp", [P, 3, 288])
        c_max = sb("c_max", [P, 32])
        c_sum = sb("c_sum", [P, 32])
        pc_t = sb("pc_t", [P, GP, SEQ])
        probs = sb("probs", [P, 2, 768])
        probs_t = sb("probs_t", [P, 2, 2, 384])
        u_max = sb("u_max", [P, 2, 4])
        u_sum = sb("u_sum", [P, 2, 4])
        u_fac = sb("u_fac", [P, 2, 4])
        q_pad = sb("q_pad", [P, GP, NB, P])
        p_cmp = sb("p_cmp", [P, CT])
        p_cmp_x = sb("p_cmp_x", [P, NB, CT])
        p_tail = sb("p_tail", [P, 2, NB])
        one_max = sb("one_max", [P, 3])
        one_sum = sb("one_sum", [P, 3])
        p_cmp_t = sb("p_cmp_t", [P, P])
        p_tail_t = sb("p_tail_t", [2 * NB, P])
        pu_ext = sb("pu_ext", [P, 4, HIST + SEQ])
        pu_one = sb("pu_one", [P, 4, NB, HIST + 1])
        pu_sum = sb("pu_sum", [P, 4, NB])
        hc_one = sb("hc_one", [P, 4, 3, NB])
        state = sb("state", [P, N_ST])
        rstd = sb("rstd", [P, T])

        zf = z[:, :, :].rearrange("p a t -> p (a t)")
        mf = m[:, :, :].rearrange("p a t -> p (a t)")
        NE = HIST + SEQ
        sum_a = zf[:, 0:4 * NE].rearrange("p (g t) -> p g t", g=4)
        sum_b = mf[:, 0:4 * NE].rearrange("p (g t) -> p g t", g=4)
        hc_ext = mf[:, 0:4 * (2 + SEQ)].rearrange("p (g t) -> p g t", g=4)
        g = h[:, CC:CC + 6, :].rearrange("p (a j) t -> p a j t", a=2)
        probs_flat = probs[:, :, :].rearrange("p a n -> p (a n)")
        cs = probs_flat[:, 0:32 * CT].rearrange("p (n c) -> p n c", c=CT)
        p_one = probs_flat[:, 0:2 * KEYS].rearrange("p (a n) -> p a n", a=2)
        p_one_t = probs_t[:, :, :, :].rearrange("p a b n -> p (a b n)")[:, 0:4 * P].rearrange("p (a n) -> p a n", a=2)
        cmp_view = [c[:, :].rearrange("p (s t) -> p s t", t=PAST) for c in (cache_a, cache_b)]
        k_one = cache_a[:, 0:NB * GP * KEYS].rearrange("p (b g t) -> p b g t", b=NB, g=GP)
        v_one = cache_b[:, 0:NB * 2 * 2 * P].rearrange("p (b t n) -> p b t n", b=NB, t=2)

        def c(name):
            at, n = CST[name]
            return cst[:, at:at + n]

        def pr(name, i=0, n=None):
            at, size = PRM[name]
            return prm[:, at + i:at + i + (size if n is None else n)]

        ident, perm = c("ident"), c("perm")

        consts_loaded, x_loaded, pages_loaded = sem("consts_loaded"), sem("x_loaded"), sem("pages_loaded")
        params_loaded = sem("params_loaded")
        landed = [sem(f"weight_landed{s}") for s in range(RING)]
        cmp_k_landed, cmp_v_landed = sem("cmp_k_landed"), sem("cmp_v_landed")
        sel_k_landed, sel_v_landed = sem("sel_k_landed"), sem("sel_v_landed")
        win_k_landed, win_v_landed = sem("win_k_landed"), sem("win_v_landed")
        slots_done = sem("slots_done")
        x_ready = sem("x_ready")
        filled = [sem(f"bank{b}_filled") for b in range(8)]
        emptied = [sem(f"bank{b}_emptied") for b in range(8)]
        tables_ready = sem("tables_ready")
        vector_step = sem("vector_step")
        roped = sem("roped")
        cmp_in_ready = sem("cmp_in_ready")
        v_new_ready = sem("v_new_ready")
        gate_d_ready = sem("gate_d_ready")
        cmp_out_ready = sem("cmp_out_ready")
        kc_ready = sem("kc_ready")
        cmp_shifted, cmp_exped, cmp_probs = sem("cmp_shifted"), sem("cmp_exped"), sem("cmp_probs")
        max_ready, probs_ready, pv_even = sem("max_ready"), sem("probs_ready"), sem("pv_even")
        q_pad_ready = sem("q_pad_ready")
        k_new_ready = sem("k_new_ready")
        one_max_ready, one_exped, one_probs = sem("one_max_ready"), sem("one_exped"), sem("one_probs")
        sel_v_used = sem("sel_v_used")
        sigmoids = sem("sigmoids")
        pooled, convolved = sem("pooled"), sem("convolved")
        y_ready = sem("y_ready")
        merged, squared, std_ready = sem("merged"), sem("squared"), sem("std_ready")
        mean_ready, squared_sum, centered = sem("mean_ready"), sem("squared_sum"), sem("centered")
        state_ready, state_staged = sem("state_ready"), sem("state_staged")
        pool_goes = sem("pool_goes")
        kv_stored, state_stored, win_copied, y_stored = (
            sem("kv_stored"), sem("state_stored"), sem("win_copied"), sem("y_stored"))

        block = ctx.enter_context(nc.Block())

        def wait_slot(eng, l, step, i):
            s = SLOT_OF[step, i] if (step, i) in SLOT_OF else i
            eng.wait_ge(slots_done, l * SLOTS + RING + s + 1)

        def wait_filled(eng, l, step, i, j=0):
            b, k = filled_count(step, i, j)
            eng.wait_ge(filled[b], l * FILLED[b] + k)

        def wait_emptied(eng, l, step, i, j=0):
            b, k = FILL[step, i, j]
            eng.wait_ge(emptied[b], l * FILLS[b] + k)

        @block.sync
        def _(sp):
            sp.dma_start(x[:, :, :], x_in).then_inc(x_loaded, 16)
            sp.dma_start(cst[:, :], consts).then_inc(consts_loaded, 16)
            with sp.Fori(0, DEPTH) as l:
                for i in range(SLOTS):
                    before = i - RING if i >= RING else max(j for j in range(SLOTS) if j % RING == i) - SLOTS
                    sp.wait_ge(slots_done, l * SLOTS + RING + before + 1)
                    sp.dma_start(ring[:, i % RING, :, :], weights[l, i].rearrange("p (k n) -> p k n", k=KT8)
                                 ).then_inc(landed[i % RING], 16)
                    if i == 0:
                        sp.wait_ge(x_ready, l * KT8 + KT8)
                        sp.dma_start(prm[:, :], params[l]).then_inc(params_loaded, 16)
            sp.wait_ge(x_ready, (DEPTH + 1) * KT8)
            sp.dma_start(y_out, x[:, :, :]).then_inc(y_stored, 16)
            sp.wait_ge(y_stored, 16)

        @block.gpsimd
        def _(pool):
            pool.dma_start(page[:, :], pages).then_inc(pages_loaded, 16)
            pool.wait_ge(pages_loaded, 16)

            def load_pages(l, cache, dst_of, landed_sem):
                with pool.Fori(0, NB) as b:
                    for half in range(2):
                        pg = pool.value_load(page[0:1, bass.ds(b * 2 + half, 1)], min_val=0, max_val=n_pool - 1)
                        pool.dma_start(dst_of(b, half), cache[bass.ds(l, 1), bass.ds(pg, 1)].rearrange(
                            "a b p n -> (a b p) n" if len(cache.shape) == 4 else "a b p g n -> (a b p) g n")
                            ).then_inc(landed_sem, 16)

            def cmp_dst(view):
                v = view.rearrange("p (s g) t -> p s g t", g=GP)
                return lambda b, half: v[:, bass.ds(b, 1), :, half * P:half * P + P].rearrange("p s g t -> p (s g) t")

            def go():
                pool.sem_inc(pool_goes, 1)

            with pool.Fori(0, DEPTH) as l:
                pool.wait_ge(x_ready, l * KT8 + KT8)
                go()
                load_pages(l, kcmp, cmp_dst(cmp_view[0]), cmp_k_landed)
                load_pages(l, vcmp, cmp_dst(cmp_view[1]), cmp_v_landed)
                pool.wait_ge(roped, l * len(ROPED) + 4)
                wait_emptied(pool, l, "dense", VW)
                wait_emptied(pool, l, "dense", VW + 1)
                go()
                pool.dma_start(kv_out[l], h[:, 0:12, :]).then_inc(kv_stored, 16)
                wait_slot(pool, l, "cmp_k", 0)
                go()
                load_pages(l, ksel, lambda b, half: k_one[:, bass.ds(b, 1), :, half * P:half * P + P].rearrange(
                    "p s g t -> p (s g) t"), sel_k_landed)
                wait_slot(pool, l, "cmp_v", 0)
                go()
                load_pages(l, vsel, lambda b, half: v_one[:, bass.ds(b, 1), half, :].rearrange(
                    "p s n -> p (s n)"), sel_v_landed)
                pool.wait_ge(state_ready, 2 * l + 1)
                go()
                pool.tensor_copy(state[:, ST_PP:ST_PS].rearrange("p (g t) -> p g t", g=4),
                                 pu_ext[:, :, SEQ:SEQ + HIST])
                pool.tensor_copy(state[:, ST_PS:ST_CP].rearrange("p (g b t) -> p g b t", g=4, b=NB),
                                 pu_one[:, :, :, 1:HIST + 1])
                pool.wait_ge(state_ready, 2 * l + 2)
                go()
                pool.tensor_copy(state[:, ST_CP:ST_CS].rearrange("p (g t) -> p g t", g=4), hc_ext[:, :, SEQ:SEQ + 2])
                pool.tensor_copy(state[:, ST_CS:N_ST].rearrange("p (g j b) -> p g j b", g=4, j=2),
                                 hc_one[:, :, 1:3, :]).then_inc(state_staged, 1)
                pool.wait_ge(state_staged, l + 1)
                go()
                pool.dma_start(state_out[l], state[:, :]).then_inc(state_stored, 16)
                wait_filled(pool, l, "one_scores", 0)
                go()
                pool.dma_start(k_one[:, :, :, 0:PAST].rearrange("p b g t -> p (b g) t"),
                               kwin[bass.ds(l, 1)].rearrange("a p n t -> (a p) n t")).then_inc(win_k_landed, 16)
                pool.wait_ge(sel_v_used, l + 1)
                go()
                pool.dma_start(v_one.rearrange("p b t n -> p (b t n)"),
                               vwin[bass.ds(l, 1)].rearrange("a p n -> (a p) n")).then_inc(win_v_landed, 16)
                pool.dma_start(kwin_out[l], kwin[l]).then_inc(win_copied, 16)
                pool.dma_start(vwin_out[l], vwin[l]).then_inc(win_copied, 16)
            pool.wait_ge(win_copied, 2 * DEPTH * 16)
            pool.wait_ge(kv_stored, DEPTH * 16)
            pool.wait_ge(state_stored, DEPTH * 16)

        @block.tensor
        def _(pe):
            pe.sem_inc(slots_done, RING)
            pe.sem_inc(x_ready, KT8)
            pe.wait_ge(x_loaded, 16)
            pe.wait_ge(tables_ready, 1)
            with pe.Fori(0, DEPTH) as l:
                def weight(i):
                    s = i % RING
                    pe.wait_ge(landed[s], (l * SLOTS_IN[s] + i // RING + 1) * 16)
                    return ring[:, s]

                def out_bank(step, i, j=0):
                    b, k = FILL[step, i, j]
                    if k > 1:
                        pe.wait_ge(emptied[b], l * FILLS[b] + k - 1)
                    return bank[b]

                def done(ins, step, i, j=0):
                    b, _ = FILL[step, i, j]
                    ins.then_inc(filled[b], 1)

                def product(out, w, rhs, k0=0, kn=KT8, last=True):
                    for k in range(kn):
                        ins = pe.matmul(out, w[:, k0 + k, :], rhs(k), start=(k == 0), stop=(k == kn - 1))
                    return ins

                for step, i in ORDER:
                    if step == "dense":
                        w = weight(SLOT_OF[step, i])
                        out = out_bank(step, i)
                        for k in range(KT8):
                            if i == 0:
                                pe.wait_ge(x_ready, l * KT8 + k + 1)
                            ins = pe.matmul(out[:, 0:T], w[:, k, :], x[:, k, :], start=(k == 0), stop=(k == KT8 - 1))
                        ins.then_inc(slots_done, 1)
                    elif step == "rope":
                        wait_emptied(pe, l, "dense", i)
                        out = out_bank(step, i)
                        done(pe.matmul(out[:, 0:T], perm, h[:, i, :], start=True, stop=True), step, i)
                    elif step == "v_rows":
                        if i == 0:
                            for n in (VW, VW + 1):
                                wait_emptied(pe, l, "dense", n)
                        out = out_bank(step, i)
                        for n in range(4):
                            ins = pe.transpose(out[:, n * P:n * P + P], h[:, VS + n, i * P:i * P + P], ident)
                        done(ins, step, i)
                    elif step == "v_new":
                        out = out_bank(step, i)
                        pe.wait_ge(v_new_ready, l + 1)
                        for gp in range(GP):
                            ins = pe.transpose(out[0:2 * NB, gp * P:gp * P + P],
                                               v_new_c[:, gp, :, :].rearrange("p a b -> p (a b)"), ident)
                        done(ins, step, i)
                    elif step == "gates":
                        wait_emptied(pe, l, "dense", NG)
                        out = out_bank(step, i)
                        for qi in range(2):
                            pe.transpose(out[:, qi * P:qi * P + P], h[:, NG, (1 - qi) * P:(2 - qi) * P], ident)
                        pe.wait_ge(gate_d_ready, l + 1)
                        ins = pe.matmul(out[:, 2 * P:2 * P + 3], gate_d[0:48, :, :].rearrange("p a b -> p (a b)"),
                                        c("gate_type")[0:48, :], start=True, stop=True)
                        done(ins, step, i)
                    elif step in ("cmp_k", "cmp_v"):
                        which = int(step == "cmp_v")
                        out = out_bank(step, i)
                        pe.wait_ge(cmp_v_landed if which else cmp_k_landed, (l + 1) * 16 * 2 * NB)
                        pe.wait_ge(cmp_in_ready, 2 * l + 1 + which)
                        for tap in range(TAPS):
                            if tap % KT8 == 0:
                                w = weight((SLOT_CV if which else SLOT_CK) + tap // KT8)
                            rows = cmp_view[which][:, 0:19, tap:tap + CT * (NC - 1) + 1:CT]
                            ins = pe.matmul(bank[PT1 if which else PT0][:, 0:19 * NC].rearrange(
                                "p (s c) -> p s c", c=NC), w[:, tap % KT8, :], rows,
                                start=(tap == 0), stop=(tap == TAPS - 1))
                            if tap % KT8 == KT8 - 1:
                                ins.then_inc(slots_done, 1)
                    elif step == "cmp_rope":
                        out = out_bank(step, i)
                        wait_emptied(pe, l, "cmp_k", 0)
                        done(pe.matmul(out[:, 0:288], perm, kc_all[:, :, :, :].rearrange("p g s c -> p (g s c)"),
                                       start=True, stop=True), step, i)
                    elif step == "cmp_vrows":
                        out = out_bank(step, i)
                        pe.wait_ge(cmp_out_ready, l + 1)
                        for gp in range(GP):
                            pe.transpose(out[:, gp * P:gp * P + P],
                                         vc_rep[:, gp, :, :].rearrange("p a b -> p (a b)"), ident)
                            ins = pe.transpose(out[:, (2 + gp) * P:(3 + gp) * P],
                                               vc_all[:, gp, 0:NB, :].rearrange("p a b -> p (a b)"), ident)
                        done(ins, step, i)
                    elif step == "cmp_scores":
                        out = out_bank(step, i)
                        pe.wait_ge(kc_ready, l + 1)
                        pe.wait_ge(roped, (l + 1) * len(ROPED))
                        for qi in range(2):
                            for n in range(8):
                                col = qi * 256 + n * 32
                                ins = pe.matmul(out[:, col:col + 32], h[:, Q + n, (1 - qi) * P:(2 - qi) * P],
                                                kc_bd[:, n // R, :, :].rearrange("p a b -> p (a b)"),
                                                start=True, stop=True)
                        done(ins, step, i)
                    elif step == "cmp_turn":
                        out = out_bank(step, i)
                        pe.wait_ge(cmp_probs, l + 1)
                        for gp in range(GP):
                            for qi in range(2):
                                src = cs[:, qi * 16 + gp * 8:qi * 16 + gp * 8 + 8, :].rearrange("p a b -> p (a b)")
                                col = gp * SEQ + (1 - qi) * P
                                ins = pe.transpose(out[:, col:col + P], src, ident)
                        done(ins, step, i)
                    elif step == "scores":
                        tile, g2 = Q + i // 2, i % 2
                        gp = i // 8
                        rows = slice(g2 * HD, g2 * HD + HD)
                        for j, (q0, n) in enumerate(((P, 2 * P), (0, P))):
                            out = out_bank(step, i, j)
                            for br, kt in enumerate((KS, KW)):
                                reg = out[:, br * n:br * n + n]
                                pe.matmul(reg, h[rows, tile, q0:q0 + P], h[rows, kt + gp, 0:n], start=True, stop=False)
                                ins = pe.matmul(reg[:, n - P:n], ident_b[:, :], causal_b[:, :], start=False, stop=True)
                            done(ins, step, i, j)
                    elif step == "turn":
                        pe.wait_ge(probs_ready, l * HEADS + i + 1)
                        for br in range(2):
                            out = out_bank(step, i, br)
                            late, early = br * 256, 512 + br * P
                            pe.transpose(out[:, 0:P], probs[:, i % 2, early:early + P], ident)
                            pe.transpose(out[:, P:2 * P], probs[:, i % 2, late:late + P], ident)
                            ins = pe.transpose(out[:, 2 * P:3 * P], probs[:, i % 2, late + P:late + 2 * P], ident)
                            done(ins, step, i, br)
                    elif step == "pv":
                        gp, r, g2 = i // 8, i // 2 % R, i % 2
                        if g2 == 0:
                            if i == 0:
                                wait_emptied(pe, l, "v_rows", 0)
                                wait_emptied(pe, l, "v_rows", 1)
                                wait_emptied(pe, l, "cmp_turn", 0)
                                wait_emptied(pe, l, "cmp_vrows", 0)
                            out = out_bank(step, i + 1)
                            pe.matmul(out[:, 0:SEQ], vc_bd[:, gp, r, :], pc_t[:, gp, :], start=True, stop=False,
                                      skip_group_check=True)
                        out = bank[OT][g2 * HD:g2 * HD + HD, :]
                        gcol = (2 * gp + g2) * HD
                        for br in range(2):
                            wait_emptied(pe, l, "turn", i, br)
                            pt = probs_t[:, i % 2, br, :]
                            pe.matmul(out[:, 0:SEQ], v_rows[:, 0, br * 256 + gcol:br * 256 + gcol + HD],
                                      pt[:, 0:SEQ], start=False, stop=False, skip_group_check=True)
                            ins = pe.matmul(out[:, P:SEQ], v_rows[:, 1, br * 256 + gcol:br * 256 + gcol + HD],
                                            pt[:, SEQ:SEQ + P], start=False, stop=(br == 1), skip_group_check=True)
                        if g2:
                            done(ins, step, i)
                        else:
                            ins.then_inc(pv_even, 1)
                    elif step == "one_cmp_scores":
                        out = out_bank(step, i)
                        pe.wait_ge(q_pad_ready, l + 1)
                        for n in range(GP * NB):
                            gp, b = n % GP, n // GP
                            ins = pe.matmul(out[:, 0:CT], q_pad[:, gp, b, :], kc_all[:, gp, b, :],
                                            start=(n == 0), stop=(n == GP * NB - 1))
                        done(ins, step, i)
                    elif step == "one_scores":
                        out = out_bank(step, i)
                        pe.wait_ge(win_k_landed if i else sel_k_landed, (l + 1) * (16 if i else 16 * 2 * NB))
                        pe.wait_ge(k_new_ready, 2 * l + i + 1)
                        for n in range(GP * NB):
                            gp, b = n % GP, n // GP
                            ins = pe.matmul(out[:, 0:KEYS], q_pad[:, gp, b, :], k_one[:, b, gp, :],
                                            start=(n == 0), stop=(n == GP * NB - 1))
                        done(ins, step, i)
                    elif step == "one_turn":
                        out = out_bank(step, i)
                        pe.wait_ge(one_probs, 2 * l + i + 1)
                        for half in range(2):
                            ins = pe.transpose(out[:, half * P:half * P + P],
                                               p_one[:, i, half * P:half * P + P], ident)
                        done(ins, step, i)
                    elif step == "one_cmp_turn":
                        out = out_bank(step, i)
                        pe.transpose(out[:, 0:P], p_cmp_x[:, :, :].rearrange("p b c -> p (b c)"), ident)
                        ins = pe.transpose(out[0:2 * NB, P:2 * P], p_tail[:, :, :].rearrange("p a b -> p (a b)"),
                                           ident)
                        done(ins, step, i)
                    elif step == "one_pv":
                        if i == 0:
                            out = out_bank("one_pv", 1)
                        wait_emptied(pe, l, "one_turn", i)
                        pe.wait_ge(win_v_landed if i else sel_v_landed, (l + 1) * (16 if i else 16 * 2 * NB))
                        out = bank[OT][:, 0:P].rearrange("p (g n b) -> p g n b", g=GP, b=NB)
                        pt = p_one_t[:, i, :].rearrange("p (t g n b) -> p t g n b", t=2, g=GP, b=NB)
                        for b in range(NB):
                            for gp in range(GP):
                                for half in range(2):
                                    ins = pe.matmul(out[:, gp, :, b], v_one[:, b, half, gp * P:gp * P + P],
                                                    pt[:, half, gp, :, b],
                                                    start=(i == 0 and b == 0 and gp == 0 and half == 0),
                                                    stop=False, skip_group_check=True)
                        if i == 0:
                            ins.then_inc(sel_v_used, 1)
                        else:
                            wait_emptied(pe, l, "one_cmp_turn", 0)
                            wait_emptied(pe, l, "v_new", 0)
                            for gp in range(GP):
                                cols = slice(gp * HD, gp * HD + HD)
                                pe.matmul(bank[OT][:, cols], vc_one[:, gp, :], p_cmp_t[:, cols],
                                          start=False, stop=False, skip_group_check=True)
                                ins = pe.matmul(bank[OT][:, cols], v_new[:, gp * P:gp * P + P], p_tail_t[:, cols],
                                                start=False, stop=(gp == 1), skip_group_check=True)
                            done(ins, step, i)
                    elif step == "mix":
                        out = out_bank(step, i)
                        if i == 0:
                            pe.wait_ge(pooled, l + 1)
                        done(pe.matmul(out[:, 0:T], pr("pool_w", i * P, P), h[:, PU + i, :], start=True, stop=True),
                             step, i)
                    elif step == "merge":
                        for j in range(3):
                            w = weight(SLOT_MERGE + 5 * i + j)
                            out = out_bank(step, i, j)
                            product(out[:, 0:T], w, lambda k: x[:, k, :]).then_inc(slots_done, 1)
                        w = weight(SLOT_MERGE + 5 * i + 3)
                        if i == 0:
                            for n in range(4):
                                wait_emptied(pe, l, "mix", n)
                            pe.wait_ge(y_ready, 2 * l + 1)
                        out = out_bank(step, i, 3)
                        product(out[:, 0:T], w, lambda k: h[:, PU + k, :], 0, 4)
                        out = out_bank(step, i, 4)
                        product(out[:, 0:T], w, lambda k: h[:, CB + k, :], 4, 4).then_inc(slots_done, 1)
                        w = weight(SLOT_MERGE + 5 * i + 4)
                        if i == 0:
                            pe.wait_ge(y_ready, 2 * l + 2)
                        out = out_bank(step, i, 5)
                        product(out[:, 0:T], w, lambda k: h[:, Q + k, :]).then_inc(slots_done, 1)
                    elif step == "out":
                        w = weight(SLOT_OUT + i)
                        out = out_bank(step, i)
                        if i == 0:
                            pe.wait_ge(merged, (l + 1) * KT8)
                        product(out[:, 0:T], w, lambda k: m[:, k, :]).then_inc(slots_done, 1)
                    elif step == "mean":
                        wait_emptied(pe, l, "out", i)
                        ins = pe.matmul(bank[SA][:, 0:T], ones[:, :], z[:, i, :], start=(i == 0), stop=(i == KT8 - 1))
                        if i == KT8 - 1:
                            ins.then_inc(mean_ready, 1)
                    elif step == "norm":
                        for k in range(KT8):
                            if k % 2 == 0:
                                pe.wait_ge(squared, l * 4 + k // 2 + 1)
                            ins = pe.matmul(bank[SB][:, 0:T], ones[:, :], m[:, k, :], start=(k == 0),
                                            stop=(k == KT8 - 1))
                        ins.then_inc(squared_sum, 1)

        @block.scalar
        def _(act):
            act.wait_ge(tables_ready, 1)
            with act.Fori(0, DEPTH) as l:
                def emptied_by(ins, step, i, j=0):
                    ins.then_inc(emptied[FILL[step, i, j][0]], 1)

                for step, i in ORDER:
                    if step == "dense":
                        wait_slot(act, l, step, i)
                        src = bank[FILL[step, i, 0][0]][:, 0:T]
                        emptied_by(act.activation(h[:, i, :], src, ACT.Sigmoid if i == NG else ACT.Copy), step, i)
                    elif step == "v_rows":
                        wait_filled(act, l, step, i)
                        src = bank[FILL[step, i, 0][0]]
                        emptied_by(act.activation(v_rows[:, i, :], src[:, :], ACT.Copy), step, i)
                    elif step == "cmp_scores":
                        act.wait_ge(cmp_shifted, l + 1)
                        act.activation(cs[:, :, :], cs[:, :, :], ACT.Exp, scale=QK).then_inc(cmp_exped, 1)
                    elif step == "cmp_turn":
                        wait_filled(act, l, step, i)
                        emptied_by(act.activation(pc_t[:, :, :].rearrange("p g t -> p (g t)"), bank[PT0][:, :],
                                                  ACT.Copy), step, i)
                    elif step == "scores":
                        act.wait_ge(max_ready, l * HEADS + i + 1)
                        if i >= 2:
                            wait_filled(act, l, "turn", i - 2, 1)
                        at = 0
                        for j, n in enumerate((2 * P, P)):
                            src = bank[(SA, SB)[j]]
                            for br in range(2):
                                ins = act.activation(probs[:, i % 2, at:at + n], src[:, br * n:br * n + n], ACT.Exp,
                                                     bias=u_max[:, i % 2, 2 * j + br:2 * j + br + 1], scale=QK,
                                                     accum_out=u_sum[:, i % 2, 2 * j + br:2 * j + br + 1])
                                at += n
                            emptied_by(ins, step, i, j)
                    elif step == "turn":
                        wait_filled(act, l, step, i, 0)
                        if i >= 2:
                            if i % 2:
                                wait_filled(act, l, "pv", i - 2)
                            else:
                                act.wait_ge(pv_even, l * 8 + i // 2)
                        emptied_by(act.activation(probs_t[:, i % 2, 0, :], bank[PT0][:, 0:384], ACT.Copy), step, i, 0)
                    elif step == "pv" and i % 2:
                        wait_filled(act, l, step, i)
                        emptied_by(act.activation(h[:, Q + i // 2, 0:SEQ], bank[OT][:, 0:SEQ], ACT.Copy), step, i)
                    elif step == "one_cmp_scores":
                        act.wait_ge(one_max_ready, 3 * l + 1)
                        act.activation(p_cmp[:, 0:NC], bank[SB][:, 0:NC], ACT.Exp, bias=one_max[:, 2:3], scale=QK,
                                       accum_out=one_sum[:, 2:3]).then_inc(emptied[SB], 1)
                    elif step == "one_scores":
                        act.wait_ge(one_max_ready, 3 * l + 2 + i)
                        emptied_by(act.activation(p_one[:, i, :], bank[(SA, PT0)[i]][:, 0:KEYS], ACT.Exp,
                                                  bias=one_max[:, i:i + 1], scale=QK,
                                                  accum_out=one_sum[:, i:i + 1]), step, i)
                    elif step == "one_turn":
                        wait_filled(act, l, step, i)
                        emptied_by(act.activation(p_one_t[:, i, :], bank[(PT1, SB)[i]][:, 0:2 * P], ACT.Copy), step, i)
                    elif step == "silu":
                        act.wait_ge(pooled, l + 1)
                        act.wait_ge(convolved, l + 1)
                        for n in (KEPT - 2, KEPT - 1):
                            wait_emptied(act, l, "dense", n)
                        act.wait_ge(state_staged, l + 1)
                        act.activation(z[:, 0:4, :], h[:, PZ:PZ + 4, :], ACT.Sigmoid).then_inc(sigmoids, 1)
                        act.activation(z[:, 4:8, :], h[:, CZ:CZ + 4, :], ACT.Sigmoid).then_inc(sigmoids, 1)
                        act.activation(m[:, :, :], h[:, AZ:AZ + 8, :], ACT.Sigmoid).then_inc(sigmoids, 1)
                    elif step == "merge":
                        if i >= 2:
                            act.wait_ge(merged, l * KT8 + i - 1)
                        for j in range(3):
                            act.wait_ge(slots_done, l * SLOTS + RING + SLOT_MERGE + 5 * i + j + 1)
                            emptied_by(act.activation(g[:, i % 2, j, :], bank[FILL[step, i, j][0]][:, 0:T],
                                                      ACT.Sigmoid), step, i, j)
                    elif step == "norm":
                        for k in range(4):
                            act.wait_ge(centered, l * 4 + k + 1)
                            act.activation(m[:, 2 * k:2 * k + 2, :], z[:, 2 * k:2 * k + 2, :], ACT.Square
                                           ).then_inc(squared, 1)
                        act.wait_ge(squared_sum, l + 1)
                        act.activation(rstd[:, :], bank[SB][:, 0:T], ACT.Sqrt, bias=eps[:, :]).then_inc(std_ready, 1)

        @block.vector
        def _(dve):
            dve.wait_ge(consts_loaded, 16)
            dve.memset(ones[:, :], 1.0 / D_MODEL)
            dve.memset(eps[:, :], EPS)
            for which in range(2):
                dve.memset(cmp_view[which][:, 18, :], 0.0)
            for t in (kc_all, vc_all, kc_bd, q_pad, p_cmp, pu_ext):
                dims = " ".join("abcd"[:len(t.shape) - 1])
                dve.memset(t[tuple(slice(None) for _ in t.shape)].rearrange(f"p {dims} -> p ({dims})")
                           if len(t.shape) > 2 else t[:, :], 0.0)
            dve.tensor_copy(causal_b[:, :], c("causal"))
            dve.tensor_copy(ident_b[:, :], ident).then_inc(tables_ready, 1)
            dve.wait_ge(tables_ready, 1)
            with dve.Fori(0, DEPTH) as l:
                steps = [0]

                def link(ins):
                    steps[0] += 1
                    ins.then_inc(vector_step, 1)
                    dve.wait_ge(vector_step, l * VECTOR_STEPS + steps[0])

                def emptied_by(ins, step, i, j=0):
                    ins.then_inc(emptied[FILL[step, i, j][0]], 1)
                    wait_emptied(dve, l, step, i, j)

                def rotate(src, psum, cos, sin, scratch):
                    dve.tensor_tensor(scratch, psum, sin, ALU.mult)
                    return dve.tensor_tensor(src, src, cos, ALU.mult)

                for step, i in ORDER:
                    if step == "rope":
                        wait_filled(dve, l, step, i)
                        emptied_by(dve.tensor_tensor(tmp[:, 0, 0:T], bank[MI][:, 0:T], c("rope_s"), ALU.mult), step, i)
                        link(dve.tensor_tensor(h[:, i, :], h[:, i, :], c("rope_c"), ALU.mult))
                        wait_emptied(dve, l, step, i)
                        dve.tensor_tensor(h[:, i, :], h[:, i, :], tmp[:, 0, 0:T], ALU.add).then_inc(roped, 1)
                        dve.wait_ge(roped, l * len(ROPED) + ROPED.index(i) + 1)
                        if i == Q + 7:
                            dve.wait_ge(roped, (l + 1) * len(ROPED))
                            for g2 in range(2):
                                rows = slice(g2 * HD, g2 * HD + HD)
                                for gp in range(GP):
                                    src = h[rows, Q + gp * R:Q + gp * R + R, SEQ:T]
                                    for r in range(R):
                                        col = gp * HD + (r * 2 + g2) * NB
                                        diag = q_pad[rows, gp, :, :].rearrange("p b n -> p (b n)")[
                                            :, col:col + (NB - 1) * (P + 1) + 1:P + 1]
                                        ins = dve.tensor_copy(diag, src[:, r, :])
                            ins.then_inc(q_pad_ready, 1)
                            dve.wait_ge(q_pad_ready, l + 1)
                    elif step == "v_new":
                        for n in (VW, VW + 1):
                            wait_emptied(dve, l, "dense", n)
                        dve.tensor_copy(v_new_c[:, :, :, :], h[:, VS:VS + 4, SEQ:T].rearrange(
                            "p (a g) b -> p g a b", a=2)).then_inc(v_new_ready, 1)
                        dve.wait_ge(v_new_ready, l + 1)
                        wait_filled(dve, l, step, i)
                        emptied_by(dve.tensor_copy(v_new[:, :], bank[MI][0:2 * NB, 0:2 * P]), step, i)
                        dve.wait_ge(params_loaded, (l + 1) * 16)
                        for which, name in enumerate(("pe_k", "pe_v")):
                            src = (KC, VC)[which]
                            for gp in range(GP):
                                dve.tensor_copy(cmp_view[which][:, 16 + gp, :], h[:, src + gp, 0:SEQ])
                            dve.tensor_copy(cmp_view[which][:, 18, 0:TAPS], pr(name)).then_inc(cmp_in_ready, 1)
                            dve.wait_ge(cmp_in_ready, 2 * l + 1 + which)
                    elif step == "gates":
                        wait_emptied(dve, l, "dense", NG)
                        dve.tensor_tensor(gate_d[0:48, :, :],
                                          h[0:48, NG, SEQ:T].unsqueeze(1).to_broadcast([48, HEADS, NB]),
                                          c("gate_head")[0:48, :].unsqueeze(2).to_broadcast([48, HEADS, NB]),
                                          ALU.mult).then_inc(gate_d_ready, 1)
                        dve.wait_ge(gate_d_ready, l + 1)
                        wait_filled(dve, l, step, i)
                        link(dve.tensor_copy(gate[:, 0:96].rearrange("p (q n) -> p q n", q=2),
                                             bank[MI][:, 0:2 * P].rearrange("p (q n) -> p q n", q=2)[:, :, 0:48]))
                        emptied_by(dve.tensor_copy(gate[:, 96:99], bank[MI][:, 2 * P:2 * P + 3]), step, i)
                    elif step in ("cmp_k", "cmp_v"):
                        which = int(step == "cmp_v")
                        b = PT1 if which else PT0
                        wait_slot(dve, l, step, 0)
                        link(dve.tensor_copy(bias[:, which:which + 1], bank[b][:, 18 * NC:18 * NC + 1]))
                        out = (vc_all if which else kc_all)[:, :, :, 0:NC].rearrange("p g s c -> p s g c")
                        src = bank[b][:, 0:18 * NC].rearrange("p (s g c) -> p s g c", g=GP, c=NC)
                        for gp in range(GP):
                            ins = dve.tensor_scalar(out[:, :, gp, :], src[:, :, gp, :], bias[:, which:which + 1], None,
                                                    ALU.add)
                            if gp == 0:
                                link(ins)
                        emptied_by(ins, step, i)
                        wait_emptied(dve, l, step, 0)
                        if which:
                            dve.tensor_copy(vc_rep[:, :, :, :], vc_all[:, :, NB, :].unsqueeze(2).to_broadcast(
                                [P, GP, 8, CT])).then_inc(cmp_out_ready, 1)
                            dve.wait_ge(cmp_out_ready, l + 1)
                    elif step == "cmp_rope":
                        wait_filled(dve, l, step, i)
                        flat = kc_all[:, :, :, :].rearrange("p g s c -> p (g s) c")
                        rot = tmp[:, 0, :].rearrange("p (n c) -> p n c", c=CT)
                        emptied_by(dve.tensor_tensor(rot, bank[MI][:, 0:288].rearrange("p (n c) -> p n c", c=CT),
                                                     c("cmp_s").unsqueeze(1).to_broadcast([P, 18, CT]), ALU.mult),
                                   step, i)
                        link(dve.tensor_tensor(flat, flat, c("cmp_c").unsqueeze(1).to_broadcast([P, 18, CT]),
                                               ALU.mult))
                        wait_emptied(dve, l, step, i)
                        link(dve.tensor_tensor(flat, flat, rot, ALU.add))
                        for g2 in range(2):
                            rows = slice(g2 * HD, g2 * HD + HD)
                            ins = dve.tensor_copy(kc_bd[rows, :, g2, :], kc_all[rows, :, NB, :])
                        ins.then_inc(kc_ready, 1)
                        dve.wait_ge(kc_ready, l + 1)
                    elif step == "cmp_vrows":
                        wait_filled(dve, l, step, i)
                        for gp in range(GP):
                            dve.tensor_tensor(vc_bd[:, gp, :, :],
                                              bank[MI][:, gp * P:gp * P + P].unsqueeze(1).to_broadcast([P, R, P]),
                                              c("own_head").rearrange("p (r n) -> p r n", r=R), ALU.mult)
                        emptied_by(dve.tensor_copy(vc_one[:, :, :].rearrange("p g n -> p (g n)"),
                                                   bank[MI][:, 2 * P:4 * P]), step, i)
                    elif step == "cmp_scores":
                        wait_filled(dve, l, step, i)
                        mask = c("cmp_mask").rearrange("p (q c) -> p q c", q=2)
                        for qi in range(2):
                            ins = dve.tensor_tensor(cs[:, qi * 16:qi * 16 + 16, :], bank[SA][:, qi * 256:qi * 256 + 256]
                                                    .rearrange("p (n c) -> p n c", c=CT),
                                                    mask[:, qi, :].unsqueeze(1).to_broadcast([P, 16, CT]), ALU.add)
                            if qi == 0:
                                link(ins)
                        emptied_by(ins, step, i)
                        wait_emptied(dve, l, step, i)
                        link(dve.tensor_reduce(c_max[:, :], cs[:, :, :], AX_X, ALU.max))
                        link(dve.tensor_scalar(c_max[:, :], c_max[:, :], FLOOR, None, ALU.max))
                        dve.tensor_tensor(cs[:, :, :], cs[:, :, :], c_max[:, :].unsqueeze(2).to_broadcast([P, 32, CT]),
                                          ALU.subtract).then_inc(cmp_shifted, 1)
                        dve.wait_ge(cmp_shifted, l + 1)
                        dve.wait_ge(cmp_exped, l + 1)
                        link(dve.tensor_reduce(c_sum[:, :], cs[:, :, :], AX_X, ALU.add))
                        link(dve.tensor_scalar(c_sum[:, :], c_sum[:, :], 1e-30, None, ALU.max))
                        link(dve.reciprocal(c_sum[:, :], c_sum[:, :]))
                        wait_emptied(dve, l, "gates", 0)
                        link(dve.tensor_tensor(c_sum[:, :].rearrange("p (q n) -> p q n", q=2),
                                               c_sum[:, :].rearrange("p (q n) -> p q n", q=2),
                                               gate[:, 0:96].rearrange("p (q n) -> p q n", q=2)[:, :, 0:16], ALU.mult))
                        dve.tensor_tensor(cs[:, :, :], cs[:, :, :], c_sum[:, :].unsqueeze(2).to_broadcast([P, 32, CT]),
                                          ALU.mult).then_inc(cmp_probs, 1)
                        dve.wait_ge(cmp_probs, l + 1)
                    elif step == "scores":
                        for j, n in enumerate((2 * P, P)):
                            wait_filled(dve, l, step, i, j)
                            link(dve.tensor_reduce(u_fac[:, i % 2, 2 * j:2 * j + 2],
                                                   bank[(SA, SB)[j]][:, 0:2 * n].rearrange("p (a n) -> p a n", a=2),
                                                   AX_X, ALU.max))
                        dve.tensor_scalar(u_max[:, i % 2, :], u_fac[:, i % 2, :], -QK, None, ALU.mult
                                          ).then_inc(max_ready, 1)
                        dve.wait_ge(max_ready, l * HEADS + i + 1)
                    elif step == "turn":
                        wait_emptied(dve, l, "scores", i, 0)
                        wait_emptied(dve, l, "scores", i, 1)
                        fac = u_fac[:, i % 2, :]
                        link(dve.tensor_scalar(fac, u_sum[:, i % 2, :], 1e-30, None, ALU.max))
                        link(dve.reciprocal(fac, fac))
                        link(dve.tensor_tensor(fac.rearrange("p (q a) -> p q a", q=2),
                                               fac.rearrange("p (q a) -> p q a", q=2),
                                               gate[:, 0:96].rearrange("p (q a n) -> p q a n", q=2, a=3)[:, :, 1:3, i],
                                               ALU.mult))
                        at = 0
                        for j, n in enumerate((256, 256, 128, 128)):
                            ins = dve.tensor_scalar(probs[:, i % 2, at:at + n], probs[:, i % 2, at:at + n],
                                                    u_fac[:, i % 2, j:j + 1], None, ALU.mult)
                            at += n
                        ins.then_inc(probs_ready, 1)
                        dve.wait_ge(probs_ready, l * HEADS + i + 1)
                        wait_filled(dve, l, step, i, 1)
                        if i >= 2:
                            if i % 2:
                                wait_filled(dve, l, "pv", i - 2)
                            else:
                                dve.wait_ge(pv_even, l * 8 + i // 2)
                        emptied_by(dve.tensor_copy(probs_t[:, i % 2, 1, :], bank[PT1][:, 0:384]), step, i, 1)
                    elif step == "pool":
                        for n in (PU + 2, PU + 3):
                            wait_emptied(dve, l, "dense", n)
                        dve.tensor_copy(pu_ext[:, :, HIST:NE], h[:, PU:PU + 4, 0:SEQ])
                        dve.tensor_copy(pu_one[:, :, :, 0:HIST], pr("pool_hist").rearrange(
                            "p (g b t) -> p g b t", g=4, b=NB))
                        dve.tensor_copy(pu_one[:, :, :, HIST], h[:, PU:PU + 4, SEQ:T]).then_inc(state_ready, 1)
                        dve.wait_ge(state_ready, 2 * l + 1)
                        src, dst, shift = pu_ext[:, :, :], [sum_a, sum_b], 1
                        for k in range(4):
                            to = dst[k % 2]
                            first = 2 * shift - 1
                            link(dve.tensor_tensor(to[:, k:4, first:NE], src[:, k:4, first:NE],
                                                   src[:, k:4, first - shift:NE - shift], ALU.add))
                            src, shift = to, 2 * shift
                        for k, w in enumerate(WINDOWS):
                            s = dst[k % 2]
                            dve.scalar_tensor_tensor(out=h[:, PU + k, 0:SEQ], in0=s[:, k, HIST:NE], scalar=1.0 / w,
                                                     in1=pu_ext[:, k, HIST:NE], op0=ALU.mult, op1=ALU.subtract)
                            ins = dve.tensor_tensor(tmp[:, 0, k * CT:k * CT + CT], s[:, k, HIST:HIST + CT],
                                                    c("inv_count")[:, k * CT:k * CT + CT], ALU.mult)
                            ins = dve.tensor_reduce(pu_sum[:, k, :], pu_one[:, k, :, HIST + 1 - w:HIST + 1], AX_X,
                                                    ALU.add)
                        link(ins)
                        for k, w in enumerate(WINDOWS):
                            dve.tensor_tensor(h[:, PU + k, 0:CT], tmp[:, 0, k * CT:k * CT + CT],
                                              pu_ext[:, k, HIST:HIST + CT], ALU.subtract)
                            ins = dve.scalar_tensor_tensor(out=h[:, PU + k, SEQ:T], in0=pu_sum[:, k, :],
                                                           scalar=1.0 / w, in1=pu_one[:, k, :, HIST],
                                                           op0=ALU.mult, op1=ALU.subtract)
                        ins.then_inc(pooled, 1)
                        dve.wait_ge(pooled, l + 1)
                    elif step == "conv":
                        for n in (CX + 2, CX + 3):
                            wait_emptied(dve, l, "dense", n)
                        dve.memset(hc_ext[:, :, 0:2], 0.0)
                        dve.tensor_tensor(hc_ext[:, :, 2:2 + SEQ], h[:, CC:CC + 4, 0:SEQ], h[:, CX:CX + 4, 0:SEQ],
                                          ALU.mult)
                        dve.tensor_copy(hc_one[:, :, 0:2, :], pr("conv_hist").rearrange("p (g j b) -> p g j b",
                                                                                       g=4, j=2))
                        dve.tensor_tensor(hc_one[:, :, 2, :], h[:, CC:CC + 4, SEQ:T], h[:, CX:CX + 4, SEQ:T],
                                          ALU.mult).then_inc(state_ready, 1)
                        dve.wait_ge(state_ready, 2 * l + 2)
                        for j in range(3):
                            for k in range(4):
                                w = pr("conv_w", k * 3 + j, 1)
                                for dst, src in ((h[:, CC + k, 0:SEQ], hc_ext[:, k, j:j + SEQ]),
                                                 (h[:, CC + k, SEQ:T], hc_one[:, k, j, :])):
                                    if j == 0:
                                        ins = dve.tensor_scalar(dst, src, w, None, ALU.mult)
                                    else:
                                        ins = dve.scalar_tensor_tensor(out=dst, in0=src, scalar=w, in1=dst,
                                                                       op0=ALU.mult, op1=ALU.add)
                            link(ins)
                        dve.tensor_tensor(h[:, CB:CB + 4, :], h[:, CB:CB + 4, :], h[:, CC:CC + 4, :], ALU.mult
                                          ).then_inc(convolved, 1)
                        dve.wait_ge(convolved, l + 1)
                    elif step == "one_cmp_scores":
                        wait_filled(dve, l, step, i)
                        link(dve.tensor_reduce(one_max[:, 2:3], bank[SB][:, 0:NC], AX_X, ALU.max))
                        dve.tensor_scalar(one_max[:, 2:3], one_max[:, 2:3], -QK, None, ALU.mult
                                          ).then_inc(one_max_ready, 1)
                        dve.wait_ge(one_max_ready, 3 * l + 1)
                        dve.tensor_copy(k_one[:, :, :, PAST], h[:, KS:KS + 2, SEQ:T].rearrange("p g b -> p b g")
                                        ).then_inc(k_new_ready, 1)
                        dve.wait_ge(k_new_ready, 2 * l + 1)
                        wait_emptied(dve, l, step, i)
                        link(dve.tensor_scalar(one_sum[:, 2:3], one_sum[:, 2:3], 1e-30, None, ALU.max))
                        link(dve.reciprocal(one_sum[:, 2:3], one_sum[:, 2:3]))
                        link(dve.tensor_tensor(one_sum[:, 2:3], one_sum[:, 2:3], gate[:, 96:97], ALU.mult))
                        link(dve.tensor_scalar(p_cmp[:, :], p_cmp[:, :], one_sum[:, 2:3], None, ALU.mult))
                        link(dve.tensor_tensor(p_cmp_x[:, :, :], p_cmp[:, :].unsqueeze(1).to_broadcast([P, NB, CT]),
                                               c("own_row").unsqueeze(2).to_broadcast([P, NB, CT]), ALU.mult))
                    elif step == "one_scores":
                        src = bank[(SA, PT0)[i]]
                        wait_filled(dve, l, step, i)
                        link(dve.tensor_reduce(one_max[:, i:i + 1], src[:, 0:KEYS], AX_X, ALU.max))
                        dve.tensor_scalar(one_max[:, i:i + 1], one_max[:, i:i + 1], -QK, None, ALU.mult
                                          ).then_inc(one_max_ready, 1)
                        dve.wait_ge(one_max_ready, 3 * l + 2 + i)
                        if i == 0:
                            dve.tensor_copy(k_one[:, :, :, PAST], h[:, KW:KW + 2, SEQ:T].rearrange("p g b -> p b g")
                                            ).then_inc(k_new_ready, 1)
                            dve.wait_ge(k_new_ready, 2 * l + 2)
                        wait_emptied(dve, l, step, i)
                        link(dve.tensor_scalar(one_sum[:, i:i + 1], one_sum[:, i:i + 1], 1e-30, None, ALU.max))
                        link(dve.reciprocal(one_sum[:, i:i + 1], one_sum[:, i:i + 1]))
                        link(dve.tensor_tensor(one_sum[:, i:i + 1], one_sum[:, i:i + 1], gate[:, 97 + i:98 + i],
                                               ALU.mult))
                        link(dve.tensor_scalar(p_one[:, i, :], p_one[:, i, :], one_sum[:, i:i + 1], None, ALU.mult))
                        dve.tensor_scalar(p_tail[:, i, :], c("own_row"), p_one[:, i, PAST:KEYS], None, ALU.mult
                                          ).then_inc(one_probs, 1)
                        dve.wait_ge(one_probs, 2 * l + i + 1)
                    elif step == "one_cmp_turn":
                        wait_filled(dve, l, step, i)
                        link(dve.tensor_copy(p_cmp_t[:, :], bank[MI][:, 0:P]))
                        emptied_by(dve.tensor_copy(p_tail_t[:, :], bank[MI][0:2 * NB, P:2 * P]), step, i)
                    elif step == "one_pv" and i == 1:
                        wait_filled(dve, l, step, i)
                        for g2 in range(2):
                            rows = slice(g2 * HD, g2 * HD + HD)
                            src = bank[OT][rows, 0:P].rearrange("p (n a b) -> p n a b", a=2, b=NB)[:, :, g2, :]
                            ins = dve.tensor_copy(h[rows, Q:Q + 8, SEQ:T], src)
                            if g2 == 0:
                                link(ins)
                        emptied_by(ins, step, i)
                    elif step == "silu":
                        dve.wait_ge(sigmoids, 3 * l + 1)
                        link(dve.tensor_tensor(z[:, 0:4, :], z[:, 0:4, :], h[:, PZ:PZ + 4, :], ALU.mult))
                    elif step == "mix":
                        wait_filled(dve, l, step, i)
                        emptied_by(dve.scalar_tensor_tensor(out=h[:, PU + i, :], in0=bank[FILL[step, i, 0][0]][:, 0:T],
                                                            scalar=pr("pool_scale", i, 1), in1=z[:, i, :],
                                                            op0=ALU.mult, op1=ALU.mult), step, i)
                        if i == 3:
                            dve.wait_ge(sigmoids, 3 * l + 2)
                            link(dve.tensor_tensor(z[:, 4:8, :], z[:, 4:8, :], h[:, CZ:CZ + 4, :], ALU.mult))
                            dve.tensor_tensor(h[:, CB:CB + 4, :], h[:, CB:CB + 4, :], z[:, 4:8, :], ALU.mult
                                              ).then_inc(y_ready, 1)
                            dve.wait_ge(y_ready, 2 * l + 1)
                            dve.wait_ge(sigmoids, 3 * l + 3)
                            link(dve.tensor_tensor(m[:, :, :], m[:, :, :], h[:, AZ:AZ + 8, :], ALU.mult))
                            wait_emptied(dve, l, "pv", HEADS - 1)
                            wait_emptied(dve, l, "one_pv", 1)
                            dve.tensor_tensor(h[:, Q:Q + 8, :], h[:, Q:Q + 8, :], m[:, :, :], ALU.mult
                                              ).then_inc(y_ready, 1)
                            dve.wait_ge(y_ready, 2 * l + 2)
                    elif step == "merge":
                        for j in range(3):
                            wait_emptied(dve, l, step, i, j)
                        wait_slot(dve, l, step, SLOT_MERGE + 5 * i + 3)
                        banks = [bank[FILL[step, i, 3 + j][0]] for j in range(3)]
                        emptied_by(dve.tensor_tensor(m[:, i, :], g[:, i % 2, 0, :], banks[0][:, 0:T], ALU.mult),
                                   step, i, 3)
                        emptied_by(dve.tensor_tensor(tmp[:, 0, 0:T], g[:, i % 2, 1, :], banks[1][:, 0:T], ALU.mult),
                                   step, i, 4)
                        wait_slot(dve, l, step, SLOT_MERGE + 5 * i + 4)
                        emptied_by(dve.tensor_tensor(tmp[:, 1, 0:T], g[:, i % 2, 2, :], banks[2][:, 0:T], ALU.mult),
                                   step, i, 5)
                        wait_emptied(dve, l, step, i, 3)
                        wait_emptied(dve, l, step, i, 4)
                        link(dve.tensor_tensor(m[:, i, :], m[:, i, :], tmp[:, 0, 0:T], ALU.add))
                        wait_emptied(dve, l, step, i, 5)
                        dve.tensor_tensor(m[:, i, :], m[:, i, :], tmp[:, 1, 0:T], ALU.add).then_inc(merged, 1)
                        dve.wait_ge(merged, l * KT8 + i + 1)
                    elif step == "out":
                        wait_slot(dve, l, step, i)
                        emptied_by(dve.scalar_tensor_tensor(out=z[:, i, :], in0=x[:, i, :], scalar=ALPHA,
                                                            in1=bank[FILL[step, i, 0][0]][:, 0:T],
                                                            op0=ALU.mult, op1=ALU.add), step, i)
                    elif step == "norm":
                        dve.wait_ge(mean_ready, l + 1)
                        wait_emptied(dve, l, "out", KT8 - 1)
                        wait_emptied(dve, l, "out", KT8 - 2)
                        for k in range(4):
                            part = z[:, 2 * k:2 * k + 2, :]
                            dve.tensor_tensor(part, part, bank[SA][:, 0:T].unsqueeze(1).to_broadcast([P, 2, T]),
                                              ALU.subtract).then_inc(centered, 1)
                            dve.wait_ge(centered, l * 4 + k + 1)
                        dve.wait_ge(std_ready, l + 1)
                        link(dve.reciprocal(rstd[:, :], rstd[:, :]))
                        dve.wait_ge(kv_stored, (l + 1) * 16)
                        dve.wait_ge(state_stored, (l + 1) * 16)
                        for k in range(4):
                            part = z[:, 2 * k:2 * k + 2, :]
                            link(dve.tensor_tensor(part, part, rstd[:, :].unsqueeze(1).to_broadcast([P, 2, T]),
                                                   ALU.mult))
                            for n in (2 * k, 2 * k + 1):
                                dve.tensor_scalar(x[:, n, :], z[:, n, :], pr("ln_g", n, 1), pr("ln_b", n, 1),
                                                  ALU.mult, ALU.add).then_inc(x_ready, 1)
                                dve.wait_ge(x_ready, (l + 1) * KT8 + n + 1)
                assert steps[0] == VECTOR_STEPS, f"VECTOR_STEPS is {steps[0]}"


def _constants():
    t = {k: np.zeros((P, n), np.float32) for k, (_, n) in CST.items()}
    half = 8
    inv = (1.0 / (500000.0 ** (np.arange(0, 16, 2, dtype=np.float32) / 16))).astype(np.float32)
    pos = np.concatenate([np.arange(SEQ), np.full(NB, PAST)]).astype(np.float32)
    cpos = (np.arange(NC) * CT + TAPS - 1).astype(np.float32)
    for cos, sin, at in (("rope_c", "rope_s", pos), ("cmp_c", "cmp_s", cpos)):
        ang = (at[None, :] * inv[:, None]).astype(np.float32).astype(np.float64)
        n = len(at)
        t[cos][:, 0:n] = 1.0
        for g2 in range(2):
            a = g2 * HD
            t[cos][a:a + half, 0:n] = np.cos(ang)
            t[cos][a + half:a + 2 * half, 0:n] = np.cos(ang)
            t[sin][a:a + half, 0:n] = -np.sin(ang)
            t[sin][a + half:a + 2 * half, 0:n] = np.sin(ang)
    for g2 in range(2):
        for d in range(half):
            t["perm"][g2 * HD + d, g2 * HD + d + half] = 1.0
            t["perm"][g2 * HD + d + half, g2 * HD + d] = 1.0
    t["ident"] = np.eye(P, dtype=np.float32)
    q = np.arange(P)
    t["causal"] = np.where(q[None, :] <= q[:, None], 0.0, MASKED).astype(np.float32)
    end = np.arange(CT) * CT + TAPS - 1
    for qi in range(2):
        rows = q + (1 - qi) * P
        ok = (end[None, :] <= rows[:, None]) & (np.arange(CT)[None, :] < NC)
        t["cmp_mask"][:, qi * CT:(qi + 1) * CT] = np.where(ok, 0.0, MASKED)
    t["own_row"] = (q[:, None] % NB == np.arange(NB)[None, :]).astype(np.float32)
    r_of, g_of = q // 32, q // CT % 2
    for r in range(R):
        t["own_head"][:, r * P:(r + 1) * P] = ((r_of == r)[:, None] & (g_of[:, None] == (q // HD)[None, :]))
    for k, w in enumerate(WINDOWS):
        t["inv_count"][:, k * CT:(k + 1) * CT] = (1.0 / np.minimum(w, np.arange(CT) + 1)).astype(np.float32)
    t["gate_head"] = (q[:, None] % HEADS == np.arange(HEADS)[None, :]).astype(np.float32)
    t["gate_type"] = (q[:, None] // HEADS == np.arange(3)[None, :]).astype(np.float32)
    return np.concatenate([t[k] for k in CST], axis=1).astype(np.float32)


def kernel(**inputs):
    import concourse.bacc as _bacc
    from concourse.bass_utils import run_bass_kernel_spmd as _run

    a = {k: np.asarray(v) for k, v in inputs.items()}
    D = DEPTH

    def tiles(w):
        _, kk, n = w.shape
        return w.reshape(D, kk // P, P, n // P, P).transpose(0, 3, 2, 1, 4).reshape(D, n // P, P, kk // P * P)

    sizes = (512, 512, 512, 512, 512, 512, 1024, 256, 256, 256, 256, 256, 256, 48, 1024, 3072)
    at = dict(zip(("pu", "pz", "cb", "cc", "cx", "cz", "q", "kc", "vc", "ks", "vs", "kw", "vw", "ng", "az", "mg"),
                  np.concatenate([[0], np.cumsum(sizes)[:-1]])))
    head = np.arange(HEADS).reshape(GP, 2, R).transpose(0, 2, 1).reshape(-1)
    by_head = (head[:, None] * HD + np.arange(HD)[None, :]).reshape(-1)
    w_in = a["w_in"]

    def part(name, n):
        return w_in[:, :, at[name]:at[name] + n]

    ng = np.zeros((D, D_MODEL, P), np.float32)
    ng[:, :, 0:48] = w_in[:, :, at["ng"] + (head[None, :] * 3 + np.arange(3)[:, None]).reshape(-1)]
    first = tiles(np.concatenate([part("kc", 256), part("vc", 256), part("ks", 256), part("kw", 256),
                                  part("vs", 256), part("vw", 256), w_in[:, :, at["q"] + by_head], ng], axis=2))
    second = tiles(np.concatenate([part("pu", 512), part("pz", 512), part("cb", 512), part("cc", 512),
                                   part("cx", 512), part("cz", 512), w_in[:, :, at["az"] + by_head]], axis=2))
    taps = a["cmp_w"].reshape(D, 2, TAPS, HD, HD).transpose(0, 1, 3, 2, 4)
    cmp = np.zeros((D, 2, 2, HD, TAPS, 2, HD), np.float32)
    for g2 in range(2):
        cmp[:, :, g2, :, :, g2, :] = taps
    cmp = cmp.reshape(D, 2, P, 4, 8 * P).transpose(0, 1, 3, 2, 4).reshape(D, 8, P, 8 * P)
    mg = tiles(part("mg", 3072)).reshape(D, 3, KT8, P, 8 * P)
    ab = np.concatenate([tiles(a["proj_a"]), tiles(a["proj_b"])], axis=3)
    pc = tiles(a["proj_c"][:, by_head, :])
    merge = np.stack([mg[:, 0], mg[:, 1], mg[:, 2], ab, pc], axis=2).reshape(D, 5 * KT8, P, 8 * P)
    weights = np.concatenate([first, cmp, second, merge, tiles(a["w_out"])], axis=1)

    def by_part(v, n):
        return v.reshape(D, n, P).transpose(0, 2, 1)

    pe = a["cmp_pe"].transpose(0, 1, 3, 2)
    pe = np.concatenate([pe, pe], axis=2)
    params = np.concatenate([
        by_part(a["pool_scale"], 4),
        a["conv_w"].reshape(D, 3, 4, P).transpose(0, 3, 2, 1).reshape(D, P, 12),
        by_part(a["ln_g"], 8), by_part(a["ln_b"], 8), pe[:, 0], pe[:, 1],
        a["state_pool"].reshape(D, NB, HIST, 4, P).transpose(0, 4, 3, 1, 2).reshape(D, P, -1),
        a["state_conv"].reshape(D, NB, 2, 4, P).transpose(0, 4, 3, 2, 1).reshape(D, P, -1),
        a["pool_w"].transpose(0, 2, 1, 3).reshape(D, P, 4 * P)], axis=2)
    xs = np.concatenate([a["x_prompt"].reshape(SEQ, D_MODEL), a["x_sample"].reshape(NB, D_MODEL)], axis=0)
    pool_n = a["cache_k_cmp"].shape[1]

    def cache_cols(v):
        return v.reshape(D, pool_n, P, GP, P).transpose(0, 1, 4, 3, 2)

    arrays = {
        "x_in": xs.T.reshape(KT8, P, T).transpose(1, 0, 2), "weights": weights, "params": params,
        "consts": _constants(), "pages": a["page_table"].reshape(1, -1).astype(np.int32),
        "kcmp": cache_cols(a["cache_k_cmp"]), "vcmp": cache_cols(a["cache_v_cmp"]),
        "ksel": cache_cols(a["cache_k_sel"]), "vsel": a["cache_v_sel"].reshape(D, pool_n, P, 4 * HD),
        "kwin": a["state_k_win"].reshape(D, NB, PAST, GP, P).transpose(0, 4, 1, 3, 2).reshape(D, P, NB * GP, PAST),
        "vwin": a["state_v_win"].reshape(D, NB, 2, P, 4 * HD).transpose(0, 3, 1, 2, 4).reshape(D, P, -1),
    }
    outs = {"y": (P, KT8, T), "kv": (D, P, 12, T), "state": (D, P, N_ST),
            "kwin_out": (D, P, NB * GP, PAST), "vwin_out": (D, P, NB * 4 * HD * 2)}
    nc = _bacc.Bacc("TRN2", target_bir_lowering=False, num_devices=1)
    args = []
    for name in arrays:
        arrays[name] = np.ascontiguousarray(arrays[name])
        args.append(nc.dram_tensor(name + "_dram", arrays[name].shape, mybir.dt.from_np(arrays[name].dtype),
                                   kind="ExternalInput").ap())
    for name, shape in outs.items():
        args.append(nc.dram_tensor(name + "_dram", shape, F32, kind="ExternalOutput").ap())
    trunk(nc, *args)
    got = _run(nc, [{name + "_dram": v for name, v in arrays.items()}], core_ids=[0]).results[0]
    got = {name: got[name + "_dram"] for name in outs}

    y = np.asarray(got["y"]).transpose(2, 1, 0).reshape(T, D_MODEL)
    kv = np.asarray(got["kv"]).reshape(D, P, 6, GP, T).transpose(2, 0, 4, 3, 1).reshape(6, D, T, 4, HD)
    kc, vc, ks, kw, vs, vw = (kv[n] for n in range(6))
    st = np.asarray(got["state"])

    def p_of(v):
        return v[:, 0:SEQ].reshape(D, 1, SEQ, 4, HD)

    def s_of(v):
        return v[:, SEQ:T].reshape(D, NB, 1, 4, HD)

    kwo = np.asarray(got["kwin_out"]).reshape(D, P, NB, GP, PAST).transpose(0, 2, 4, 3, 1).reshape(D, NB, PAST, 4, HD)
    vwo = np.asarray(got["vwin_out"]).reshape(D, P, NB, 2, 4 * HD).transpose(0, 2, 3, 1, 4).reshape(
        D, NB, PAST, 4, HD)
    p_pool = st[:, :, ST_PP:ST_PS].reshape(D, P, 4, HIST).transpose(0, 3, 2, 1).reshape(D, 1, HIST, 512)
    s_pool = st[:, :, ST_PS:ST_CP].reshape(D, P, 4, NB, HIST).transpose(0, 3, 4, 2, 1).reshape(D, NB, HIST, 512)
    p_conv = st[:, :, ST_CP:ST_CS].reshape(D, P, 4, 2).transpose(0, 3, 2, 1).reshape(D, 1, 2, 512)
    s_conv = st[:, :, ST_CS:N_ST].reshape(D, P, 4, 2, NB).transpose(0, 4, 3, 2, 1).reshape(D, NB, 2, 512)
    out = (y[0:SEQ].reshape(1, SEQ, D_MODEL), y[SEQ:T].reshape(NB, 1, D_MODEL),
           p_of(kc), p_of(vc), p_of(ks), p_of(vs), p_of(kw), p_of(vw), p_pool, p_conv,
           s_of(kc), s_of(vc), s_of(ks), s_of(vs),
           np.concatenate([kwo, s_of(kw)], axis=2), np.concatenate([vwo, s_of(vw)], axis=2), s_pool, s_conv)
    return tuple(np.ascontiguousarray(v) for v in out)
```

```python
from contextlib import ExitStack

import numpy as np

import concourse.bass as bass
from concourse import mybir

F32 = mybir.dt.float32
F32R = mybir.dt.float32r
BF16 = mybir.dt.bfloat16
I32 = mybir.dt.int32
ALU = mybir.AluOpType
ACT = mybir.ActivationFunctionType
AX_X = mybir.AxisListType.X

P = 128
DEPTH = 2
D_MODEL = 1024
SEQ = 256
NB = 8
T = SEQ + NB
PAST = 256
KEYS = PAST + 1
HD = 64
HEADS = 16
GP = 2
R = 4
CT = 16
TAPS = 32
NC = 15
KT8 = D_MODEL // P
ALPHA = (2 * DEPTH) ** 0.25
EPS = 1e-5
QK = HD ** -0.5
MASKED = -1.0e30
FLOOR = -1.0e29
WINDOWS = (2, 4, 8, 16)
HIST = 15

KC, VC, KS, KW, VS, VW, Q, NG = 0, 2, 4, 6, 8, 10, 12, 20
PU, CB, CC, CX, PZ, CZ, AZ = 21, 25, 29, 33, 37, 41, 45
KEPT = 53
LATE = 38
Y_A_HI, Y_B_HI, Y_C_HI, M_HI = VS, CZ, KC, AZ
LATE_PV = 46
ROPED = [KS, KS + 1, KW, KW + 1] + list(range(Q, Q + 8))

RING = 5
PRM = {}
_at = 0
for _name, _n in (("pool_scale", 4), ("conv_w", 12), ("ln_g", 8), ("ln_b", 8), ("pe_k", TAPS), ("pe_v", TAPS),
                  ("pool_hist", 4 * NB * HIST), ("conv_hist", 4 * 2 * NB), ("pool_w", 4 * P)):
    PRM[_name] = (_at, _n)
    _at += _n
N_PRM = _at
CST = {}
_at = 0
for _name, _n in (("rope_c", T), ("rope_s", T), ("cmp_c", CT), ("cmp_s", CT), ("ident", P), ("perm", P),
                  ("causal", P), ("cmp_mask", 2 * CT), ("own_row", NB), ("own_head", 4 * P),
                  ("inv_count", 4 * CT), ("gate_head", HEADS), ("gate_type", 3)):
    CST[_name] = (_at, _n)
    _at += _n
N_CST = _at
ST_PP, ST_PS, ST_CP, ST_CS, N_ST = 0, 60, 540, 548, 612


def make_order():
    order = []
    for n in range(21):
        order.append(("dense", n))
        if n - 1 in ROPED:
            order.append(("rope", n - 1))
        if n == 13:
            order += [("v_rows", 0), ("v_rows", 1)]
        if n == 15:
            order.append(("v_new_in", 0))
        if n == 17:
            order.append(("v_new", 0))
    order += [("cmp_k", 0), ("gates", 0), ("cmp_v", 0), ("cmp_rope", 0), ("dense", 21), ("cmp_vrows", 0),
              ("cmp_scores", 0), ("dense", 22), ("dense", 23), ("cmp_turn", 0), ("dense", 24)]
    nxt = 25
    for u in range(HEADS):
        order.append(("scores", u))
        if u > 0:
            order.append(("turn", u - 1))
        order.append(("dense", nxt))
        nxt += 1
        if u > 0:
            order.append(("pv", u - 1))
        order.append(("scale", u))
        if 1 <= u <= POOL_STAGES:
            order.append(("pool", u - 1))
    order += [("one_cmp_scores", 0), ("one_scores", 0), ("turn", HEADS - 1), ("dense", 41), ("pv", HEADS - 1),
              ("one_turn", 0), ("dense", 42), ("conv", 0), ("dense", 43), ("conv", 1), ("one_pv", 0),
              ("conv", 2), ("conv", 3), ("one_scores", 1), ("dense", 44), ("one_turn", 1), ("one_cmp_turn", 0),
              ("dense", 45), ("one_pv", 1), ("silu", 0), ("silu", 1), ("conv", 4), ("y", 0),
              ("dense", 46), ("mix", 0), ("mix", 1), ("y_high", 0), ("dense", 47), ("mix", 2), ("mix", 3),
              ("dense", 48), ("y_rest", 0), ("y_high", 1), ("dense", 49), ("y", 2), ("dense", 50), ("y_high", 2),
              ("y_rest", 1)]
    late = [("dense", 51), ("dense", 52)] + [("gate", n) for n in range(3 * GATE_RING)]
    for n, s in enumerate(late):
        order.append(s)
        part = 2 + n // 2
        if n % 2 == 0 and part <= 5:
            order.append(("y_rest", part))
            if part < 5:
                order.append(("y", part + 1))
        elif part < 5:
            order.append(("y_high", part + 1))
    for i in range(KT8):
        order.append(("merge", i))
        if i + GATE_RING < KT8:
            order += [("gate", 3 * (i + GATE_RING) + j) for j in range(3)]
    for i in range(KT8):
        order.append(("out", i))
        if i:
            order.append(("mean", i - 1))
    order += [("mean", KT8 - 1), ("norm", 0)]
    return order


POOL_STAGES = 8
GATE_RING = 3
Y_PARTS = [(CB, Y_B_HI, 4), (PU, Y_A_HI, 4)] + [(Q + 2 * n, Y_C_HI + 2 * n, 2) for n in range(4)]
ORDER = make_order()
_silu = [s for s in ORDER if s[0] == "silu" or s[0] == "dense" and s[1] >= AZ]
SIGMOIDS, SIGMOIDS_BEFORE = len(_silu), {s: n + 1 for n, s in enumerate(_silu)}
SLOTS_OF_STEP = {"dense": 1, "cmp_k": 4, "cmp_v": 4, "gate": 1, "merge": 2, "out": 1}
SLOT_OF, SLOTS = {}, 0
for _step in ORDER:
    if _step[0] in SLOTS_OF_STEP:
        SLOT_OF[_step] = SLOTS
        SLOTS += SLOTS_OF_STEP[_step[0]]
SLOT_CK, SLOT_CV = SLOT_OF["cmp_k", 0], SLOT_OF["cmp_v", 0]
SPLIT_SLOTS = [n for n in range(SLOTS) if not SLOT_CK <= n < SLOT_CV + 4]
SPLIT_NO = {n: d for d, n in enumerate(SPLIT_SLOTS)}
SPLITS = len(SPLIT_SLOTS)
HI_RING = 3
D0, D1, SA, SB, PT0, PT1, OT, MI = range(8)


def banks_of(step, i):
    if step == "dense":
        return [i % 2]
    if step == "gate":
        return [(KEPT + i) % 2]
    if step == "merge":
        return [SA, SB, PT0] if i % 2 == 0 else [PT1, OT, MI]
    if step == "out":
        return [(KEPT + 3 * KT8 + i) % 2]
    if step == "turn":
        return [PT0, PT1]
    if step == "scores":
        return [SA, SB]
    if step == "pv":
        return [OT] if i % 2 else []
    if step == "mix":
        return [(SA, SB, PT0, PT1)[i]]
    if step == "v_rows":
        return [(PT0, PT1)[i]]
    if step == "one_scores":
        return [(SA, PT0)[i]]
    if step == "one_turn":
        return [(PT1, SB)[i]]
    if step == "one_pv":
        return [OT] if i else []
    return {"rope": [MI], "v_new": [MI], "cmp_k": [PT0], "gates": [MI], "cmp_v": [PT1], "cmp_rope": [MI],
            "cmp_vrows": [MI], "cmp_scores": [SA], "cmp_turn": [PT0], "one_cmp_scores": [SB],
            "one_cmp_turn": [MI]}.get(step, [])


def plan_fills():
    fill, total = {}, [0] * 8
    for step, i in ORDER:
        for j, b in enumerate(banks_of(step, i)):
            total[b] += 1
            fill[step, i, j] = (b, total[b])
    return fill, total


FILL, FILLS = plan_fills()
BY_SLOT = set(SLOTS_OF_STEP)
FILLED = [sum(1 for (s, i, j), (b, k) in FILL.items() if b == bank and s not in BY_SLOT) for bank in range(8)]


def filled_count(step, i, j):
    bank, k = FILL[step, i, j]
    return bank, sum(1 for (s, a, c), (b, m) in FILL.items() if b == bank and m <= k and s not in BY_SLOT)




def plan_splits():
    split = {}
    for step, i in ORDER:
        if step in SLOTS_OF_STEP and step not in ("cmp_k", "cmp_v"):
            used = [SPLIT_NO[SLOT_OF[step, i] + j] for j in range(SLOTS_OF_STEP[step])]
            split[step, i] = [d + 2 for d in used if d + 2 not in (SLOT_CK, SLOT_CK + 1)]
    for u in range(HEADS):
        split["scores", u] = split.pop(("dense", 25 + u))
    split["cmp_v", 0] = [SLOT_CK, SLOT_CK + 1]
    split["out", KT8 - 2], split["out", KT8 - 1], split["norm", 0] = [], [SPLITS], [SPLITS + 1]
    return split


SPLIT_AT = plan_splits()
SLOTS_IN = [sum(1 for i in range(SLOTS) if i % RING == s) for s in range(RING)]
VECTOR_STEPS = 150


def trunk(nc, x_in, weights, params, consts, pages, kcmp, vcmp, ksel, vsel, kwin, vwin,
          y_out, kv_out, state_out, kwin_out, vwin_out):
    n_pool = kcmp.shape[1]
    with ExitStack() as ctx:
        def sb(name, shape, dt=F32):
            return ctx.enter_context(nc.sbuf_tensor(name, shape, dt))

        def sem(name):
            return ctx.enter_context(nc.semaphore(name))

        bank = [ctx.enter_context(nc.psum_tensor(f"bank{b}", [P, 512], F32)) for b in range(8)]

        def shared(name, shape, at, dt=F32R):
            return nc.alloc_sbuf_tensor_at(name, shape, dt, offset=at)

        x_hi = sb("x_hi", [P, KT8, T], F32R)
        x_lo = sb("x_lo", [P, KT8, T], F32R)
        z = sb("z", [P, KT8, T])
        m_at = nc.sbuf_base
        m = sb("m", [P, KT8, T])
        m_lo = shared("m_lo", [P, KT8, T], m_at)
        h_at = nc.sbuf_base
        h = sb("h", [P, KEPT, T])
        h_r = shared("h_rounded", [P, KEPT, T], h_at)
        ring_at = nc.sbuf_base
        ring = sb("ring", [P, RING, KT8, P])
        w_lo = shared("w_lo", [P, RING, KT8, P], ring_at)
        w_hi = sb("w_hi", [P, HI_RING, KT8, P], F32R)
        cache_a = sb("cache_a", [P, 10 * GP * PAST])
        cache_b = sb("cache_b", [P, 10 * GP * PAST])
        prm = sb("prm", [P, N_PRM])
        cst = sb("cst", [P, N_CST])
        page = sb("page", [1, NB * 2], I32)
        causal_b = sb("causal_b", [P, P], BF16)
        ident_b = sb("ident_b", [P, P], BF16)
        ones = sb("ones", [P, P])
        eps = sb("eps", [P, 1])
        v_rows = sb("v_rows", [P, 2, 4 * P])
        v_new_c = sb("v_new_c", [P, GP, 2, NB])
        v_new = sb("v_new", [2 * NB, GP * P])
        gate = sb("gate", [P, 99])
        gate_d = sb("gate_d", [P, HEADS, NB])
        kc_all = sb("kc_all", [P, GP, NB + 1, CT])
        vc_all = sb("vc_all", [P, GP, NB + 1, CT])
        vc_rep = sb("vc_rep", [P, GP, 8, CT])
        kc_bd = sb("kc_bd", [P, GP, 2, CT])
        vc_one = sb("vc_one", [P, GP, P])
        bias = sb("bias", [P, 2])
        tmp = sb("tmp", [P, 3, 288])
        c_max = sb("c_max", [P, 32])
        c_sum = sb("c_sum", [P, 32])
        probs = sb("probs", [P, 2, 768])
        probs_t = sb("probs_t", [P, 2, 2, 384])
        u_max = sb("u_max", [P, 2, 4])
        u_sum = sb("u_sum", [P, 2, 4])
        u_fac = sb("u_fac", [P, 2, 4])
        p_cmp = sb("p_cmp", [P, CT])
        p_cmp_x = sb("p_cmp_x", [P, NB, CT])
        p_tail = sb("p_tail", [P, 2, NB])
        one_max = sb("one_max", [P, 3])
        one_sum = sb("one_sum", [P, 3])
        p_cmp_t = sb("p_cmp_t", [P, P])
        p_tail_t = sb("p_tail_t", [2 * NB, P])
        pu_one = sb("pu_one", [P, 4, NB, HIST + 1])
        pu_sum = sb("pu_sum", [P, 4, NB])
        hc_one = sb("hc_one", [P, 4, 3, NB])
        state = sb("state", [P, N_ST])
        rstd = sb("rstd", [P, T])

        NE = HIST + SEQ
        hf = h[:, LATE:KEPT, :].rearrange("p a t -> p (a t)")
        sum_a = hf[:, 0:4 * NE].rearrange("p (g t) -> p g t", g=4)
        sum_b = hf[:, 4 * NE:8 * NE].rearrange("p (g t) -> p g t", g=4)
        pc_t = hf[:, 8 * NE:8 * NE + GP * SEQ].rearrange("p (g t) -> p g t", g=GP)
        vc_at = 8 * NE + GP * SEQ
        vc_bd = hf[:, vc_at:vc_at + GP * R * P].rearrange("p (g r n) -> p g r n", g=GP, r=R)
        zf = z[:, :, :].rearrange("p a t -> p (a t)")
        mf = m[:, :, :].rearrange("p a t -> p (a t)")
        q_pad = zf[:, 0:GP * NB * P].rearrange("p (g b n) -> p g b n", g=GP, b=NB)
        pu_ext = mf[:, 0:4 * NE].rearrange("p (g t) -> p g t", g=4)
        hc_ext = mf[:, 0:4 * (2 + SEQ)].rearrange("p (g t) -> p g t", g=4)
        g = h[:, CC:CC + 3 * GATE_RING, :].rearrange("p (a j) t -> p a j t", j=3)
        probs_flat = probs[:, :, :].rearrange("p a n -> p (a n)")
        cs = probs_flat[:, 0:32 * CT].rearrange("p (n c) -> p n c", c=CT)
        p_one = probs_flat[:, 0:2 * KEYS].rearrange("p (a n) -> p a n", a=2)
        p_one_t = probs_t[:, :, :, :].rearrange("p a b n -> p (a b n)")[:, 0:4 * P].rearrange("p (a n) -> p a n", a=2)
        cmp_view = [c[:, :].rearrange("p (s t) -> p s t", t=PAST) for c in (cache_a, cache_b)]
        k_one = cache_a[:, 0:NB * GP * KEYS].rearrange("p (b g t) -> p b g t", b=NB, g=GP)
        v_one = cache_b[:, 0:NB * 2 * 2 * P].rearrange("p (b t n) -> p b t n", b=NB, t=2)

        def c(name):
            at, n = CST[name]
            return cst[:, at:at + n]

        def pr(name, i=0, n=None):
            at, size = PRM[name]
            return prm[:, at + i:at + i + (size if n is None else n)]

        ident, perm = c("ident"), c("perm")

        consts_loaded, x_loaded, pages_loaded = sem("consts_loaded"), sem("x_loaded"), sem("pages_loaded")
        params_loaded = sem("params_loaded")
        landed = [sem(f"weight_landed{s}") for s in range(RING)]
        cmp_k_landed, cmp_v_landed = sem("cmp_k_landed"), sem("cmp_v_landed")
        sel_k_landed, sel_v_landed = sem("sel_k_landed"), sem("sel_v_landed")
        win_k_landed, win_v_landed = sem("win_k_landed"), sem("win_v_landed")
        slots_done = sem("slots_done")
        x_ready = sem("x_ready")
        x_hi_ready = sem("x_hi_ready")
        w_hi_ready, w_lo_ready = sem("w_hi_ready"), sem("w_lo_ready")
        output_ready = sem("output_ready")
        scaled, residual = sem("scaled"), sem("residual")
        filled = [sem(f"bank{b}_filled") for b in range(8)]
        emptied = [sem(f"bank{b}_emptied") for b in range(8)]
        tables_ready = sem("tables_ready")
        vector_step = sem("vector_step")
        roped = sem("roped")
        cmp_in_ready = sem("cmp_in_ready")
        v_new_ready = sem("v_new_ready")
        gate_d_ready = sem("gate_d_ready")
        cmp_out_ready = sem("cmp_out_ready")
        kc_ready = sem("kc_ready")
        cmp_shifted, cmp_exped, cmp_probs = sem("cmp_shifted"), sem("cmp_exped"), sem("cmp_probs")
        max_ready, probs_ready, pv_even = sem("max_ready"), sem("probs_ready"), sem("pv_even")
        q_pad_clear, q_pad_ready = sem("q_pad_clear"), sem("q_pad_ready")
        k_new_ready = sem("k_new_ready")
        one_max_ready, one_exped, one_probs = sem("one_max_ready"), sem("one_exped"), sem("one_probs")
        sel_v_used = sem("sel_v_used")
        sigmoids = sem("sigmoids")
        pooled, convolved = sem("pooled"), sem("convolved")
        y_ready = sem("y_ready")
        y_hi_ready, y_split = sem("y_hi_ready"), sem("y_split")
        m_hi_ready, m_split = sem("m_hi_ready"), sem("m_split")
        merged, squared, std_ready = sem("merged"), sem("squared"), sem("std_ready")
        mean_ready, squared_sum, centered = sem("mean_ready"), sem("squared_sum"), sem("centered")
        state_ready, state_staged = sem("state_ready"), sem("state_staged")
        pool_goes = sem("pool_goes")
        kv_stored, state_stored, win_copied, y_stored = (
            sem("kv_stored"), sem("state_stored"), sem("win_copied"), sem("y_stored"))

        def split_weight(d):
            following, d = divmod(d, SPLITS)
            slot = SPLIT_SLOTS[d]
            return following, d, slot, slot % RING, d % HI_RING

        block = ctx.enter_context(nc.Block())

        def wait_slot(eng, l, step, i, j=None):
            s = SLOT_OF[step, i] + (SLOTS_OF_STEP[step] - 1 if j is None else j)
            eng.wait_ge(slots_done, l * SLOTS + RING + s + 1)

        def wait_filled(eng, l, step, i, j=0):
            b, k = filled_count(step, i, j)
            eng.wait_ge(filled[b], l * FILLED[b] + k)

        def wait_emptied(eng, l, step, i, j=0):
            b, k = FILL[step, i, j]
            eng.wait_ge(emptied[b], l * FILLS[b] + k)

        @block.sync
        def _(sp):
            def load(row, i):
                return sp.dma_start(ring[:, i % RING, :, :], weights[row].rearrange("a p (k n) -> (a p) k n", k=KT8)
                                    ).then_inc(landed[i % RING], 16)

            sp.dma_start(m[:, :, :], x_in).then_inc(x_loaded, 16)
            for i in range(2):
                load(slice(i, i + 1), i)
            sp.dma_start(cst[:, :], consts).then_inc(consts_loaded, 16)
            with sp.Fori(0, DEPTH) as l:
                for n in range(2, SLOTS + 2):
                    following, i = divmod(n, SLOTS)
                    before = i - RING if i >= RING else max(j for j in range(SLOTS) if j % RING == i) - SLOTS
                    sp.wait_ge(slots_done, (l + following) * SLOTS + RING + before + 1)
                    load(bass.ds(l * SLOTS + n, 1), i)
                    if n == RING:
                        sp.wait_ge(x_ready, l * (KT8 // 2) + KT8 // 2)
                        sp.dma_start(prm[:, :], params[l]).then_inc(params_loaded, 16)
            for n in range(2):
                half = slice(4 * n, 4 * n + 4)
                sp.wait_ge(output_ready, n + 1)
                sp.dma_start(y_out[:, half, :], m[:, half, :]).then_inc(y_stored, 16)
            sp.wait_ge(y_stored, 32)

        @block.gpsimd
        def _(pool):
            pool.dma_start(page[:, :], pages).then_inc(pages_loaded, 16)
            pool.wait_ge(pages_loaded, 16)

            def load_pages(l, cache, dst_of, landed_sem):
                with pool.Fori(0, NB) as b:
                    for half in range(2):
                        pg = pool.value_load(page[0:1, bass.ds(b * 2 + half, 1)], min_val=0, max_val=n_pool - 1)
                        pool.dma_start(dst_of(b, half), cache[bass.ds(l, 1), bass.ds(pg, 1)].rearrange(
                            "a b p n -> (a b p) n" if len(cache.shape) == 4 else "a b p g n -> (a b p) g n")
                            ).then_inc(landed_sem, 16)

            def cmp_dst(view):
                v = view.rearrange("p (s g) t -> p s g t", g=GP)
                return lambda b, half: v[:, bass.ds(b, 1), :, half * P:half * P + P].rearrange("p s g t -> p (s g) t")

            def go():
                pool.sem_inc(pool_goes, 1)

            with pool.Fori(0, DEPTH) as l:
                pool.wait_ge(x_ready, l * (KT8 // 2) + KT8 // 2)
                go()
                load_pages(l, kcmp, cmp_dst(cmp_view[0]), cmp_k_landed)
                load_pages(l, vcmp, cmp_dst(cmp_view[1]), cmp_v_landed)
                pool.wait_ge(roped, l * len(ROPED) + 4)
                wait_emptied(pool, l, "dense", VW)
                wait_emptied(pool, l, "dense", VW + 1)
                go()
                pool.dma_start(kv_out[l], h[:, 0:12, :]).then_inc(kv_stored, 16)
                wait_slot(pool, l, "cmp_k", 0)
                go()
                load_pages(l, ksel, lambda b, half: k_one[:, bass.ds(b, 1), :, half * P:half * P + P].rearrange(
                    "p s g t -> p (s g) t"), sel_k_landed)
                wait_slot(pool, l, "cmp_v", 0)
                go()
                load_pages(l, vsel, lambda b, half: v_one[:, bass.ds(b, 1), half, :].rearrange(
                    "p s n -> p (s n)"), sel_v_landed)
                pool.wait_ge(state_ready, 2 * l + 1)
                go()
                pool.tensor_copy(state[:, ST_PP:ST_PS].rearrange("p (g t) -> p g t", g=4),
                                 pu_ext[:, :, SEQ:SEQ + HIST])
                pool.tensor_copy(state[:, ST_PS:ST_CP].rearrange("p (g b t) -> p g b t", g=4, b=NB),
                                 pu_one[:, :, :, 1:HIST + 1]).then_inc(state_staged, 1)
                pool.wait_ge(state_ready, 2 * l + 2)
                go()
                pool.tensor_copy(state[:, ST_CP:ST_CS].rearrange("p (g t) -> p g t", g=4), hc_ext[:, :, SEQ:SEQ + 2])
                pool.tensor_copy(state[:, ST_CS:N_ST].rearrange("p (g j b) -> p g j b", g=4, j=2),
                                 hc_one[:, :, 1:3, :]).then_inc(state_staged, 1)
                pool.wait_ge(state_staged, 2 * l + 2)
                go()
                pool.dma_start(state_out[l], state[:, :]).then_inc(state_stored, 16)
                wait_filled(pool, l, "one_scores", 0)
                go()
                pool.dma_start(k_one[:, :, :, 0:PAST].rearrange("p b g t -> p (b g) t"),
                               kwin[bass.ds(l, 1)].rearrange("a p n t -> (a p) n t")).then_inc(win_k_landed, 16)
                pool.wait_ge(sel_v_used, l + 1)
                go()
                pool.dma_start(v_one.rearrange("p b t n -> p (b t n)"),
                               vwin[bass.ds(l, 1)].rearrange("a p n -> (a p) n")).then_inc(win_v_landed, 16)
                pool.dma_start(kwin_out[l], kwin[l]).then_inc(win_copied, 16)
                pool.dma_start(vwin_out[l], vwin[l]).then_inc(win_copied, 16)
            pool.wait_ge(win_copied, 2 * DEPTH * 16)
            pool.wait_ge(kv_stored, DEPTH * 16)
            pool.wait_ge(state_stored, DEPTH * 16)

        @block.tensor
        def _(pe):
            pe.sem_inc(slots_done, RING)
            with pe.Fori(0, DEPTH) as l:
                def weight(i):
                    s = i % RING
                    pe.wait_ge(landed[s], (l * SLOTS_IN[s] + i // RING + 1) * 16)
                    return ring[:, s]

                def split_weight_at(i):
                    d = SPLIT_NO[i]
                    pe.wait_ge(w_lo_ready, l * SPLITS + d + 1)
                    return w_hi[:, d % HI_RING], w_lo[:, i % RING]

                def out_bank(step, i, j=0):
                    b, k = FILL[step, i, j]
                    if k > 1:
                        pe.wait_ge(emptied[b], l * FILLS[b] + k - 1)
                    return bank[b]

                def done(ins, step, i, j=0):
                    b, _ = FILL[step, i, j]
                    ins.then_inc(filled[b], 1)

                def product(out, w, rhs, k0=0, kn=KT8, ready=None):
                    w_high, w_rest = w
                    for k in range(kn):
                        if ready:
                            ready(k)
                        high, rest = rhs(k)
                        pe.matmul(out, w_high[:, k0 + k, :], high, start=(k == 0), stop=False)
                        pe.matmul(out, w_rest[:, k0 + k, :], high, start=False, stop=False)
                        ins = pe.matmul(out, w_high[:, k0 + k, :], rest, start=False, stop=(k == kn - 1))
                    return ins

                def x_tile(k):
                    return x_hi[:, k, :], x_lo[:, k, :]

                for step, i in ORDER:
                    if step == "dense":
                        if i > 1:
                            w = split_weight_at(SLOT_OF[step, i])
                            product(out_bank(step, i)[:, 0:T], w, x_tile).then_inc(slots_done, 1)
                        elif i == 0:
                            outs, ws = [], []
                            for n in range(2):
                                ws.append(split_weight_at(n))
                                outs.append(out_bank(step, n)[:, 0:T])
                                for k in range(KT8):
                                    if n == 0 and k % 2 == 0:
                                        pe.wait_ge(x_hi_ready, l * (KT8 // 2) + k // 2 + 1)
                                    for part in ws[n]:
                                        pe.matmul(outs[n], part[:, k, :], x_hi[:, k, :],
                                                  start=(k == 0 and part is ws[n][0]), stop=False)
                            for n in range(2):
                                for k in range(KT8):
                                    if n == 0 and k % 2 == 0:
                                        pe.wait_ge(x_ready, l * (KT8 // 2) + k // 2 + 1)
                                    ins = pe.matmul(outs[n], ws[n][0][:, k, :], x_lo[:, k, :], start=False,
                                                    stop=(k == KT8 - 1))
                                ins.then_inc(slots_done, 1)
                    elif step == "rope":
                        wait_emptied(pe, l, "dense", i)
                        out = out_bank(step, i)
                        done(pe.matmul(out[:, 0:T], perm, h[:, i, :], start=True, stop=True), step, i)
                    elif step == "v_rows":
                        if i == 0:
                            for n in (VW, VW + 1):
                                wait_emptied(pe, l, "dense", n)
                        out = out_bank(step, i)
                        for n in range(4):
                            ins = pe.transpose(out[:, n * P:n * P + P], h[:, VS + n, i * P:i * P + P], ident)
                        done(ins, step, i)
                    elif step == "v_new":
                        out = out_bank(step, i)
                        pe.wait_ge(v_new_ready, l + 1)
                        for gp in range(GP):
                            ins = pe.transpose(out[0:2 * NB, gp * P:gp * P + P],
                                               v_new_c[:, gp, :, :].rearrange("p a b -> p (a b)"), ident)
                        done(ins, step, i)
                    elif step == "gates":
                        wait_emptied(pe, l, "dense", NG)
                        out = out_bank(step, i)
                        for qi in range(2):
                            pe.transpose(out[:, qi * P:qi * P + P], h[:, NG, (1 - qi) * P:(2 - qi) * P], ident)
                        pe.wait_ge(gate_d_ready, l + 1)
                        ins = pe.matmul(out[:, 2 * P:2 * P + 3], gate_d[0:48, :, :].rearrange("p a b -> p (a b)"),
                                        c("gate_type")[0:48, :], start=True, stop=True)
                        done(ins, step, i)
                    elif step in ("cmp_k", "cmp_v"):
                        which = int(step == "cmp_v")
                        out = out_bank(step, i)
                        pe.wait_ge(cmp_v_landed if which else cmp_k_landed, (l + 1) * 16 * 2 * NB)
                        pe.wait_ge(cmp_in_ready, 2 * l + 1 + which)
                        for tap in range(TAPS):
                            if tap % KT8 == 0:
                                w = weight(SLOT_OF[step, i] + tap // KT8)
                            rows = cmp_view[which][:, 0:19, tap:tap + CT * (NC - 1) + 1:CT]
                            ins = pe.matmul(bank[PT1 if which else PT0][:, 0:19 * NC].rearrange(
                                "p (s c) -> p s c", c=NC), w[:, tap % KT8, :], rows,
                                start=(tap == 0), stop=(tap == TAPS - 1))
                            if tap % KT8 == KT8 - 1:
                                ins.then_inc(slots_done, 1)
                    elif step == "cmp_rope":
                        out = out_bank(step, i)
                        wait_emptied(pe, l, "cmp_k", 0)
                        done(pe.matmul(out[:, 0:288], perm, kc_all[:, :, :, :].rearrange("p g s c -> p (g s c)"),
                                       start=True, stop=True), step, i)
                    elif step == "cmp_vrows":
                        out = out_bank(step, i)
                        pe.wait_ge(cmp_out_ready, l + 1)
                        for gp in range(GP):
                            pe.transpose(out[:, gp * P:gp * P + P],
                                         vc_rep[:, gp, :, :].rearrange("p a b -> p (a b)"), ident)
                            ins = pe.transpose(out[:, (2 + gp) * P:(3 + gp) * P],
                                               vc_all[:, gp, 0:NB, :].rearrange("p a b -> p (a b)"), ident)
                        done(ins, step, i)
                    elif step == "cmp_scores":
                        out = out_bank(step, i)
                        pe.wait_ge(kc_ready, l + 1)
                        pe.wait_ge(roped, (l + 1) * len(ROPED))
                        for qi in range(2):
                            for n in range(8):
                                col = qi * 256 + n * 32
                                ins = pe.matmul(out[:, col:col + 32], h[:, Q + n, (1 - qi) * P:(2 - qi) * P],
                                                kc_bd[:, n // R, :, :].rearrange("p a b -> p (a b)"),
                                                start=True, stop=True)
                        done(ins, step, i)
                    elif step == "cmp_turn":
                        out = out_bank(step, i)
                        pe.wait_ge(cmp_probs, l + 1)
                        for gp in range(GP):
                            for qi in range(2):
                                src = cs[:, qi * 16 + gp * 8:qi * 16 + gp * 8 + 8, :].rearrange("p a b -> p (a b)")
                                col = gp * SEQ + (1 - qi) * P
                                ins = pe.transpose(out[:, col:col + P], src, ident)
                        done(ins, step, i)
                    elif step == "scores":
                        tile, g2 = Q + i // 2, i % 2
                        gp = i // 8
                        rows = slice(g2 * HD, g2 * HD + HD)
                        for j, (q0, n) in enumerate(((P, 2 * P), (0, P))):
                            out = out_bank(step, i, j)
                            for br, kt in enumerate((KS, KW)):
                                reg = out[:, br * n:br * n + n]
                                pe.matmul(reg, h[rows, tile, q0:q0 + P], h[rows, kt + gp, 0:n], start=True, stop=False)
                                ins = pe.matmul(reg[:, n - P:n], ident_b[:, :], causal_b[:, :], start=False, stop=True)
                            done(ins, step, i, j)
                    elif step == "turn":
                        pe.wait_ge(probs_ready, l * HEADS + i + 1)
                        for br in range(2):
                            out = out_bank(step, i, br)
                            late, early = br * 256, 512 + br * P
                            pe.transpose(out[:, 0:P], probs[:, i % 2, early:early + P], ident)
                            pe.transpose(out[:, P:2 * P], probs[:, i % 2, late:late + P], ident)
                            ins = pe.transpose(out[:, 2 * P:3 * P], probs[:, i % 2, late + P:late + 2 * P], ident)
                            done(ins, step, i, br)
                    elif step == "pv":
                        gp, r, g2 = i // 8, i // 2 % R, i % 2
                        if g2 == 0:
                            if i == 0:
                                wait_emptied(pe, l, "v_rows", 0)
                                wait_emptied(pe, l, "v_rows", 1)
                                wait_emptied(pe, l, "cmp_turn", 0)
                                wait_emptied(pe, l, "cmp_vrows", 0)
                            out = out_bank(step, i + 1)
                            pe.matmul(out[:, 0:SEQ], vc_bd[:, gp, r, :], pc_t[:, gp, :], start=True, stop=False,
                                      skip_group_check=True)
                        out = bank[OT][g2 * HD:g2 * HD + HD, :]
                        gcol = (2 * gp + g2) * HD
                        for br in range(2):
                            wait_emptied(pe, l, "turn", i, br)
                            pt = probs_t[:, i % 2, br, :]
                            pe.matmul(out[:, 0:SEQ], v_rows[:, 0, br * 256 + gcol:br * 256 + gcol + HD],
                                      pt[:, 0:SEQ], start=False, stop=False, skip_group_check=True)
                            ins = pe.matmul(out[:, P:SEQ], v_rows[:, 1, br * 256 + gcol:br * 256 + gcol + HD],
                                            pt[:, SEQ:SEQ + P], start=False, stop=(br == 1), skip_group_check=True)
                        if g2:
                            done(ins, step, i)
                        else:
                            ins.then_inc(pv_even, 1)
                    elif step == "one_cmp_scores":
                        out = out_bank(step, i)
                        pe.wait_ge(q_pad_ready, l + 1)
                        for n in range(GP * NB):
                            gp, b = n % GP, n // GP
                            ins = pe.matmul(out[:, 0:CT], q_pad[:, gp, b, :], kc_all[:, gp, b, :],
                                            start=(n == 0), stop=(n == GP * NB - 1))
                        done(ins, step, i)
                    elif step == "one_scores":
                        out = out_bank(step, i)
                        pe.wait_ge(win_k_landed if i else sel_k_landed, (l + 1) * (16 if i else 16 * 2 * NB))
                        pe.wait_ge(k_new_ready, 2 * l + i + 1)
                        for n in range(GP * NB):
                            gp, b = n % GP, n // GP
                            ins = pe.matmul(out[:, 0:KEYS], q_pad[:, gp, b, :], k_one[:, b, gp, :],
                                            start=(n == 0), stop=(n == GP * NB - 1))
                        done(ins, step, i)
                    elif step == "one_turn":
                        out = out_bank(step, i)
                        pe.wait_ge(one_probs, 2 * l + i + 1)
                        for half in range(2):
                            ins = pe.transpose(out[:, half * P:half * P + P],
                                               p_one[:, i, half * P:half * P + P], ident)
                        done(ins, step, i)
                    elif step == "one_cmp_turn":
                        out = out_bank(step, i)
                        pe.transpose(out[:, 0:P], p_cmp_x[:, :, :].rearrange("p b c -> p (b c)"), ident)
                        ins = pe.transpose(out[0:2 * NB, P:2 * P], p_tail[:, :, :].rearrange("p a b -> p (a b)"),
                                           ident)
                        done(ins, step, i)
                    elif step == "one_pv":
                        if i == 0:
                            out = out_bank("one_pv", 1)
                        wait_emptied(pe, l, "one_turn", i)
                        pe.wait_ge(win_v_landed if i else sel_v_landed, (l + 1) * (16 if i else 16 * 2 * NB))
                        out = bank[OT][:, 0:P].rearrange("p (g n b) -> p g n b", g=GP, b=NB)
                        pt = p_one_t[:, i, :].rearrange("p (t g n b) -> p t g n b", t=2, g=GP, b=NB)
                        for b in range(NB):
                            for gp in range(GP):
                                for half in range(2):
                                    ins = pe.matmul(out[:, gp, :, b], v_one[:, b, half, gp * P:gp * P + P],
                                                    pt[:, half, gp, :, b],
                                                    start=(i == 0 and b == 0 and gp == 0 and half == 0),
                                                    stop=False, skip_group_check=True)
                        if i == 0:
                            ins.then_inc(sel_v_used, 1)
                        else:
                            wait_emptied(pe, l, "one_cmp_turn", 0)
                            wait_emptied(pe, l, "v_new", 0)
                            for gp in range(GP):
                                cols = slice(gp * HD, gp * HD + HD)
                                pe.matmul(bank[OT][:, cols], vc_one[:, gp, :], p_cmp_t[:, cols],
                                          start=False, stop=False, skip_group_check=True)
                                ins = pe.matmul(bank[OT][:, cols], v_new[:, gp * P:gp * P + P], p_tail_t[:, cols],
                                                start=False, stop=(gp == 1), skip_group_check=True)
                            done(ins, step, i)
                    elif step == "mix":
                        out = out_bank(step, i)
                        if i == 0:
                            pe.wait_ge(pooled, 4 * (l + 1))
                        done(pe.matmul(out[:, 0:T], pr("pool_w", i * P, P), h[:, PU + i, :], start=True, stop=True),
                             step, i)
                    elif step == "gate":
                        w = split_weight_at(SLOT_OF[step, i])
                        product(out_bank(step, i)[:, 0:T], w, x_tile).then_inc(slots_done, 1)
                    elif step == "merge":
                        w = split_weight_at(SLOT_OF[step, i])
                        if i == 0:
                            pe.wait_ge(y_split, len(Y_PARTS) * l + 2)
                        out = out_bank(step, i, 0)
                        product(out[:, 0:T], w, lambda k: (h_r[:, Y_A_HI + k, :], h_r[:, PU + k, :]), 0, 4)
                        out = out_bank(step, i, 1)
                        product(out[:, 0:T], w, lambda k: (h_r[:, Y_B_HI + k, :], h_r[:, CB + k, :]), 4, 4
                                ).then_inc(slots_done, 1)
                        w = split_weight_at(SLOT_OF[step, i] + 1)
                        if i == 0:
                            pe.wait_ge(y_split, len(Y_PARTS) * (l + 1))
                        out = out_bank(step, i, 2)
                        product(out[:, 0:T], w, lambda k: (h_r[:, Y_C_HI + k, :], h_r[:, Q + k, :])
                                ).then_inc(slots_done, 1)
                    elif step == "out":
                        def merge_tile(k):
                            return h_r[:, M_HI + k, :], m_lo[:, k, :]

                        if i > 1:
                            w = split_weight_at(SLOT_OF[step, i])
                            product(out_bank(step, i)[:, 0:T], w, merge_tile).then_inc(slots_done, 1)
                        elif i == 0:
                            outs = [out_bank(step, n)[:, 0:T] for n in range(2)]
                            ws = [split_weight_at(SLOT_OF[step, n]) for n in range(2)]
                            for ks in (range(0, KT8 - 1), range(KT8 - 1, KT8)):
                                for n in range(2):
                                    for k in ks:
                                        if n == 0:
                                            pe.wait_ge(m_split, l * KT8 + k + 1)
                                        high, rest = merge_tile(k)
                                        w_high, w_rest = ws[n]
                                        pe.matmul(outs[n], w_high[:, k, :], high, start=(k == 0), stop=False)
                                        pe.matmul(outs[n], w_rest[:, k, :], high, start=False, stop=False)
                                        ins = pe.matmul(outs[n], w_high[:, k, :], rest, start=False,
                                                        stop=(k == KT8 - 1))
                                    if k == KT8 - 1:
                                        ins.then_inc(slots_done, 1)
                    elif step == "mean":
                        wait_emptied(pe, l, "out", i)
                        ins = pe.matmul(bank[SA][:, 0:T], ones[:, :], z[:, i, :], start=(i == 0), stop=(i == KT8 - 1))
                        if i == KT8 - 1:
                            ins.then_inc(mean_ready, 1)
                    elif step == "norm":
                        for k in range(KT8):
                            if k % 2 == 0:
                                pe.wait_ge(squared, l * 4 + k // 2 + 1)
                            ins = pe.matmul(bank[SB][:, 0:T], ones[:, :], m[:, k, :], start=(k == 0),
                                            stop=(k == KT8 - 1))
                        ins.then_inc(squared_sum, 1)

        @block.scalar
        def _(act):
            def round_weight(slot, d):
                act.activation(w_hi[:, d % HI_RING], ring[:, slot % RING], ACT.Copy).then_inc(w_hi_ready, 1)

            act.wait_ge(x_loaded, 16)
            for k in range(KT8 // 2):
                act.activation(x_hi[:, 2 * k:2 * k + 2, :], m[:, 2 * k:2 * k + 2, :], ACT.Copy
                               ).then_inc(x_hi_ready, 1)
                if k < 2:
                    act.wait_ge(landed[k], 16)
                    round_weight(k, k)
            act.wait_ge(tables_ready, 1)
            with act.Fori(0, DEPTH) as l:
                def emptied_by(ins, step, i, j=0):
                    ins.then_inc(emptied[FILL[step, i, j][0]], 1)

                def round_next(step, i, which=None):
                    for n, d in enumerate(SPLIT_AT.get((step, i), [])):
                        if which is not None and n != which:
                            continue
                        following, d, slot, s, _ = split_weight(d)
                        act.wait_ge(landed[s], ((l + following) * SLOTS_IN[s] + slot // RING + 1) * 16)
                        if d >= HI_RING:
                            act.wait_ge(slots_done, (l + following) * SLOTS + RING + SPLIT_SLOTS[d - HI_RING] + 1)
                        else:
                            last = max(e for e in range(SPLITS) if e % HI_RING == d)
                            act.wait_ge(slots_done, (l + following - 1) * SLOTS + RING + SPLIT_SLOTS[last] + 1)
                        round_weight(slot, d)

                for step, i in ORDER:
                    if step != "norm":
                        round_next(step, i)
                    if step == "dense":
                        wait_slot(act, l, step, i)
                        if i == LATE:
                            act.wait_ge(pooled, 4 * (l + 1))
                        if i == LATE_PV:
                            wait_filled(act, l, "pv", HEADS - 1)
                        src = bank[FILL[step, i, 0][0]][:, 0:T]
                        if i >= AZ:
                            act.activation(h[:, i, :], src, ACT.Sigmoid).then_inc(sigmoids, 1)
                        else:
                            emptied_by(act.activation(h[:, i, :], src, ACT.Sigmoid if i == NG else ACT.Copy),
                                       step, i)
                    elif step == "v_rows":
                        wait_filled(act, l, step, i)
                        src = bank[FILL[step, i, 0][0]]
                        emptied_by(act.activation(v_rows[:, i, :], src[:, :], ACT.Copy), step, i)
                    elif step == "cmp_scores":
                        act.wait_ge(cmp_shifted, l + 1)
                        act.activation(cs[:, :, :], cs[:, :, :], ACT.Exp, scale=QK).then_inc(cmp_exped, 1)
                    elif step == "cmp_turn":
                        wait_filled(act, l, step, i)
                        emptied_by(act.activation(pc_t[:, :, :].rearrange("p g t -> p (g t)"), bank[PT0][:, :],
                                                  ACT.Copy), step, i)
                    elif step == "scores":
                        act.wait_ge(max_ready, l * HEADS + i + 1)
                        if i >= 2:
                            wait_filled(act, l, "turn", i - 2, 1)
                        at = 0
                        for j, n in enumerate((2 * P, P)):
                            src = bank[(SA, SB)[j]]
                            for br in range(2):
                                ins = act.activation(probs[:, i % 2, at:at + n], src[:, br * n:br * n + n], ACT.Exp,
                                                     bias=u_max[:, i % 2, 2 * j + br:2 * j + br + 1], scale=QK,
                                                     accum_out=u_sum[:, i % 2, 2 * j + br:2 * j + br + 1])
                                at += n
                            emptied_by(ins, step, i, j)
                    elif step == "turn":
                        wait_filled(act, l, step, i, 0)
                        if i >= 2:
                            if i % 2:
                                wait_filled(act, l, "pv", i - 2)
                            else:
                                act.wait_ge(pv_even, l * 8 + i // 2)
                        emptied_by(act.activation(probs_t[:, i % 2, 0, :], bank[PT0][:, 0:384], ACT.Copy), step, i, 0)
                    elif step == "pv" and i % 2:
                        wait_filled(act, l, step, i)
                        emptied_by(act.activation(h[:, Q + i // 2, 0:SEQ], bank[OT][:, 0:SEQ], ACT.Copy), step, i)
                    elif step == "one_cmp_scores":
                        act.wait_ge(one_max_ready, 3 * l + 1)
                        act.activation(p_cmp[:, 0:NC], bank[SB][:, 0:NC], ACT.Exp, bias=one_max[:, 2:3], scale=QK,
                                       accum_out=one_sum[:, 2:3]).then_inc(emptied[SB], 1)
                    elif step == "one_scores":
                        act.wait_ge(one_max_ready, 3 * l + 2 + i)
                        emptied_by(act.activation(p_one[:, i, :], bank[(SA, PT0)[i]][:, 0:KEYS], ACT.Exp,
                                                  bias=one_max[:, i:i + 1], scale=QK,
                                                  accum_out=one_sum[:, i:i + 1]), step, i)
                    elif step == "one_turn":
                        wait_filled(act, l, step, i)
                        emptied_by(act.activation(p_one_t[:, i, :], bank[(PT1, SB)[i]][:, 0:2 * P], ACT.Copy), step, i)
                    elif step == "silu":
                        wait_filled(act, l, "one_scores", 1)
                        for n in (2, 3):
                            wait_emptied(act, l, "dense", PZ + 4 * i + n)
                        act.activation(z[:, 4 * i:4 * i + 4, :], h[:, PZ + 4 * i:PZ + 4 * i + 4, :], ACT.Sigmoid
                                       ).then_inc(sigmoids, 1)
                    elif step == "y_high":
                        src, dst, tiles = Y_PARTS[i]
                        act.wait_ge(y_ready, len(Y_PARTS) * l + i + 1)
                        if i == 1:
                            act.wait_ge(kv_stored, (l + 1) * 16)
                        act.activation(h_r[:, dst:dst + tiles, :], h[:, src:src + tiles, :], ACT.Copy
                                       ).then_inc(y_hi_ready, 1)
                    elif step == "gate":
                        tile, j = divmod(i, 3)
                        if tile >= GATE_RING:
                            act.wait_ge(merged, l * KT8 + tile - GATE_RING + 1)
                        wait_slot(act, l, step, i)
                        emptied_by(act.activation(g[:, tile % GATE_RING, j, :], bank[FILL[step, i, 0][0]][:, 0:T],
                                                  ACT.Sigmoid), step, i)
                    elif step == "merge":
                        act.wait_ge(merged, l * KT8 + i + 1)
                        act.activation(h_r[:, M_HI + i, :], m[:, i, :], ACT.Copy).then_inc(m_hi_ready, 1)
                    elif step == "norm":
                        for k in range(4):
                            act.wait_ge(centered, l * 4 + k + 1)
                            act.activation(m[:, 2 * k:2 * k + 2, :], z[:, 2 * k:2 * k + 2, :], ACT.Square
                                           ).then_inc(squared, 1)
                        round_next(step, i)
                        act.wait_ge(squared_sum, l + 1)
                        act.activation(rstd[:, :], bank[SB][:, 0:T], ACT.Sqrt, bias=eps[:, :]).then_inc(std_ready, 1)
                        for n in range(KT8):
                            if n % 2 == 0:
                                act.wait_ge(scaled, l * 4 + n // 2 + 1)
                            ins = act.activation(x_hi[:, n, :], z[:, n, :], ACT.Identity, bias=pr("ln_b", n, 1))
                            if n % 2:
                                ins.then_inc(x_hi_ready, 1)

        @block.vector
        def _(dve):
            def rest_of_weight(slot, d):
                dve.tensor_tensor(w_lo[:, slot % RING], ring[:, slot % RING], w_hi[:, d % HI_RING].bitcast(F32),
                                  ALU.subtract).then_inc(w_lo_ready, 1)

            def rest_of_input(k):
                dve.tensor_tensor(x_lo[:, 2 * k:2 * k + 2, :], m[:, 2 * k:2 * k + 2, :],
                                  x_hi[:, 2 * k:2 * k + 2, :].bitcast(F32), ALU.subtract).then_inc(x_ready, 1)

            for k in range(KT8 // 2):
                dve.wait_ge(x_hi_ready, k + 1)
                rest_of_input(k)
                if k < 2:
                    dve.wait_ge(w_hi_ready, k + 1)
                    rest_of_weight(k, k)
            dve.wait_ge(consts_loaded, 16)
            dve.memset(ones[:, :], 1.0 / D_MODEL)
            dve.memset(eps[:, :], EPS)
            for which in range(2):
                dve.memset(cmp_view[which][:, 18, :], 0.0)
            for t in (kc_all, vc_all, kc_bd, p_cmp):
                dims = " ".join("abcd"[:len(t.shape) - 1])
                dve.memset(t[tuple(slice(None) for _ in t.shape)].rearrange(f"p {dims} -> p ({dims})")
                           if len(t.shape) > 2 else t[:, :], 0.0)
            dve.tensor_copy(causal_b[:, :], c("causal"))
            dve.tensor_copy(ident_b[:, :], ident).then_inc(tables_ready, 1)
            dve.wait_ge(tables_ready, 1)
            with dve.Fori(0, DEPTH) as l:
                steps = [0]

                def link(ins):
                    steps[0] += 1
                    ins.then_inc(vector_step, 1)
                    dve.wait_ge(vector_step, l * VECTOR_STEPS + steps[0])

                def emptied_by(ins, step, i, j=0):
                    ins.then_inc(emptied[FILL[step, i, j][0]], 1)
                    wait_emptied(dve, l, step, i, j)

                def rotate(src, psum, cos, sin, scratch):
                    dve.tensor_tensor(scratch, psum, sin, ALU.mult)
                    return dve.tensor_tensor(src, src, cos, ALU.mult)

                def rest_next(step, i, which=None):
                    for n, d in enumerate(SPLIT_AT.get((step, i), [])):
                        if which is not None and n != which:
                            continue
                        following, d, slot, _, _ = split_weight(d)
                        dve.wait_ge(w_hi_ready, (l + following) * SPLITS + d + 1)
                        rest_of_weight(slot, d)

                for step, i in ORDER:
                    if step not in ("scores", "merge", "norm"):
                        rest_next(step, i)
                    if step == "dense" and i >= AZ:
                        dve.wait_ge(sigmoids, l * SIGMOIDS + SIGMOIDS_BEFORE[step, i])
                        emptied_by(dve.tensor_tensor(h[:, i, :], h[:, i, :], bank[FILL[step, i, 0][0]][:, 0:T],
                                                     ALU.mult), step, i)
                    if step == "cmp_k":
                        dve.wait_ge(x_hi_ready, (l + 1) * (KT8 // 2))
                        dve.memset(zf[:, 0:GP * NB * P], 0.0).then_inc(q_pad_clear, 1)
                        dve.wait_ge(q_pad_clear, l + 1)
                        dve.wait_ge(roped, (l + 1) * len(ROPED))
                        for g2 in range(2):
                            rows = slice(g2 * HD, g2 * HD + HD)
                            for gp in range(GP):
                                src = h[rows, Q + gp * R:Q + gp * R + R, SEQ:T]
                                for r in range(R):
                                    col = gp * HD + (r * 2 + g2) * NB
                                    diag = q_pad[rows, gp, :, :].rearrange("p b n -> p (b n)")[
                                        :, col:col + (NB - 1) * (P + 1) + 1:P + 1]
                                    ins = dve.tensor_copy(diag, src[:, r, :])
                        ins.then_inc(q_pad_ready, 1)
                        dve.wait_ge(q_pad_ready, l + 1)
                        wait_emptied(dve, l, "dense", NG)
                        dve.tensor_tensor(gate_d[0:48, :, :],
                                          h[0:48, NG, SEQ:T].unsqueeze(1).to_broadcast([48, HEADS, NB]),
                                          c("gate_head")[0:48, :].unsqueeze(2).to_broadcast([48, HEADS, NB]),
                                          ALU.mult).then_inc(gate_d_ready, 1)
                        dve.wait_ge(gate_d_ready, l + 1)
                    if step == "rope":
                        wait_filled(dve, l, step, i)
                        emptied_by(dve.tensor_tensor(tmp[:, 0, 0:T], bank[MI][:, 0:T], c("rope_s"), ALU.mult), step, i)
                        link(dve.tensor_tensor(h[:, i, :], h[:, i, :], c("rope_c"), ALU.mult))
                        wait_emptied(dve, l, step, i)
                        dve.tensor_tensor(h[:, i, :], h[:, i, :], tmp[:, 0, 0:T], ALU.add).then_inc(roped, 1)
                        dve.wait_ge(roped, l * len(ROPED) + ROPED.index(i) + 1)
                    elif step == "v_new_in":
                        for n in (VW, VW + 1):
                            wait_emptied(dve, l, "dense", n)
                        dve.tensor_copy(v_new_c[:, :, :, :], h[:, VS:VS + 4, SEQ:T].rearrange(
                            "p (a g) b -> p g a b", a=2)).then_inc(v_new_ready, 1)
                        dve.wait_ge(v_new_ready, l + 1)
                    elif step == "v_new":
                        wait_filled(dve, l, step, i)
                        emptied_by(dve.tensor_copy(v_new[:, :], bank[MI][0:2 * NB, 0:2 * P]), step, i)
                        dve.wait_ge(params_loaded, (l + 1) * 16)
                        for which, name in enumerate(("pe_k", "pe_v")):
                            src = (KC, VC)[which]
                            for gp in range(GP):
                                dve.tensor_copy(cmp_view[which][:, 16 + gp, :], h[:, src + gp, 0:SEQ])
                            dve.tensor_copy(cmp_view[which][:, 18, 0:TAPS], pr(name)).then_inc(cmp_in_ready, 1)
                            dve.wait_ge(cmp_in_ready, 2 * l + 1 + which)
                    elif step == "gates":
                        wait_filled(dve, l, step, i)
                        link(dve.tensor_copy(gate[:, 0:96].rearrange("p (q n) -> p q n", q=2),
                                             bank[MI][:, 0:2 * P].rearrange("p (q n) -> p q n", q=2)[:, :, 0:48]))
                        emptied_by(dve.tensor_copy(gate[:, 96:99], bank[MI][:, 2 * P:2 * P + 3]), step, i)
                    elif step in ("cmp_k", "cmp_v"):
                        which = int(step == "cmp_v")
                        b = PT1 if which else PT0
                        wait_slot(dve, l, step, 0)
                        link(dve.tensor_copy(bias[:, which:which + 1], bank[b][:, 18 * NC:18 * NC + 1]))
                        out = (vc_all if which else kc_all)[:, :, :, 0:NC].rearrange("p g s c -> p s g c")
                        src = bank[b][:, 0:18 * NC].rearrange("p (s g c) -> p s g c", g=GP, c=NC)
                        for gp in range(GP):
                            ins = dve.tensor_scalar(out[:, :, gp, :], src[:, :, gp, :], bias[:, which:which + 1], None,
                                                    ALU.add)
                            if gp == 0:
                                link(ins)
                        emptied_by(ins, step, i)
                        wait_emptied(dve, l, step, 0)
                        if which:
                            dve.tensor_copy(vc_rep[:, :, :, :], vc_all[:, :, NB, :].unsqueeze(2).to_broadcast(
                                [P, GP, 8, CT])).then_inc(cmp_out_ready, 1)
                            dve.wait_ge(cmp_out_ready, l + 1)
                    elif step == "cmp_rope":
                        wait_filled(dve, l, step, i)
                        flat = kc_all[:, :, :, :].rearrange("p g s c -> p (g s) c")
                        rot = tmp[:, 0, :].rearrange("p (n c) -> p n c", c=CT)
                        emptied_by(dve.tensor_tensor(rot, bank[MI][:, 0:288].rearrange("p (n c) -> p n c", c=CT),
                                                     c("cmp_s").unsqueeze(1).to_broadcast([P, 18, CT]), ALU.mult),
                                   step, i)
                        link(dve.tensor_tensor(flat, flat, c("cmp_c").unsqueeze(1).to_broadcast([P, 18, CT]),
                                               ALU.mult))
                        wait_emptied(dve, l, step, i)
                        link(dve.tensor_tensor(flat, flat, rot, ALU.add))
                        for g2 in range(2):
                            rows = slice(g2 * HD, g2 * HD + HD)
                            ins = dve.tensor_copy(kc_bd[rows, :, g2, :], kc_all[rows, :, NB, :])
                        ins.then_inc(kc_ready, 1)
                        dve.wait_ge(kc_ready, l + 1)
                    elif step == "cmp_vrows":
                        wait_filled(dve, l, step, i)
                        for gp in range(GP):
                            dve.tensor_tensor(vc_bd[:, gp, :, :],
                                              bank[MI][:, gp * P:gp * P + P].unsqueeze(1).to_broadcast([P, R, P]),
                                              c("own_head").rearrange("p (r n) -> p r n", r=R), ALU.mult)
                        emptied_by(dve.tensor_copy(vc_one[:, :, :].rearrange("p g n -> p (g n)"),
                                                   bank[MI][:, 2 * P:4 * P]), step, i)
                    elif step == "cmp_scores":
                        wait_filled(dve, l, step, i)
                        mask = c("cmp_mask").rearrange("p (q c) -> p q c", q=2)
                        for qi in range(2):
                            ins = dve.tensor_tensor(cs[:, qi * 16:qi * 16 + 16, :], bank[SA][:, qi * 256:qi * 256 + 256]
                                                    .rearrange("p (n c) -> p n c", c=CT),
                                                    mask[:, qi, :].unsqueeze(1).to_broadcast([P, 16, CT]), ALU.add)
                            if qi == 0:
                                link(ins)
                        emptied_by(ins, step, i)
                        wait_emptied(dve, l, step, i)
                        link(dve.tensor_reduce(c_max[:, :], cs[:, :, :], AX_X, ALU.max))
                        link(dve.tensor_scalar(c_max[:, :], c_max[:, :], FLOOR, None, ALU.max))
                        dve.tensor_tensor(cs[:, :, :], cs[:, :, :], c_max[:, :].unsqueeze(2).to_broadcast([P, 32, CT]),
                                          ALU.subtract).then_inc(cmp_shifted, 1)
                        dve.wait_ge(cmp_shifted, l + 1)
                        dve.wait_ge(cmp_exped, l + 1)
                        link(dve.tensor_reduce(c_sum[:, :], cs[:, :, :], AX_X, ALU.add))
                        link(dve.tensor_scalar(c_sum[:, :], c_sum[:, :], 1e-30, None, ALU.max))
                        link(dve.reciprocal(c_sum[:, :], c_sum[:, :]))
                        wait_emptied(dve, l, "gates", 0)
                        link(dve.tensor_tensor(c_sum[:, :].rearrange("p (q n) -> p q n", q=2),
                                               c_sum[:, :].rearrange("p (q n) -> p q n", q=2),
                                               gate[:, 0:96].rearrange("p (q n) -> p q n", q=2)[:, :, 0:16], ALU.mult))
                        dve.tensor_tensor(cs[:, :, :], cs[:, :, :], c_sum[:, :].unsqueeze(2).to_broadcast([P, 32, CT]),
                                          ALU.mult).then_inc(cmp_probs, 1)
                        dve.wait_ge(cmp_probs, l + 1)
                    elif step == "scores":
                        for j, n in enumerate((2 * P, P)):
                            wait_filled(dve, l, step, i, j)
                            link(dve.tensor_reduce(u_fac[:, i % 2, 2 * j:2 * j + 2],
                                                   bank[(SA, SB)[j]][:, 0:2 * n].rearrange("p (a n) -> p a n", a=2),
                                                   AX_X, ALU.max))
                        dve.tensor_scalar(u_max[:, i % 2, :], u_fac[:, i % 2, :], -QK, None, ALU.mult
                                          ).then_inc(max_ready, 1)
                        dve.wait_ge(max_ready, l * HEADS + i + 1)
                        rest_next(step, i)
                    elif step == "scale":
                        wait_emptied(dve, l, "scores", i, 0)
                        wait_emptied(dve, l, "scores", i, 1)
                        fac = u_fac[:, i % 2, :]
                        link(dve.tensor_scalar(fac, u_sum[:, i % 2, :], 1e-30, None, ALU.max))
                        link(dve.reciprocal(fac, fac))
                        link(dve.tensor_tensor(fac.rearrange("p (q a) -> p q a", q=2),
                                               fac.rearrange("p (q a) -> p q a", q=2),
                                               gate[:, 0:96].rearrange("p (q a n) -> p q a n", q=2, a=3)[:, :, 1:3, i],
                                               ALU.mult))
                        at = 0
                        for j, n in enumerate((256, 256, 128, 128)):
                            ins = dve.tensor_scalar(probs[:, i % 2, at:at + n], probs[:, i % 2, at:at + n],
                                                    u_fac[:, i % 2, j:j + 1], None, ALU.mult)
                            at += n
                        ins.then_inc(probs_ready, 1)
                        dve.wait_ge(probs_ready, l * HEADS + i + 1)
                    elif step == "turn":
                        wait_filled(dve, l, step, i, 1)
                        if i >= 2:
                            if i % 2:
                                wait_filled(dve, l, "pv", i - 2)
                            else:
                                dve.wait_ge(pv_even, l * 8 + i // 2)
                        emptied_by(dve.tensor_copy(probs_t[:, i % 2, 1, :], bank[PT1][:, 0:384]), step, i, 1)
                    elif step == "pool" and i == 0:
                        for n in (PU + 2, PU + 3):
                            wait_emptied(dve, l, "dense", n)
                        dve.memset(pu_ext[:, :, 0:HIST], 0.0)
                        dve.tensor_copy(pu_ext[:, :, HIST:NE], h[:, PU:PU + 4, 0:SEQ])
                        dve.tensor_copy(pu_one[:, :, :, 0:HIST], pr("pool_hist").rearrange(
                            "p (g b t) -> p g b t", g=4, b=NB))
                        dve.tensor_copy(pu_one[:, :, :, HIST], h[:, PU:PU + 4, SEQ:T]).then_inc(state_ready, 1)
                        dve.wait_ge(state_ready, 2 * l + 1)
                    elif step == "pool" and i <= 3:
                        for k in ((0,), (1,), (2, 3))[i - 1]:
                            src, to = (sum_a, sum_b)[(k - 1) % 2] if k else pu_ext, (sum_a, sum_b)[k % 2]
                            shift = 2 ** k
                            first = 2 * shift - 1
                            link(dve.tensor_tensor(to[:, k:4, first:NE], src[:, k:4, first:NE],
                                                   src[:, k:4, first - shift:NE - shift], ALU.add))
                    elif step == "pool":
                        k = i - 4
                        w = WINDOWS[k]
                        sums = (sum_a, sum_b)[k % 2]
                        link(dve.scalar_tensor_tensor(out=h[:, PU + k, 0:SEQ], in0=sums[:, k, HIST:NE],
                                                      scalar=1.0 / w, in1=pu_ext[:, k, HIST:NE], op0=ALU.mult,
                                                      op1=ALU.subtract))
                        dve.tensor_tensor(tmp[:, 0, k * CT:k * CT + CT], sums[:, k, HIST:HIST + CT],
                                          c("inv_count")[:, k * CT:k * CT + CT], ALU.mult)
                        link(dve.tensor_reduce(pu_sum[:, k, :], pu_one[:, k, :, HIST + 1 - w:HIST + 1], AX_X,
                                               ALU.add))
                        dve.tensor_tensor(h[:, PU + k, 0:CT], tmp[:, 0, k * CT:k * CT + CT],
                                          pu_ext[:, k, HIST:HIST + CT], ALU.subtract)
                        dve.scalar_tensor_tensor(out=h[:, PU + k, SEQ:T], in0=pu_sum[:, k, :], scalar=1.0 / w,
                                                 in1=pu_one[:, k, :, HIST], op0=ALU.mult, op1=ALU.subtract
                                                 ).then_inc(pooled, 1)
                        dve.wait_ge(pooled, 4 * l + k + 1)
                    elif step == "conv" and i == 0:
                        for n in (CX + 2, CX + 3):
                            wait_emptied(dve, l, "dense", n)
                        dve.wait_ge(state_staged, 2 * l + 1)
                        dve.memset(hc_ext[:, :, 0:2], 0.0)
                        dve.tensor_tensor(hc_ext[:, :, 2:2 + SEQ], h[:, CC:CC + 4, 0:SEQ], h[:, CX:CX + 4, 0:SEQ],
                                          ALU.mult)
                        dve.tensor_copy(hc_one[:, :, 0:2, :], pr("conv_hist").rearrange("p (g j b) -> p g j b",
                                                                                       g=4, j=2))
                        dve.tensor_tensor(hc_one[:, :, 2, :], h[:, CC:CC + 4, SEQ:T], h[:, CX:CX + 4, SEQ:T],
                                          ALU.mult).then_inc(state_ready, 1)
                        dve.wait_ge(state_ready, 2 * l + 2)
                    elif step == "conv" and i <= 3:
                        j = i - 1
                        for k in range(4):
                            w = pr("conv_w", k * 3 + j, 1)
                            for dst, src in ((h[:, CC + k, 0:SEQ], hc_ext[:, k, j:j + SEQ]),
                                             (h[:, CC + k, SEQ:T], hc_one[:, k, j, :])):
                                if j == 0:
                                    ins = dve.tensor_scalar(dst, src, w, None, ALU.mult)
                                else:
                                    ins = dve.scalar_tensor_tensor(out=dst, in0=src, scalar=w, in1=dst,
                                                                   op0=ALU.mult, op1=ALU.add)
                        link(ins)
                    elif step == "conv":
                        dve.tensor_tensor(h[:, CB:CB + 4, :], h[:, CB:CB + 4, :], h[:, CC:CC + 4, :], ALU.mult
                                          ).then_inc(convolved, 1)
                        dve.wait_ge(convolved, l + 1)
                    elif step == "one_cmp_scores":
                        wait_filled(dve, l, step, i)
                        link(dve.tensor_reduce(one_max[:, 2:3], bank[SB][:, 0:NC], AX_X, ALU.max))
                        dve.tensor_scalar(one_max[:, 2:3], one_max[:, 2:3], -QK, None, ALU.mult
                                          ).then_inc(one_max_ready, 1)
                        dve.wait_ge(one_max_ready, 3 * l + 1)
                        dve.tensor_copy(k_one[:, :, :, PAST], h[:, KS:KS + 2, SEQ:T].rearrange("p g b -> p b g")
                                        ).then_inc(k_new_ready, 1)
                        dve.wait_ge(k_new_ready, 2 * l + 1)
                        wait_emptied(dve, l, step, i)
                        link(dve.tensor_scalar(one_sum[:, 2:3], one_sum[:, 2:3], 1e-30, None, ALU.max))
                        link(dve.reciprocal(one_sum[:, 2:3], one_sum[:, 2:3]))
                        link(dve.tensor_tensor(one_sum[:, 2:3], one_sum[:, 2:3], gate[:, 96:97], ALU.mult))
                        link(dve.tensor_scalar(p_cmp[:, :], p_cmp[:, :], one_sum[:, 2:3], None, ALU.mult))
                        link(dve.tensor_tensor(p_cmp_x[:, :, :], p_cmp[:, :].unsqueeze(1).to_broadcast([P, NB, CT]),
                                               c("own_row").unsqueeze(2).to_broadcast([P, NB, CT]), ALU.mult))
                    elif step == "one_scores":
                        src = bank[(SA, PT0)[i]]
                        wait_filled(dve, l, step, i)
                        link(dve.tensor_reduce(one_max[:, i:i + 1], src[:, 0:KEYS], AX_X, ALU.max))
                        dve.tensor_scalar(one_max[:, i:i + 1], one_max[:, i:i + 1], -QK, None, ALU.mult
                                          ).then_inc(one_max_ready, 1)
                        dve.wait_ge(one_max_ready, 3 * l + 2 + i)
                        if i == 0:
                            dve.tensor_copy(k_one[:, :, :, PAST], h[:, KW:KW + 2, SEQ:T].rearrange("p g b -> p b g")
                                            ).then_inc(k_new_ready, 1)
                            dve.wait_ge(k_new_ready, 2 * l + 2)
                        wait_emptied(dve, l, step, i)
                        link(dve.tensor_scalar(one_sum[:, i:i + 1], one_sum[:, i:i + 1], 1e-30, None, ALU.max))
                        link(dve.reciprocal(one_sum[:, i:i + 1], one_sum[:, i:i + 1]))
                        link(dve.tensor_tensor(one_sum[:, i:i + 1], one_sum[:, i:i + 1], gate[:, 97 + i:98 + i],
                                               ALU.mult))
                        link(dve.tensor_scalar(p_one[:, i, :], p_one[:, i, :], one_sum[:, i:i + 1], None, ALU.mult))
                        dve.tensor_scalar(p_tail[:, i, :], c("own_row"), p_one[:, i, PAST:KEYS], None, ALU.mult
                                          ).then_inc(one_probs, 1)
                        dve.wait_ge(one_probs, 2 * l + i + 1)
                    elif step == "one_cmp_turn":
                        wait_filled(dve, l, step, i)
                        link(dve.tensor_copy(p_cmp_t[:, :], bank[MI][:, 0:P]))
                        emptied_by(dve.tensor_copy(p_tail_t[:, :], bank[MI][0:2 * NB, P:2 * P]), step, i)
                    elif step == "one_pv" and i == 1:
                        wait_filled(dve, l, step, i)
                        for g2 in range(2):
                            rows = slice(g2 * HD, g2 * HD + HD)
                            src = bank[OT][rows, 0:P].rearrange("p (n a b) -> p n a b", a=2, b=NB)[:, :, g2, :]
                            ins = dve.tensor_copy(h[rows, Q:Q + 8, SEQ:T], src)
                            if g2 == 0:
                                link(ins)
                        emptied_by(ins, step, i)
                    elif step == "silu":
                        dve.wait_ge(sigmoids, l * SIGMOIDS + SIGMOIDS_BEFORE[step, i])
                        tiles = h[:, PZ + 4 * i:PZ + 4 * i + 4, :]
                        link(dve.tensor_tensor(tiles, z[:, 4 * i:4 * i + 4, :], tiles, ALU.mult))
                    elif step == "mix":
                        wait_filled(dve, l, step, i)
                        emptied_by(dve.scalar_tensor_tensor(out=h[:, PU + i, :], in0=bank[FILL[step, i, 0][0]][:, 0:T],
                                                            scalar=pr("pool_scale", i, 1), in1=h[:, PZ + i, :],
                                                            op0=ALU.mult, op1=ALU.mult), step, i)
                        if i == 3:
                            dve.sem_inc(y_ready, 1)
                    elif step == "y":
                        src, _, tiles = Y_PARTS[i]
                        gates = CZ if i == 0 else AZ + 2 * (i - 2)
                        if i == 2:
                            wait_emptied(dve, l, "pv", HEADS - 1)
                        ins = dve.tensor_tensor(h[:, src:src + tiles, :], h[:, src:src + tiles, :],
                                                h[:, gates:gates + tiles, :], ALU.mult)
                        ins.then_inc(y_ready, 1)
                        dve.wait_ge(y_ready, len(Y_PARTS) * l + i + 1)
                    elif step == "y_rest":
                        lo, hi, tiles = Y_PARTS[i]
                        dve.wait_ge(y_hi_ready, len(Y_PARTS) * l + i + 1)
                        dve.tensor_tensor(h_r[:, lo:lo + tiles, :], h[:, lo:lo + tiles, :],
                                          h_r[:, hi:hi + tiles, :].bitcast(F32), ALU.subtract).then_inc(y_split, 1)
                    elif step == "merge":
                        rest_next(step, i, 0)
                        for j in range(3):
                            wait_emptied(dve, l, "gate", 3 * i + j)
                        wait_slot(dve, l, step, i, 0)
                        banks = [bank[FILL[step, i, j][0]] for j in range(3)]
                        emptied_by(dve.tensor_tensor(m[:, i, :], g[:, i % GATE_RING, 0, :], banks[0][:, 0:T], ALU.mult),
                                   step, i, 0)
                        emptied_by(dve.tensor_tensor(tmp[:, 0, 0:T], g[:, i % GATE_RING, 1, :], banks[1][:, 0:T], ALU.mult),
                                   step, i, 1)
                        wait_emptied(dve, l, step, i, 0)
                        wait_emptied(dve, l, step, i, 1)
                        link(dve.tensor_tensor(m[:, i, :], m[:, i, :], tmp[:, 0, 0:T], ALU.add))
                        rest_next(step, i, 1)
                        wait_slot(dve, l, step, i, 1)
                        emptied_by(dve.tensor_tensor(tmp[:, 1, 0:T], g[:, i % GATE_RING, 2, :], banks[2][:, 0:T], ALU.mult),
                                   step, i, 2)
                        wait_emptied(dve, l, step, i, 2)
                        dve.tensor_tensor(m[:, i, :], m[:, i, :], tmp[:, 1, 0:T], ALU.add).then_inc(merged, 1)
                        dve.wait_ge(merged, l * KT8 + i + 1)
                        dve.wait_ge(m_hi_ready, l * KT8 + i + 1)
                        dve.tensor_tensor(m_lo[:, i, :], m[:, i, :], h_r[:, M_HI + i, :].bitcast(F32), ALU.subtract
                                          ).then_inc(m_split, 1)
                    elif step == "out":
                        dve.tensor_tensor(z[:, i, :], x_hi[:, i, :].bitcast(F32), x_lo[:, i, :].bitcast(F32),
                                          ALU.add).then_inc(residual, 1)
                        dve.wait_ge(residual, l * KT8 + i + 1)
                        wait_slot(dve, l, step, i)
                        emptied_by(dve.scalar_tensor_tensor(out=z[:, i, :], in0=z[:, i, :], scalar=ALPHA,
                                                            in1=bank[FILL[step, i, 0][0]][:, 0:T],
                                                            op0=ALU.mult, op1=ALU.add), step, i)
                    elif step == "norm":
                        dve.wait_ge(mean_ready, l + 1)
                        wait_emptied(dve, l, "out", KT8 - 1)
                        wait_emptied(dve, l, "out", KT8 - 2)
                        for k in range(4):
                            part = z[:, 2 * k:2 * k + 2, :]
                            dve.tensor_tensor(part, part, bank[SA][:, 0:T].unsqueeze(1).to_broadcast([P, 2, T]),
                                              ALU.subtract).then_inc(centered, 1)
                            dve.wait_ge(centered, l * 4 + k + 1)
                        rest_next(step, i)
                        dve.wait_ge(std_ready, l + 1)
                        link(dve.reciprocal(rstd[:, :], rstd[:, :]))
                        dve.wait_ge(state_stored, (l + 1) * 16)
                        for k in range(4):
                            for n in (2 * k, 2 * k + 1):
                                ins = dve.scalar_tensor_tensor(out=z[:, n, :], in0=z[:, n, :],
                                                               scalar=pr("ln_g", n, 1), in1=rstd[:, :],
                                                               op0=ALU.mult, op1=ALU.mult)
                            ins.then_inc(scaled, 1)
                        dve.wait_ge(scaled, (l + 1) * 4)
                        for k in range(4):
                            dve.wait_ge(x_hi_ready, (l + 1) * 4 + k + 1)
                            for n in (2 * k, 2 * k + 1):
                                ins = dve.scalar_tensor_tensor(out=x_lo[:, n, :], in0=z[:, n, :],
                                                               scalar=pr("ln_b", n, 1),
                                                               in1=x_hi[:, n, :].bitcast(F32),
                                                               op0=ALU.add, op1=ALU.subtract)
                            ins.then_inc(x_ready, 1)
                        dve.wait_ge(x_ready, (l + 2) * 4)
                assert steps[0] == VECTOR_STEPS, f"VECTOR_STEPS is {steps[0]}"
            for n in range(2):
                half = slice(4 * n, 4 * n + 4)
                dve.tensor_tensor(m[:, half, :], x_hi[:, half, :].bitcast(F32), x_lo[:, half, :].bitcast(F32),
                                  ALU.add).then_inc(output_ready, 1)


def _constants():
    t = {k: np.zeros((P, n), np.float32) for k, (_, n) in CST.items()}
    half = 8
    inv = (1.0 / (500000.0 ** (np.arange(0, 16, 2, dtype=np.float32) / 16))).astype(np.float32)
    pos = np.concatenate([np.arange(SEQ), np.full(NB, PAST)]).astype(np.float32)
    cpos = (np.arange(NC) * CT + TAPS - 1).astype(np.float32)
    for cos, sin, at in (("rope_c", "rope_s", pos), ("cmp_c", "cmp_s", cpos)):
        ang = (at[None, :] * inv[:, None]).astype(np.float32).astype(np.float64)
        n = len(at)
        t[cos][:, 0:n] = 1.0
        for g2 in range(2):
            a = g2 * HD
            t[cos][a:a + half, 0:n] = np.cos(ang)
            t[cos][a + half:a + 2 * half, 0:n] = np.cos(ang)
            t[sin][a:a + half, 0:n] = -np.sin(ang)
            t[sin][a + half:a + 2 * half, 0:n] = np.sin(ang)
    for g2 in range(2):
        for d in range(half):
            t["perm"][g2 * HD + d, g2 * HD + d + half] = 1.0
            t["perm"][g2 * HD + d + half, g2 * HD + d] = 1.0
    t["ident"] = np.eye(P, dtype=np.float32)
    q = np.arange(P)
    t["causal"] = np.where(q[None, :] <= q[:, None], 0.0, MASKED).astype(np.float32)
    end = np.arange(CT) * CT + TAPS - 1
    for qi in range(2):
        rows = q + (1 - qi) * P
        ok = (end[None, :] <= rows[:, None]) & (np.arange(CT)[None, :] < NC)
        t["cmp_mask"][:, qi * CT:(qi + 1) * CT] = np.where(ok, 0.0, MASKED)
    t["own_row"] = (q[:, None] % NB == np.arange(NB)[None, :]).astype(np.float32)
    r_of, g_of = q // 32, q // CT % 2
    for r in range(R):
        t["own_head"][:, r * P:(r + 1) * P] = ((r_of == r)[:, None] & (g_of[:, None] == (q // HD)[None, :]))
    for k, w in enumerate(WINDOWS):
        t["inv_count"][:, k * CT:(k + 1) * CT] = (1.0 / np.minimum(w, np.arange(CT) + 1)).astype(np.float32)
    t["gate_head"] = (q[:, None] % HEADS == np.arange(HEADS)[None, :]).astype(np.float32)
    t["gate_type"] = (q[:, None] // HEADS == np.arange(3)[None, :]).astype(np.float32)
    return np.concatenate([t[k] for k in CST], axis=1).astype(np.float32)


def kernel(**inputs):
    import concourse.bacc as _bacc
    from concourse.bass_utils import run_bass_kernel_spmd as _run

    a = {k: np.asarray(v) for k, v in inputs.items()}
    D = DEPTH

    def tiles(w):
        _, kk, n = w.shape
        return w.reshape(D, kk // P, P, n // P, P).transpose(0, 3, 2, 1, 4).reshape(D, n // P, P, kk // P * P)

    sizes = (512, 512, 512, 512, 512, 512, 1024, 256, 256, 256, 256, 256, 256, 48, 1024, 3072)
    at = dict(zip(("pu", "pz", "cb", "cc", "cx", "cz", "q", "kc", "vc", "ks", "vs", "kw", "vw", "ng", "az", "mg"),
                  np.concatenate([[0], np.cumsum(sizes)[:-1]])))
    head = np.arange(HEADS).reshape(GP, 2, R).transpose(0, 2, 1).reshape(-1)
    by_head = (head[:, None] * HD + np.arange(HD)[None, :]).reshape(-1)
    w_in = a["w_in"]

    def part(name, n):
        return w_in[:, :, at[name]:at[name] + n]

    ng = np.zeros((D, D_MODEL, P), np.float32)
    ng[:, :, 0:48] = w_in[:, :, at["ng"] + (head[None, :] * 3 + np.arange(3)[:, None]).reshape(-1)]
    first = tiles(np.concatenate([part("kc", 256), part("vc", 256), part("ks", 256), part("kw", 256),
                                  part("vs", 256), part("vw", 256), w_in[:, :, at["q"] + by_head], ng], axis=2))
    second = tiles(np.concatenate([part("pu", 512), part("cb", 512), part("cc", 512), part("cx", 512),
                                   part("pz", 512), part("cz", 512), w_in[:, :, at["az"] + by_head]], axis=2))
    taps = a["cmp_w"].reshape(D, 2, TAPS, HD, HD).transpose(0, 1, 3, 2, 4)
    cmp = np.zeros((D, 2, 2, HD, TAPS, 2, HD), np.float32)
    for g2 in range(2):
        cmp[:, :, g2, :, :, g2, :] = taps
    cmp = cmp.reshape(D, 2, P, 4, 8 * P).transpose(0, 1, 3, 2, 4).reshape(D, 8, P, 8 * P)
    mg = tiles(part("mg", 3072)).reshape(D, 3, KT8, P, 8 * P)
    ab = np.concatenate([tiles(a["proj_a"]), tiles(a["proj_b"])], axis=3)
    pc = tiles(a["proj_c"][:, by_head, :])
    out_w = tiles(a["w_out"])
    dense = np.concatenate([first, second], axis=1)
    rows = {"dense": lambda i: [dense[:, i]], "cmp_k": lambda i: [cmp[:, n] for n in range(4)],
            "cmp_v": lambda i: [cmp[:, 4 + n] for n in range(4)], "gate": lambda i: [mg[:, i % 3, i // 3]],
            "merge": lambda i: [ab[:, i], pc[:, i]], "out": lambda i: [out_w[:, i]]}
    weights = np.stack([row for step, i in ORDER if step in rows for row in rows[step](i)], axis=1)
    weights = np.concatenate([weights.reshape(D * SLOTS, P, KT8 * P), weights[0, 0:2]], axis=0)

    def by_part(v, n):
        return v.reshape(D, n, P).transpose(0, 2, 1)

    pe = a["cmp_pe"].transpose(0, 1, 3, 2)
    pe = np.concatenate([pe, pe], axis=2)
    params = np.concatenate([
        by_part(a["pool_scale"], 4),
        a["conv_w"].reshape(D, 3, 4, P).transpose(0, 3, 2, 1).reshape(D, P, 12),
        by_part(a["ln_g"], 8), by_part(a["ln_b"], 8), pe[:, 0], pe[:, 1],
        a["state_pool"].reshape(D, NB, HIST, 4, P).transpose(0, 4, 3, 1, 2).reshape(D, P, -1),
        a["state_conv"].reshape(D, NB, 2, 4, P).transpose(0, 4, 3, 2, 1).reshape(D, P, -1),
        a["pool_w"].transpose(0, 2, 1, 3).reshape(D, P, 4 * P)], axis=2)
    xs = np.concatenate([a["x_prompt"].reshape(SEQ, D_MODEL), a["x_sample"].reshape(NB, D_MODEL)], axis=0)
    pool_n = a["cache_k_cmp"].shape[1]

    def cache_cols(v):
        return v.reshape(D, pool_n, P, GP, P).transpose(0, 1, 4, 3, 2)

    arrays = {
        "x_in": xs.T.reshape(KT8, P, T).transpose(1, 0, 2), "weights": weights, "params": params,
        "consts": _constants(), "pages": a["page_table"].reshape(1, -1).astype(np.int32),
        "kcmp": cache_cols(a["cache_k_cmp"]), "vcmp": cache_cols(a["cache_v_cmp"]),
        "ksel": cache_cols(a["cache_k_sel"]), "vsel": a["cache_v_sel"].reshape(D, pool_n, P, 4 * HD),
        "kwin": a["state_k_win"].reshape(D, NB, PAST, GP, P).transpose(0, 4, 1, 3, 2).reshape(D, P, NB * GP, PAST),
        "vwin": a["state_v_win"].reshape(D, NB, 2, P, 4 * HD).transpose(0, 3, 1, 2, 4).reshape(D, P, -1),
    }
    outs = {"y": (P, KT8, T), "kv": (D, P, 12, T), "state": (D, P, N_ST),
            "kwin_out": (D, P, NB * GP, PAST), "vwin_out": (D, P, NB * 4 * HD * 2)}
    nc = _bacc.Bacc("TRN2", target_bir_lowering=False, num_devices=1)
    args = []
    for name in arrays:
        arrays[name] = np.ascontiguousarray(arrays[name])
        args.append(nc.dram_tensor(name + "_dram", arrays[name].shape, mybir.dt.from_np(arrays[name].dtype),
                                   kind="ExternalInput").ap())
    for name, shape in outs.items():
        args.append(nc.dram_tensor(name + "_dram", shape, F32, kind="ExternalOutput").ap())
    trunk(nc, *args)
    got = _run(nc, [{name + "_dram": v for name, v in arrays.items()}], core_ids=[0]).results[0]
    got = {name: got[name + "_dram"] for name in outs}

    y = np.asarray(got["y"]).transpose(2, 1, 0).reshape(T, D_MODEL)
    kv = np.asarray(got["kv"]).reshape(D, P, 6, GP, T).transpose(2, 0, 4, 3, 1).reshape(6, D, T, 4, HD)
    kc, vc, ks, kw, vs, vw = (kv[n] for n in range(6))
    st = np.asarray(got["state"])

    def p_of(v):
        return v[:, 0:SEQ].reshape(D, 1, SEQ, 4, HD)

    def s_of(v):
        return v[:, SEQ:T].reshape(D, NB, 1, 4, HD)

    kwo = np.asarray(got["kwin_out"]).reshape(D, P, NB, GP, PAST).transpose(0, 2, 4, 3, 1).reshape(D, NB, PAST, 4, HD)
    vwo = np.asarray(got["vwin_out"]).reshape(D, P, NB, 2, 4 * HD).transpose(0, 2, 3, 1, 4).reshape(
        D, NB, PAST, 4, HD)
    p_pool = st[:, :, ST_PP:ST_PS].reshape(D, P, 4, HIST).transpose(0, 3, 2, 1).reshape(D, 1, HIST, 512)
    s_pool = st[:, :, ST_PS:ST_CP].reshape(D, P, 4, NB, HIST).transpose(0, 3, 4, 2, 1).reshape(D, NB, HIST, 512)
    p_conv = st[:, :, ST_CP:ST_CS].reshape(D, P, 4, 2).transpose(0, 3, 2, 1).reshape(D, 1, 2, 512)
    s_conv = st[:, :, ST_CS:N_ST].reshape(D, P, 4, 2, NB).transpose(0, 4, 3, 2, 1).reshape(D, NB, 2, 512)
    out = (y[0:SEQ].reshape(1, SEQ, D_MODEL), y[SEQ:T].reshape(NB, 1, D_MODEL),
           p_of(kc), p_of(vc), p_of(ks), p_of(vs), p_of(kw), p_of(vw), p_pool, p_conv,
           s_of(kc), s_of(vc), s_of(ks), s_of(vs),
           np.concatenate([kwo, s_of(kw)], axis=2), np.concatenate([vwo, s_of(vw)], axis=2), s_pool, s_conv)
    return tuple(np.ascontiguousarray(v) for v in out)
```

```python
from contextlib import ExitStack

import numpy as np

import concourse.bass as bass
from concourse import mybir

F32 = mybir.dt.float32
F32R = mybir.dt.float32r
BF16 = mybir.dt.bfloat16
I32 = mybir.dt.int32
ALU = mybir.AluOpType
ACT = mybir.ActivationFunctionType
AX_X = mybir.AxisListType.X

P = 128
DEPTH = 2
D_MODEL = 1024
SEQ = 256
NB = 8
T = SEQ + NB
PAST = 256
KEYS = PAST + 1
HD = 64
HEADS = 16
GP = 2
R = 4
CT = 16
TAPS = 32
CMP_CACHED = NB * 2 * 4 * P // 2
CMP_OWN = 2 * 4 * SEQ // 2
NC = 15
KT8 = D_MODEL // P
ALPHA = (2 * DEPTH) ** 0.25
EPS = 1e-5
QK = HD ** -0.5
MASKED = -1.0e30
FLOOR = -1.0e29
WINDOWS = (2, 4, 8, 16)
HIST = 15

KC, VC, KS, KW, VS, VW, Q, NG = 0, 2, 4, 6, 8, 10, 12, 20
PU, CB, CC, CX, PZ, CZ, AZ = 21, 25, 29, 33, 37, 41, 45
KEPT = 53
LATE = 38
Y_A_HI, Y_B_HI, Y_C_HI, M_HI = VS, CZ, KC, AZ
LATE_PV = 46
ROPED = [KS, KS + 1, KW, KW + 1] + list(range(Q, Q + 8))

RING = 5
PRM = {}
_at = 0
for _name, _n in (("pool_scale", 4), ("conv_w", 12), ("ln_g", 8), ("ln_b", 8), ("pe_k", CT), ("pe_v", CT),
                  ("pool_hist", 4 * NB * HIST), ("conv_hist", 4 * 2 * NB), ("pool_w", 4 * P)):
    PRM[_name] = (_at, _n)
    _at += _n
N_PRM = _at
CST = {}
_at = 0
for _name, _n in (("rope_c", T), ("rope_s", T), ("cmp_c", CT), ("cmp_s", CT), ("ident", P), ("perm", P),
                  ("causal", P), ("cmp_mask", 2 * CT), ("own_row", NB), ("own_head", 4 * P),
                  ("inv_count", 4 * CT), ("gate_head", HEADS), ("gate_type", 3),
                  ("own_pick", GP * 2 * HD)):
    CST[_name] = (_at, _n)
    _at += _n
N_CST = _at
ST_PP, ST_PS, ST_CP, ST_CS, N_ST = 0, 60, 540, 548, 612


def make_order():
    order = []
    for n in range(21):
        order.append(("dense", n))
        if n - 1 in ROPED:
            order.append(("rope", n - 1))
        if n in (9, 10):
            order.append(("cmp_swap", n - 9))
        if n == 13:
            order += [("v_rows", 0), ("v_rows", 1)]
        if n == 15:
            order.append(("v_new_in", 0))
        if n == 18:
            order.append(("v_new", 0))
    order += [("cmp_k", 0), ("gates", 0), ("cmp_v", 0), ("cmp_sum", 0), ("cmp_sum", 1), ("dense", 21),
              ("cmp_rope", 0), ("cmp_vrows", 0), ("dense", 22), ("cmp_scores", 0), ("dense", 23), ("cmp_soft", 0),
              ("dense", 24)]
    nxt = 25
    for u in range(HEADS):
        order.append(("scores", u))
        if u == 0:
            order.append(("cmp_turn", 0))
        if u > 0:
            order.append(("turn", u - 1))
        order.append(("exp", u))
        order.append(("dense", nxt))
        nxt += 1
        if u > 0:
            order.append(("pv", u - 1))
        order.append(("scale", u))
        if u in POOL_AFTER:
            order.append(("pool", POOL_AFTER.index(u)))
    order += [("one_cmp_scores", 0), ("one_scores", 0), ("turn", HEADS - 1), ("dense", 41), ("pv", HEADS - 1),
              ("one_turn", 0), ("dense", 42), ("conv", 0), ("dense", 43), ("one_pv", 0), ("conv", 1),
              ("dense", 44), ("conv", 2), ("dense", 45), ("one_scores", 1), ("dense", 46), ("one_turn", 1),
              ("one_cmp_turn", 0), ("conv", 3), ("dense", 47), ("one_pv", 1), ("silu", 0), ("mix", 0),
              ("dense", 48), ("one_out", 0), ("silu", 1), ("mix", 1), ("dense", 49), ("conv", 4), ("mix", 2),
              ("dense", 50), ("y", 0), ("mix", 3), ("dense", 51), ("y_high", 0), ("y", 2),
              ("dense", 52), ("y_high", 1), ("y_rest", 0), ("y_high", 2)]
    for n in range(3 * GATE_RING):
        order.append(("gate", n))
        order += [[("y_rest", 1), ("y_rest", 2), ("y", 3)], [("y_high", 3)], [("y_rest", 3), ("y", 4)],
                  [("y_high", 4)], [("y_rest", 4), ("y", 5)], [("y_high", 5)], [("y_rest", 5)], [], []][n]
    for i in range(KT8):
        if i >= GATE_RING:
            order += [("gate", 3 * i + j) for j in range(3)]
        order.append(("merge", i))
    for i in range(KT8):
        order.append(("out", i))
        if i:
            order.append(("mean", i - 1))
    order += [("mean", KT8 - 1), ("norm", 0)]
    return order


POOL_AFTER = (1, 3, 4, 6, 7, 9, 10, 12)
GATE_RING = 3
Y_PARTS = [(CB, Y_B_HI, 4), (PU, Y_A_HI, 4)] + [(Q + 2 * n, Y_C_HI + 2 * n, 2) for n in range(4)]
ORDER = make_order()
_silu = [s for s in ORDER if s[0] == "silu" or s[0] == "dense" and s[1] >= AZ]
SIGMOIDS, SIGMOIDS_BEFORE = len(_silu), {s: n + 1 for n, s in enumerate(_silu)}
SLOTS_OF_STEP = {"dense": 1, "cmp_k": 1, "cmp_v": 1, "gate": 1, "merge": 2, "out": 1}
SLOT_OF, SLOTS = {}, 0
for _step in ORDER:
    if _step[0] in SLOTS_OF_STEP:
        SLOT_OF[_step] = SLOTS
        SLOTS += SLOTS_OF_STEP[_step[0]]
SLOT_CK, SLOT_CV = SLOT_OF["cmp_k", 0], SLOT_OF["cmp_v", 0]
SPLIT_SLOTS = [n for n in range(SLOTS) if not SLOT_CK <= n < SLOT_CV + 1]
SPLIT_NO = {n: d for d, n in enumerate(SPLIT_SLOTS)}
SPLITS = len(SPLIT_SLOTS)
HI_RING = 3
D0, D1, SA, SB, PT0, PT1, OT, MI = range(8)


def banks_of(step, i):
    if step == "dense":
        return [i % 2]
    if step == "gate":
        return [(KEPT + i) % 2]
    if step == "merge":
        return [SA, SB, PT0] if i % 2 == 0 else [PT1, OT, MI]
    if step == "out":
        return [(KEPT + 3 * KT8 + i) % 2]
    if step == "turn":
        return [PT0, PT1]
    if step == "scores":
        return [SA, SB]
    if step == "pv":
        return [OT] if i % 2 else []
    if step == "mix":
        return [(SA, SB, PT0, PT1)[i]]
    if step == "v_rows":
        return [(PT0, PT1)[i]]
    if step == "cmp_sum":
        return [(PT1, SA)[i]]
    if step == "one_scores":
        return [(SA, PT0)[i]]
    if step == "one_turn":
        return [(PT1, SB)[i]]
    if step == "one_pv":
        return [OT] if i else []
    return {"rope": [MI], "v_new": [SB], "cmp_swap": [MI], "cmp_k": [SA, SB], "gates": [MI],
            "cmp_v": [OT, PT0], "cmp_rope": [MI],
            "cmp_vrows": [SB], "cmp_scores": [SA], "cmp_turn": [PT0], "one_cmp_scores": [SB],
            "one_cmp_turn": [MI], "one_out": [MI]}.get(step, [])


def plan_fills():
    fill, total = {}, [0] * 8
    for step, i in ORDER:
        for j, b in enumerate(banks_of(step, i)):
            total[b] += 1
            fill[step, i, j] = (b, total[b])
    return fill, total


FILL, FILLS = plan_fills()
BY_SLOT = set(SLOTS_OF_STEP)
FILLED = [sum(1 for (s, i, j), (b, k) in FILL.items() if b == bank and s not in BY_SLOT) for bank in range(8)]


def filled_count(step, i, j):
    bank, k = FILL[step, i, j]
    return bank, sum(1 for (s, a, c), (b, m) in FILL.items() if b == bank and m <= k and s not in BY_SLOT)



def plan_splits():
    split = {}
    for step, i in ORDER:
        if step in SLOTS_OF_STEP and step not in ("cmp_k", "cmp_v"):
            used = [SPLIT_NO[SLOT_OF[step, i] + j] for j in range(SLOTS_OF_STEP[step])]
            split[step, i] = [d + 2 for d in used]
    for u in range(HEADS):
        split["scores", u] = split.pop(("dense", 25 + u))
    split["out", KT8 - 2], split["out", KT8 - 1], split["norm", 0] = [], [SPLITS], [SPLITS + 1]
    return split


SPLIT_AT = plan_splits()
SLOTS_IN = [sum(1 for i in range(SLOTS) if i % RING == s) for s in range(RING)]
VECTOR_STEPS = 152


def trunk(nc, x_in, weights, params, consts, pages, kcmp, vcmp, ksel, vsel, kwin, vwin,
          y_out, kv_out, state_out, kwin_out, vwin_out):
    n_pool = kcmp.shape[1]
    with ExitStack() as ctx:
        def sb(name, shape, dt=F32):
            return ctx.enter_context(nc.sbuf_tensor(name, shape, dt))

        def sem(name):
            return ctx.enter_context(nc.semaphore(name))

        bank = [ctx.enter_context(nc.psum_tensor(f"bank{b}", [P, 512], F32)) for b in range(8)]

        def shared(name, shape, at, dt=F32R):
            return nc.alloc_sbuf_tensor_at(name, shape, dt, offset=at)

        x_hi = sb("x_hi", [P, KT8, T], F32R)
        x_lo = sb("x_lo", [P, KT8, T], F32R)
        z = sb("z", [P, KT8, T])
        m_at = nc.sbuf_base
        m = sb("m", [P, KT8, T])
        m_lo = shared("m_lo", [P, KT8, T], m_at)
        h_at = nc.sbuf_base
        h = sb("h", [P, KEPT, T])
        h_r = shared("h_rounded", [P, KEPT, T], h_at)
        ring_at = nc.sbuf_base
        ring = sb("ring", [P, RING, KT8, P])
        w_lo = shared("w_lo", [P, RING, KT8, P], ring_at)
        w_hi = sb("w_hi", [P, HI_RING, KT8, P], F32R)
        cache_a = sb("cache_a", [P, 10 * GP * PAST])
        cache_b = sb("cache_b", [P, 10 * GP * PAST])
        prm = sb("prm", [P, N_PRM])
        cst = sb("cst", [P, N_CST])
        page = sb("page", [1, NB * 2], I32)
        causal_b = sb("causal_b", [P, P], BF16)
        ident_b = sb("ident_b", [P, P], BF16)
        ones = sb("ones", [P, P])
        eps = sb("eps", [P, 1])
        v_rows = sb("v_rows", [P, 2, 4 * P])
        v_new_c = sb("v_new_c", [P, GP, 2, NB])
        v_new = sb("v_new", [2 * NB, GP * P])
        gate = sb("gate", [P, 99])
        gate_d = sb("gate_d", [P, NB, HEADS])
        kc_all = sb("kc_all", [P, GP, NB + 1, CT])
        vc_all = sb("vc_all", [P, GP, NB + 1, CT])
        vc_rep = sb("vc_rep", [P, GP, 8, CT])
        kc_bd = sb("kc_bd", [P, GP, 2, CT])
        vc_one = sb("vc_one", [P, GP, P])
        bias = sb("bias", [P, 2])
        tmp = sb("tmp", [P, 3, 288])
        c_max = sb("c_max", [P, 32])
        c_sum = sb("c_sum", [P, 32])
        probs = sb("probs", [P, 2, 768])
        probs_t = sb("probs_t", [P, 2, 2, 384])
        u_max = sb("u_max", [P, 2, 4])
        u_sum = sb("u_sum", [P, 2, 4])
        u_fac = sb("u_fac", [P, 2, 4])
        p_cmp = sb("p_cmp", [P, CT])
        p_cmp_x = sb("p_cmp_x", [P, NB, CT])
        p_tail = sb("p_tail", [P, 2, NB])
        one_max = sb("one_max", [P, 3])
        one_sum = sb("one_sum", [P, 3])
        p_cmp_t = sb("p_cmp_t", [P, P])
        p_tail_t = sb("p_tail_t", [2 * NB, P])
        pu_one = sb("pu_one", [P, 4, NB, HIST + 1])
        pu_sum = sb("pu_sum", [P, 4, NB])
        hc_one = sb("hc_one", [P, 4, 3, NB])
        state = sb("state", [P, N_ST])
        rstd = sb("rstd", [P, T])

        NE = HIST + SEQ
        hf = h[:, LATE:KEPT, :].rearrange("p a t -> p (a t)")
        sum_a = hf[:, 0:4 * NE].rearrange("p (g t) -> p g t", g=4)
        sum_b = hf[:, 4 * NE:8 * NE].rearrange("p (g t) -> p g t", g=4)
        pc_t = hf[:, 8 * NE:8 * NE + GP * SEQ].rearrange("p (g t) -> p g t", g=GP)
        vc_at = 8 * NE + GP * SEQ
        vc_bd = hf[:, vc_at:vc_at + GP * R * P].rearrange("p (g r n) -> p g r n", g=GP, r=R)
        halves = hf[:, 0:2 * 10 * 4 * CT].rearrange("p (v s g c) -> p v s g c", v=2, s=10, g=4)
        zf = z[:, :, :].rearrange("p a t -> p (a t)")
        mf = m[:, :, :].rearrange("p a t -> p (a t)")
        q_pad = zf[:, 0:NB * GP * 32].rearrange("p (b g n) -> p b g n", b=NB, g=GP)
        pu_ext = mf[:, 0:4 * NE].rearrange("p (g t) -> p g t", g=4)
        hc_ext = mf[:, 0:4 * (2 + SEQ)].rearrange("p (g t) -> p g t", g=4)
        g = h[:, CC:CC + 3 * GATE_RING, :].rearrange("p (a j) t -> p a j t", j=3)
        probs_flat = probs[:, :, :].rearrange("p a n -> p (a n)")
        cs = probs_flat[:, 768:768 + 32 * CT].rearrange("p (n c) -> p n c", c=CT)
        p_one = probs_flat[:, 0:2 * KEYS].rearrange("p (a n) -> p a n", a=2)
        p_one_t = probs_t[:, :, :, :].rearrange("p a b n -> p (a b n)")[:, 0:4 * P].rearrange("p (a n) -> p a n", a=2)
        o_one = probs_flat[:, 768:768 + 2 * GP * P]
        cmp_view = [c[:, 0:CMP_CACHED].rearrange("p (s t) -> p s t", t=4 * HD) for c in (cache_a, cache_b)]
        k_one = cache_a[:, 0:NB * GP * KEYS].rearrange("p (b g t) -> p b g t", b=NB, g=GP)
        v_one = cache_b[:, 0:NB * 2 * 2 * P].rearrange("p (b t n) -> p b t n", b=NB, t=2)

        def c(name):
            at, n = CST[name]
            return cst[:, at:at + n]

        def pr(name, i=0, n=None):
            at, size = PRM[name]
            return prm[:, at + i:at + i + (size if n is None else n)]

        ident, perm = c("ident"), c("perm")

        consts_loaded, pages_loaded = sem("consts_loaded"), sem("pages_loaded")
        x_loaded = [sem(f"x_pair{k}_loaded") for k in range(KT8 // 2)]
        params_loaded = sem("params_loaded")
        landed = [sem(f"weight_landed{s}") for s in range(RING)]
        cmp_k_landed, cmp_v_landed = sem("cmp_k_landed"), sem("cmp_v_landed")
        sel_k_landed, sel_v_landed = sem("sel_k_landed"), sem("sel_v_landed")
        win_k_landed, win_v_landed = sem("win_k_landed"), sem("win_v_landed")
        slots_done = sem("slots_done")
        x_ready = sem("x_ready")
        x_hi_ready = sem("x_hi_ready")
        w_hi_ready, w_lo_ready = sem("w_hi_ready"), sem("w_lo_ready")
        output_ready = [sem("output_ready_scalar"), sem("output_ready_vector")]
        scaled, residual = sem("scaled"), sem("residual")
        filled = [sem(f"bank{b}_filled") for b in range(8)]
        emptied = [sem(f"bank{b}_emptied") for b in range(8)]
        tables_ready = sem("tables_ready")
        vector_step = sem("vector_step")
        roped = sem("roped")
        cmp_in_ready = sem("cmp_in_ready")
        v_new_ready = sem("v_new_ready")
        gate_d_ready = sem("gate_d_ready")
        cmp_out_ready = sem("cmp_out_ready")
        kc_ready = sem("kc_ready")
        cmp_shifted, cmp_exped, cmp_probs = sem("cmp_shifted"), sem("cmp_exped"), sem("cmp_probs")
        max_ready, probs_ready, pv_even = sem("max_ready"), sem("probs_ready"), sem("pv_even")
        q_pad_clear, q_pad_ready = sem("q_pad_clear"), sem("q_pad_ready")
        k_new_ready = sem("k_new_ready")
        one_max_ready, one_exped, one_probs = sem("one_max_ready"), sem("one_exped"), sem("one_probs")
        sel_v_used = sem("sel_v_used")
        sigmoids = sem("sigmoids")
        pooled, convolved = sem("pooled"), sem("convolved")
        y_ready = sem("y_ready")
        y_hi_ready, y_split = sem("y_hi_ready"), sem("y_split")
        m_hi_ready, m_split = sem("m_hi_ready"), sem("m_split")
        merged, squared, std_ready = sem("merged"), sem("squared"), sem("std_ready")
        mean_ready, squared_sum, centered = sem("mean_ready"), sem("squared_sum"), sem("centered")
        state_ready, state_staged = sem("state_ready"), sem("state_staged")
        pool_goes = sem("pool_goes")
        kv_stored, state_stored, win_copied, y_stored = (
            sem("kv_stored"), sem("state_stored"), sem("win_copied"), sem("y_stored"))

        def split_weight(d):
            following, d = divmod(d, SPLITS)
            slot = SPLIT_SLOTS[d]
            return following, d, slot, slot % RING, d % HI_RING

        block = ctx.enter_context(nc.Block())

        def wait_slot(eng, l, step, i, j=None):
            s = SLOT_OF[step, i] + (SLOTS_OF_STEP[step] - 1 if j is None else j)
            eng.wait_ge(slots_done, l * SLOTS + RING + s + 1)

        def wait_filled(eng, l, step, i, j=0):
            b, k = filled_count(step, i, j)
            eng.wait_ge(filled[b], l * FILLED[b] + k)

        def wait_emptied(eng, l, step, i, j=0):
            b, k = FILL[step, i, j]
            eng.wait_ge(emptied[b], l * FILLS[b] + k)

        @block.sync
        def _(sp):
            def load(row, i):
                return sp.dma_start(ring[:, i % RING, :, :], weights[row].rearrange("a p (k n) -> (a p) k n", k=KT8)
                                    ).then_inc(landed[i % RING], 16)

            load(slice(0, 1), 0)
            for k in range(KT8 // 2):
                part = slice(2 * k, 2 * k + 2)
                sp.dma_start(m[:, part, :], x_in[:, part, :]).then_inc(x_loaded[k], 16)
                if k == 1:
                    load(slice(1, 2), 1)
            with sp.Fori(0, DEPTH) as l:
                for n in range(2, SLOTS + 2):
                    following, i = divmod(n, SLOTS)
                    before = i - RING if i >= RING else max(j for j in range(SLOTS) if j % RING == i) - SLOTS
                    sp.wait_ge(slots_done, (l + following) * SLOTS + RING + before + 1)
                    load(bass.ds(l * SLOTS + n, 1), i)
                    if n == RING:
                        sp.wait_ge(x_ready, l * (KT8 // 2) + KT8 // 2)
                        sp.dma_start(prm[:, :], params[l]).then_inc(params_loaded, 16)
            for k in range(KT8 // 2):
                part = slice(2 * k, 2 * k + 2)
                sp.wait_ge(output_ready[k // 2], k % 2 + 1)
                sp.dma_start(y_out[:, part, :], m[:, part, :]).then_inc(y_stored, 16)
            sp.wait_ge(y_stored, KT8 // 2 * 16)

        @block.gpsimd
        def _(pool):
            pool.dma_start(page[:, :], pages).then_inc(pages_loaded, 16)
            pool.memset(ones[:, :], 1.0 / D_MODEL)
            pool.memset(eps[:, :], EPS)
            for which in range(2):
                pool.memset((cache_a, cache_b)[which][:, CMP_CACHED + CMP_OWN // 2:CMP_CACHED + CMP_OWN], 0.0)
            for t in (kc_all, vc_all, kc_bd):
                dims = " ".join("abcd"[:len(t.shape) - 1])
                pool.memset(t[tuple(slice(None) for _ in t.shape)].rearrange(f"p {dims} -> p ({dims})"), 0.0)
            pool.memset(p_cmp[:, :], 0.0)
            pool.wait_ge(landed[RING - 1], 16)
            pool.dma_start(cst[:, :], consts).then_inc(consts_loaded, 16)
            pool.wait_ge(consts_loaded, 16)
            pool.tensor_copy(causal_b[:, :], c("causal"))
            pool.tensor_copy(ident_b[:, :], ident).then_inc(tables_ready, 1)
            pool.wait_ge(pages_loaded, 16)

            def load_pages(l, cache, dst_of, landed_sem):
                with pool.Fori(0, NB) as b:
                    for half in range(2):
                        pg = pool.value_load(page[0:1, bass.ds(b * 2 + half, 1)], min_val=0, max_val=n_pool - 1)
                        pool.dma_start(dst_of(b, half), cache[bass.ds(l, 1), bass.ds(pg, 1)].rearrange(
                            "a b p n -> (a b p) n" if len(cache.shape) == 4 else "a b p g n -> (a b p) g n")
                            ).then_inc(landed_sem, 16)

            def cmp_dst(view):
                return lambda b, half: view[:, bass.ds(b * 2 + half, 1), :].rearrange("p s t -> p (s t)")

            def go():
                pool.sem_inc(pool_goes, 1)

            with pool.Fori(0, DEPTH) as l:
                pool.wait_ge(x_ready, l * (KT8 // 2) + KT8 // 2)
                go()
                load_pages(l, kcmp, cmp_dst(cmp_view[0]), cmp_k_landed)
                load_pages(l, vcmp, cmp_dst(cmp_view[1]), cmp_v_landed)
                pool.wait_ge(roped, l * len(ROPED) + 4)
                wait_emptied(pool, l, "dense", VW)
                wait_emptied(pool, l, "dense", VW + 1)
                go()
                pool.dma_start(kv_out[l], h[:, 0:12, :]).then_inc(kv_stored, 16)
                wait_slot(pool, l, "cmp_k", 0)
                go()
                load_pages(l, ksel, lambda b, half: k_one[:, bass.ds(b, 1), :, half * P:half * P + P].rearrange(
                    "p s g t -> p (s g) t"), sel_k_landed)
                wait_slot(pool, l, "cmp_v", 0)
                go()
                load_pages(l, vsel, lambda b, half: v_one[:, bass.ds(b, 1), half, :].rearrange(
                    "p s n -> p (s n)"), sel_v_landed)
                pool.wait_ge(max_ready, l * HEADS + 2)
                go()
                pool.dma_start(kwin_out[l], kwin[l]).then_inc(win_copied, 16)
                pool.wait_ge(max_ready, l * HEADS + 7)
                go()
                pool.dma_start(vwin_out[l], vwin[l]).then_inc(win_copied, 16)
                pool.wait_ge(state_ready, 2 * l + 1)
                go()
                pool.tensor_copy(state[:, ST_PP:ST_PS].rearrange("p (g t) -> p g t", g=4),
                                 pu_ext[:, :, SEQ:SEQ + HIST])
                pool.tensor_copy(state[:, ST_PS:ST_CP].rearrange("p (g b t) -> p g b t", g=4, b=NB),
                                 pu_one[:, :, :, 1:HIST + 1]).then_inc(state_staged, 1)
                wait_filled(pool, l, "one_scores", 0)
                go()
                pool.dma_start(k_one[:, :, :, 0:PAST].rearrange("p b g t -> p (b g) t"),
                               kwin[bass.ds(l, 1)].rearrange("a p n t -> (a p) n t")).then_inc(win_k_landed, 16)
                pool.wait_ge(state_ready, 2 * l + 2)
                go()
                pool.tensor_copy(state[:, ST_CP:ST_CS].rearrange("p (g t) -> p g t", g=4), hc_ext[:, :, SEQ:SEQ + 2])
                pool.tensor_copy(state[:, ST_CS:N_ST].rearrange("p (g j b) -> p g j b", g=4, j=2),
                                 hc_one[:, :, 1:3, :]).then_inc(state_staged, 1)
                pool.wait_ge(state_staged, 2 * l + 2)
                go()
                pool.dma_start(state_out[l], state[:, :]).then_inc(state_stored, 16)
                pool.wait_ge(sel_v_used, l + 1)
                go()
                pool.dma_start(v_one.rearrange("p b t n -> p (b t n)"),
                               vwin[bass.ds(l, 1)].rearrange("a p n -> (a p) n")).then_inc(win_v_landed, 16)
            pool.wait_ge(win_copied, 2 * DEPTH * 16)
            pool.wait_ge(kv_stored, DEPTH * 16)
            pool.wait_ge(state_stored, DEPTH * 16)

        @block.tensor
        def _(pe):
            pe.sem_inc(slots_done, RING)
            with pe.Fori(0, DEPTH) as l:
                def weight(i):
                    s = i % RING
                    pe.wait_ge(landed[s], (l * SLOTS_IN[s] + i // RING + 1) * 16)
                    return ring[:, s]

                def split_weight_at(i):
                    d = SPLIT_NO[i]
                    pe.wait_ge(w_lo_ready, l * SPLITS + d + 1)
                    return w_hi[:, d % HI_RING], w_lo[:, i % RING]

                def out_bank(step, i, j=0):
                    b, k = FILL[step, i, j]
                    if k > 1:
                        pe.wait_ge(emptied[b], l * FILLS[b] + k - 1)
                    return bank[b]

                def done(ins, step, i, j=0):
                    b, _ = FILL[step, i, j]
                    ins.then_inc(filled[b], 1)

                def product(out, w, rhs, k0=0, kn=KT8, ready=None):
                    w_high, w_rest = w
                    for k in range(kn):
                        if ready:
                            ready(k)
                        high, rest = rhs(k)
                        pe.matmul(out, w_high[:, k0 + k, :], high, start=(k == 0), stop=False)
                        pe.matmul(out, w_rest[:, k0 + k, :], high, start=False, stop=False)
                        ins = pe.matmul(out, w_high[:, k0 + k, :], rest, start=False, stop=(k == kn - 1))
                    return ins

                def own_scores(out, n, keys):
                    for q in range(2):
                        for gp in range(GP):
                            for b4 in range(4):
                                b = 4 * q + b4
                                ins = pe.matmul(out[32 * b4:32 * b4 + 32, 0:n], q_pad[:, b, gp, :], keys(b, gp),
                                                start=(q == 0 and gp == 0), stop=(q == 1 and gp == 1),
                                                skip_group_check=True)
                    return ins

                def x_tile(k):
                    return x_hi[:, k, :], x_lo[:, k, :]

                for step, i in ORDER:
                    if step == "dense":
                        if i > 1:
                            w = split_weight_at(SLOT_OF[step, i])
                            product(out_bank(step, i)[:, 0:T], w, x_tile).then_inc(slots_done, 1)
                        elif i == 0:
                            outs, ws = [], []
                            for n in range(2):
                                ws.append(split_weight_at(n))
                                outs.append(out_bank(step, n)[:, 0:T])
                                for k in range(KT8):
                                    if n == 0 and k % 2 == 0:
                                        pe.wait_ge(x_hi_ready, l * (KT8 // 2) + k // 2 + 1)
                                    for part in ws[n]:
                                        pe.matmul(outs[n], part[:, k, :], x_hi[:, k, :],
                                                  start=(k == 0 and part is ws[n][0]), stop=False)
                            for n in range(2):
                                for k in range(KT8):
                                    if n == 0 and k % 2 == 0:
                                        pe.wait_ge(x_ready, l * (KT8 // 2) + k // 2 + 1)
                                    ins = pe.matmul(outs[n], ws[n][0][:, k, :], x_lo[:, k, :], start=False,
                                                    stop=(k == KT8 - 1))
                                ins.then_inc(slots_done, 1)
                    elif step == "rope":
                        if i == ROPED[0]:
                            pe.wait_ge(tables_ready, 1)
                        wait_emptied(pe, l, "dense", i)
                        out = out_bank(step, i)
                        done(pe.matmul(out[:, 0:T], perm, h[:, i, :], start=True, stop=True), step, i)
                    elif step == "v_rows":
                        if i == 0:
                            for n in (VW, VW + 1):
                                wait_emptied(pe, l, "dense", n)
                        out = out_bank(step, i)
                        for n in range(4):
                            ins = pe.transpose(out[:, n * P:n * P + P], h[:, VS + n, i * P:i * P + P], ident)
                        done(ins, step, i)
                    elif step == "v_new":
                        out = out_bank(step, i)
                        pe.wait_ge(v_new_ready, l + 1)
                        for gp in range(GP):
                            ins = pe.transpose(out[0:2 * NB, gp * P:gp * P + P],
                                               v_new_c[:, gp, :, :].rearrange("p a b -> p (a b)"), ident)
                        done(ins, step, i)
                    elif step == "gates":
                        wait_emptied(pe, l, "dense", NG)
                        out = out_bank(step, i)
                        for qi in range(2):
                            pe.transpose(out[:, qi * P:qi * P + P], h[:, NG, (1 - qi) * P:(2 - qi) * P], ident)
                        pe.wait_ge(gate_d_ready, l + 1)
                        ins = pe.matmul(out[:, 2 * P:2 * P + 3], gate_d[0:48, :, :].rearrange("p a b -> p (a b)"),
                                        c("gate_type")[0:48, :], start=True, stop=True)
                        done(ins, step, i)
                    elif step in ("cmp_k", "cmp_v"):
                        which = int(step == "cmp_v")
                        outs = [out_bank(step, i, j) for j in range(2)]
                        pe.wait_ge(cmp_v_landed if which else cmp_k_landed, (l + 1) * 16 * 2 * NB)
                        pe.wait_ge(cmp_in_ready, 2 * l + 1 + which)
                        w = weight(SLOT_OF[step, i])
                        rows = (cache_a, cache_b)[which]
                        for tap in range(KT8):
                            pe.matmul(outs[0][:, 0:CMP_CACHED // KT8], w[:, tap, :], rows[:, tap:CMP_CACHED:KT8],
                                      start=(tap == 0), stop=(tap == KT8 - 1))
                            ins = pe.matmul(outs[1][:, 0:CMP_OWN // KT8], w[:, tap, :],
                                            rows[:, CMP_CACHED + tap:CMP_CACHED + CMP_OWN:KT8],
                                            start=(tap == 0), stop=(tap == KT8 - 1))
                        ins.then_inc(slots_done, 1)
                    elif step == "cmp_swap":
                        src = (KC, VC)[i]
                        for gp in range(GP):
                            wait_emptied(pe, l, "dense", src + gp)
                        out = out_bank(step, i)
                        for gp in range(GP):
                            for j in range(2):
                                ins = pe.matmul(out[j * HD:j * HD + HD, gp * SEQ:(gp + 1) * SEQ],
                                                ident[:, (1 - j) * HD:(2 - j) * HD], h[:, src + gp, 0:SEQ],
                                                start=True, stop=True)
                        done(ins, step, i)
                    elif step == "cmp_sum":
                        out = out_bank(step, i)
                        for j in range(2):
                            wait_emptied(pe, l, "cmp_v" if i else "cmp_k", 0, j)
                        for half in range(2):
                            for g2 in range(2):
                                ins = pe.matmul(out[g2 * HD:g2 * HD + HD, 0:10 * GP * NC].rearrange(
                                    "p (s g c) -> p s g c", g=GP, c=NC), ident[:, half * HD:half * HD + HD],
                                    halves[:, i, :, g2:4:2, half:half + NC], start=(half == 0), stop=(half == 1))
                        done(ins, step, i)
                    elif step == "cmp_rope":
                        out = out_bank(step, i)
                        wait_emptied(pe, l, "cmp_sum", 0)
                        done(pe.matmul(out[:, 0:288], perm, kc_all[:, :, :, :].rearrange("p g s c -> p (g s c)"),
                                       start=True, stop=True), step, i)
                    elif step == "cmp_vrows":
                        out = out_bank(step, i)
                        pe.wait_ge(cmp_out_ready, l + 1)
                        for gp in range(GP):
                            pe.transpose(out[:, gp * P:gp * P + P],
                                         vc_rep[:, gp, :, :].rearrange("p a b -> p (a b)"), ident)
                            ins = pe.transpose(out[:, (2 + gp) * P:(3 + gp) * P],
                                               vc_all[:, gp, 0:NB, :].rearrange("p a b -> p (a b)"), ident)
                        done(ins, step, i)
                    elif step == "cmp_scores":
                        out = out_bank(step, i)
                        pe.wait_ge(kc_ready, l + 1)
                        pe.wait_ge(roped, (l + 1) * len(ROPED))
                        for qi in range(2):
                            for n in range(8):
                                col = qi * 256 + n * 32
                                ins = pe.matmul(out[:, col:col + 32], h[:, Q + n, (1 - qi) * P:(2 - qi) * P],
                                                kc_bd[:, n // R, :, :].rearrange("p a b -> p (a b)"),
                                                start=True, stop=True)
                        done(ins, step, i)
                    elif step == "cmp_turn":
                        out = out_bank(step, i)
                        pe.wait_ge(cmp_probs, l + 1)
                        for gp in range(GP):
                            for qi in range(2):
                                src = cs[:, qi * 16 + gp * 8:qi * 16 + gp * 8 + 8, :].rearrange("p a b -> p (a b)")
                                col = gp * SEQ + (1 - qi) * P
                                ins = pe.transpose(out[:, col:col + P], src, ident)
                        done(ins, step, i)
                    elif step == "scores":
                        tile, g2 = Q + i // 2, i % 2
                        gp = i // 8
                        rows = slice(g2 * HD, g2 * HD + HD)
                        for j, (q0, n) in enumerate(((P, 2 * P), (0, P))):
                            out = out_bank(step, i, j)
                            for br, kt in enumerate((KS, KW)):
                                pe.matmul(out[:, br * n:br * n + n], h[rows, tile, q0:q0 + P], h[rows, kt + gp, 0:n],
                                          start=(br == 0), stop=False, skip_group_check=True)
                            ins = pe.matmul(out[:, 0:2 * n].rearrange("p (a n) -> p a n", a=2)[:, :, n - P:n],
                                            ident_b[:, :], causal_b[:, :].unsqueeze(1).to_broadcast([P, 2, P]),
                                            start=False, stop=True, skip_group_check=True)
                            done(ins, step, i, j)
                    elif step == "turn":
                        pe.wait_ge(probs_ready, l * HEADS + i + 1)
                        for br in range(2):
                            out = out_bank(step, i, br)
                            late, early = br * 256, 512 + br * P
                            pe.transpose(out[:, 0:P], probs[:, i % 2, early:early + P], ident)
                            pe.transpose(out[:, P:2 * P], probs[:, i % 2, late:late + P], ident)
                            ins = pe.transpose(out[:, 2 * P:3 * P], probs[:, i % 2, late + P:late + 2 * P], ident)
                            done(ins, step, i, br)
                    elif step == "pv":
                        gp, r, g2 = i // 8, i // 2 % R, i % 2
                        if g2 == 0:
                            if i == 0:
                                wait_emptied(pe, l, "v_rows", 0)
                                wait_emptied(pe, l, "v_rows", 1)
                                wait_emptied(pe, l, "cmp_turn", 0)
                                wait_emptied(pe, l, "cmp_vrows", 0)
                            out = out_bank(step, i + 1)
                            pe.matmul(out[:, 0:SEQ], vc_bd[:, gp, r, :], pc_t[:, gp, :], start=True, stop=False,
                                      skip_group_check=True)
                        out = bank[OT][g2 * HD:g2 * HD + HD, :]
                        gcol = (2 * gp + g2) * HD
                        for br in range(2):
                            wait_emptied(pe, l, "turn", i, br)
                            pt = probs_t[:, i % 2, br, :]
                            pe.matmul(out[:, 0:SEQ], v_rows[:, 0, br * 256 + gcol:br * 256 + gcol + HD],
                                      pt[:, 0:SEQ], start=False, stop=False, skip_group_check=True)
                            ins = pe.matmul(out[:, P:SEQ], v_rows[:, 1, br * 256 + gcol:br * 256 + gcol + HD],
                                            pt[:, SEQ:SEQ + P], start=False, stop=(br == 1), skip_group_check=True)
                        if g2:
                            done(ins, step, i)
                        else:
                            ins.then_inc(pv_even, 1)
                    elif step == "one_cmp_scores":
                        out = out_bank(step, i)
                        pe.wait_ge(q_pad_ready, l + 1)
                        ins = own_scores(out, CT, lambda b, gp: kc_all[:, gp, b, :])
                        done(ins, step, i)
                    elif step == "one_scores":
                        out = out_bank(step, i)
                        pe.wait_ge(win_k_landed if i else sel_k_landed, (l + 1) * (16 if i else 16 * 2 * NB))
                        pe.wait_ge(k_new_ready, 2 * l + i + 1)
                        ins = own_scores(out, KEYS, lambda b, gp: k_one[:, b, gp, :])
                        done(ins, step, i)
                    elif step == "one_turn":
                        out = out_bank(step, i)
                        pe.wait_ge(one_probs, 2 * l + i + 1)
                        for half in range(2):
                            ins = pe.transpose(out[:, half * P:half * P + P],
                                               p_one[:, i, half * P:half * P + P], ident)
                        done(ins, step, i)
                    elif step == "one_cmp_turn":
                        out = out_bank(step, i)
                        pe.transpose(out[:, 0:P], p_cmp_x[:, :, :].rearrange("p b c -> p (b c)"), ident)
                        ins = pe.transpose(out[0:2 * NB, P:2 * P], p_tail[:, :, :].rearrange("p a b -> p (a b)"),
                                           ident)
                        done(ins, step, i)
                    elif step == "one_pv":
                        if i == 0:
                            out_bank("one_pv", 1)
                        wait_emptied(pe, l, "one_turn", i)
                        pe.wait_ge(win_v_landed if i else sel_v_landed, (l + 1) * (16 if i else 16 * 2 * NB))
                        for half in range(2):
                            for b in range(NB):
                                rows = slice(b % 4 * 32, b % 4 * 32 + 32)
                                cols = slice(b // 4 * 2 * P, (b // 4 + 1) * 2 * P)
                                at = half * P + b % 4 * 32
                                ins = pe.matmul(bank[OT][rows, cols], p_one_t[:, i, at:at + 32],
                                                v_one[:, b, half, :], start=(i == 0 and half == 0 and b < 4),
                                                stop=(i == 1 and half == 1), skip_group_check=True)
                        if i == 0:
                            ins.then_inc(sel_v_used, 1)
                        else:
                            done(ins, step, i)
                    elif step == "one_out":
                        out = out_bank(step, i)
                        p_cmp_of = p_cmp_t[:, :].rearrange("p (b g n) -> p g b n", b=NB, g=GP)
                        p_tail_of = p_tail_t[:, :].rearrange("p (b g n) -> p g b n", b=NB, g=GP)
                        for gp in range(GP):
                            cols = out[:, gp * HD:gp * HD + HD].rearrange("p (b n) -> p b n", b=NB)
                            pe.matmul(cols, vc_one[:, gp, :], p_cmp_of[:, gp, :, :], start=(gp == 0), stop=False,
                                      skip_group_check=True)
                            pe.matmul(cols, v_new[:, gp * P:gp * P + P], p_tail_of[:, gp, :, :],
                                      start=False, stop=False, skip_group_check=True)
                        wait_emptied(pe, l, "one_pv", 1)
                        for gp in range(GP):
                            for q in range(2):
                                at = (q * GP + gp) * P
                                ins = pe.matmul(out[:, gp * HD:gp * HD + HD], o_one[:, at:at + P],
                                                c("own_pick")[:, (2 * gp + q) * HD:(2 * gp + q + 1) * HD],
                                                start=False, stop=(q == 1), skip_group_check=True)
                        done(ins, step, i)
                    elif step == "mix":
                        out = out_bank(step, i)
                        if i == 0:
                            pe.wait_ge(pooled, 4 * (l + 1))
                        done(pe.matmul(out[:, 0:T], pr("pool_w", i * P, P), h[:, PU + i, :], start=True, stop=True),
                             step, i)
                    elif step == "gate":
                        w = split_weight_at(SLOT_OF[step, i])
                        product(out_bank(step, i)[:, 0:T], w, x_tile).then_inc(slots_done, 1)
                    elif step == "merge":
                        w = split_weight_at(SLOT_OF[step, i])
                        if i == 0:
                            pe.wait_ge(y_split, len(Y_PARTS) * l + 2)
                        out = out_bank(step, i, 0)
                        product(out[:, 0:T], w, lambda k: (h_r[:, Y_A_HI + k, :], h_r[:, PU + k, :]), 0, 4)
                        out = out_bank(step, i, 1)
                        product(out[:, 0:T], w, lambda k: (h_r[:, Y_B_HI + k, :], h_r[:, CB + k, :]), 4, 4
                                ).then_inc(slots_done, 1)
                        w = split_weight_at(SLOT_OF[step, i] + 1)
                        if i == 0:
                            pe.wait_ge(y_split, len(Y_PARTS) * (l + 1))
                        out = out_bank(step, i, 2)
                        product(out[:, 0:T], w, lambda k: (h_r[:, Y_C_HI + k, :], h_r[:, Q + k, :])
                                ).then_inc(slots_done, 1)
                    elif step == "out":
                        def merge_tile(k):
                            return h_r[:, M_HI + k, :], m_lo[:, k, :]

                        if i > 1:
                            w = split_weight_at(SLOT_OF[step, i])
                            product(out_bank(step, i)[:, 0:T], w, merge_tile).then_inc(slots_done, 1)
                        elif i == 0:
                            outs = [out_bank(step, n)[:, 0:T] for n in range(2)]
                            ws = []
                            for ks in (range(0, KT8 - 1), range(KT8 - 1, KT8)):
                                for n in range(2):
                                    if n == len(ws):
                                        ws.append(split_weight_at(SLOT_OF[step, n]))
                                    for k in ks:
                                        if n == 0:
                                            pe.wait_ge(m_split, l * KT8 + k + 1)
                                        high, rest = merge_tile(k)
                                        w_high, w_rest = ws[n]
                                        pe.matmul(outs[n], w_high[:, k, :], high, start=(k == 0), stop=False)
                                        pe.matmul(outs[n], w_rest[:, k, :], high, start=False, stop=False)
                                        ins = pe.matmul(outs[n], w_high[:, k, :], rest, start=False,
                                                        stop=(k == KT8 - 1))
                                    if k == KT8 - 1:
                                        ins.then_inc(slots_done, 1)
                    elif step == "mean":
                        wait_emptied(pe, l, "out", i)
                        ins = pe.matmul(bank[SA][:, 0:T], ones[:, :], z[:, i, :], start=(i == 0), stop=(i == KT8 - 1))
                        if i == KT8 - 1:
                            ins.then_inc(mean_ready, 1)
                    elif step == "norm":
                        for k in range(KT8):
                            if k % 2 == 0:
                                pe.wait_ge(squared, l * 4 + k // 2 + 1)
                            ins = pe.matmul(bank[SB][:, 0:T], ones[:, :], m[:, k, :], start=(k == 0),
                                            stop=(k == KT8 - 1))
                        ins.then_inc(squared_sum, 1)

        @block.scalar
        def _(act):
            def round_weight(slot, d):
                act.activation(w_hi[:, d % HI_RING], ring[:, slot % RING], ACT.Copy).then_inc(w_hi_ready, 1)

            for k in range(KT8 // 2):
                if k % 2 == 0:
                    act.wait_ge(landed[k // 2], 16)
                    round_weight(k // 2, k // 2)
                act.wait_ge(x_loaded[k], 16)
                act.activation(x_hi[:, 2 * k:2 * k + 2, :], m[:, 2 * k:2 * k + 2, :], ACT.Copy
                               ).then_inc(x_hi_ready, 1)
            with act.Fori(0, DEPTH) as l:
                def emptied_by(ins, step, i, j=0):
                    ins.then_inc(emptied[FILL[step, i, j][0]], 1)

                def round_next(step, i, which=None):
                    for n, d in enumerate(SPLIT_AT.get((step, i), [])):
                        if which is not None and n != which:
                            continue
                        following, d, slot, s, _ = split_weight(d)
                        act.wait_ge(landed[s], ((l + following) * SLOTS_IN[s] + slot // RING + 1) * 16)
                        if d >= HI_RING:
                            act.wait_ge(slots_done, (l + following) * SLOTS + RING + SPLIT_SLOTS[d - HI_RING] + 1)
                        else:
                            last = max(e for e in range(SPLITS) if e % HI_RING == d)
                            act.wait_ge(slots_done, (l + following - 1) * SLOTS + RING + SPLIT_SLOTS[last] + 1)
                        round_weight(slot, d)

                for step, i in ORDER:
                    if step != "norm":
                        round_next(step, i)
                    if step == "dense":
                        wait_slot(act, l, step, i)
                        if i == LATE:
                            act.wait_ge(pooled, 4 * (l + 1))
                        if i == LATE_PV:
                            wait_filled(act, l, "pv", HEADS - 1)
                        src = bank[FILL[step, i, 0][0]][:, 0:T]
                        if i >= AZ:
                            act.activation(h[:, i, :], src, ACT.Sigmoid).then_inc(sigmoids, 1)
                        else:
                            emptied_by(act.activation(h[:, i, :], src, ACT.Sigmoid if i == NG else ACT.Copy),
                                       step, i)
                    elif step == "v_rows":
                        wait_filled(act, l, step, i)
                        src = bank[FILL[step, i, 0][0]]
                        emptied_by(act.activation(v_rows[:, i, :], src[:, :], ACT.Copy), step, i)
                    elif step in ("cmp_k", "cmp_v"):
                        wait_slot(act, l, step, i)
                        which = int(step == "cmp_v")
                        src = bank[FILL[step, i, 0][0]][:, :].rearrange("p (b t g n) -> p t b g n", b=NB, t=2, g=4)
                        for t in range(2):
                            ins = act.activation(halves[:, which, 0:NB, :, 8 * t:8 * t + 8], src[:, t], ACT.Copy)
                        emptied_by(ins, step, i, 0)
                        emptied_by(act.activation(halves[:, which, NB:NB + 2, :, :].rearrange(
                            "p s g c -> p (s g c)"), bank[FILL[step, i, 1][0]][:, 0:CMP_OWN // KT8], ACT.Copy), step, i, 1)
                    elif step == "cmp_soft":
                        act.wait_ge(cmp_shifted, l + 1)
                        act.activation(cs[:, :, :], cs[:, :, :], ACT.Exp, scale=QK).then_inc(cmp_exped, 1)
                    elif step == "cmp_turn":
                        wait_filled(act, l, step, i)
                        emptied_by(act.activation(pc_t[:, :, :].rearrange("p g t -> p (g t)"), bank[PT0][:, :],
                                                  ACT.Copy), step, i)
                    elif step == "exp":
                        act.wait_ge(max_ready, l * HEADS + i + 1)
                        if i >= 2:
                            wait_filled(act, l, "turn", i - 2, 1)
                        at = 0
                        for j, n in enumerate((2 * P, P)):
                            src = bank[(SA, SB)[j]]
                            for br in range(2):
                                ins = act.activation(probs[:, i % 2, at:at + n], src[:, br * n:br * n + n], ACT.Exp,
                                                     bias=u_max[:, i % 2, 2 * j + br:2 * j + br + 1], scale=QK,
                                                     accum_out=u_sum[:, i % 2, 2 * j + br:2 * j + br + 1])
                                at += n
                            emptied_by(ins, "scores", i, j)
                    elif step == "turn":
                        wait_filled(act, l, step, i, 0)
                        if i >= 2:
                            if i % 2:
                                wait_filled(act, l, "pv", i - 2)
                            else:
                                act.wait_ge(pv_even, l * 8 + i // 2)
                        emptied_by(act.activation(probs_t[:, i % 2, 0, :], bank[PT0][:, 0:384], ACT.Copy), step, i, 0)
                    elif step == "pv" and i % 2:
                        wait_filled(act, l, step, i)
                        emptied_by(act.activation(h[:, Q + i // 2, 0:SEQ], bank[OT][:, 0:SEQ], ACT.Copy), step, i)
                    elif step == "one_cmp_scores":
                        act.wait_ge(one_max_ready, 3 * l + 1)
                        act.activation(p_cmp[:, 0:NC], bank[SB][:, 0:NC], ACT.Exp, bias=one_max[:, 2:3], scale=QK,
                                       accum_out=one_sum[:, 2:3]).then_inc(emptied[SB], 1)
                    elif step == "one_scores":
                        act.wait_ge(one_max_ready, 3 * l + 2 + i)
                        emptied_by(act.activation(p_one[:, i, :], bank[(SA, PT0)[i]][:, 0:KEYS], ACT.Exp,
                                                  bias=one_max[:, i:i + 1], scale=QK,
                                                  accum_out=one_sum[:, i:i + 1]), step, i)
                    elif step == "one_turn":
                        wait_filled(act, l, step, i)
                        emptied_by(act.activation(p_one_t[:, i, :], bank[(PT1, SB)[i]][:, 0:2 * P], ACT.Copy), step, i)
                    elif step == "one_pv" and i == 1:
                        wait_filled(act, l, step, i)
                        emptied_by(act.activation(o_one, bank[OT][:, :], ACT.Copy), step, i)
                    elif step == "silu":
                        wait_filled(act, l, "one_scores", 1)
                        for n in (2, 3):
                            wait_emptied(act, l, "dense", PZ + 4 * i + n)
                        act.activation(z[:, 4 * i:4 * i + 4, :], h[:, PZ + 4 * i:PZ + 4 * i + 4, :], ACT.Sigmoid
                                       ).then_inc(sigmoids, 1)
                    elif step == "y_high":
                        src, dst, tiles = Y_PARTS[i]
                        act.wait_ge(y_ready, len(Y_PARTS) * l + i + 1)
                        if i == 1:
                            act.wait_ge(kv_stored, (l + 1) * 16)
                        act.activation(h_r[:, dst:dst + tiles, :], h[:, src:src + tiles, :], ACT.Copy
                                       ).then_inc(y_hi_ready, 1)
                    elif step == "gate":
                        tile, j = divmod(i, 3)
                        if tile >= GATE_RING:
                            act.wait_ge(merged, l * KT8 + tile - GATE_RING + 1)
                        wait_slot(act, l, step, i)
                        emptied_by(act.activation(g[:, tile % GATE_RING, j, :], bank[FILL[step, i, 0][0]][:, 0:T],
                                                  ACT.Sigmoid), step, i)
                    elif step == "merge":
                        act.wait_ge(merged, l * KT8 + i + 1)
                        act.activation(h_r[:, M_HI + i, :], m[:, i, :], ACT.Copy).then_inc(m_hi_ready, 1)
                    elif step == "norm":
                        for k in range(4):
                            act.wait_ge(centered, l * 4 + k + 1)
                            act.activation(m[:, 2 * k:2 * k + 2, :], z[:, 2 * k:2 * k + 2, :], ACT.Square
                                           ).then_inc(squared, 1)
                        round_next(step, i)
                        act.wait_ge(squared_sum, l + 1)
                        act.activation(rstd[:, :], bank[SB][:, 0:T], ACT.Sqrt, bias=eps[:, :]).then_inc(std_ready, 1)
                        for n in range(KT8):
                            if n % 2 == 0:
                                act.wait_ge(scaled, l * 4 + n // 2 + 1)
                            ins = act.activation(x_hi[:, n, :], z[:, n, :], ACT.Identity, bias=pr("ln_b", n, 1))
                            if n % 2:
                                ins.then_inc(x_hi_ready, 1)
            for n in range(KT8 // 2):
                ins = act.activation(m[:, n, :], z[:, n, :], ACT.Identity, bias=pr("ln_b", n, 1))
                if n % 2:
                    ins.then_inc(output_ready[0], 1)

        @block.vector
        def _(dve):
            def rest_of_weight(slot, d):
                dve.tensor_tensor(w_lo[:, slot % RING], ring[:, slot % RING], w_hi[:, d % HI_RING].bitcast(F32),
                                  ALU.subtract).then_inc(w_lo_ready, 1)

            def rest_of_input(k):
                dve.tensor_tensor(x_lo[:, 2 * k:2 * k + 2, :], m[:, 2 * k:2 * k + 2, :],
                                  x_hi[:, 2 * k:2 * k + 2, :].bitcast(F32), ALU.subtract).then_inc(x_ready, 1)

            for k in range(2):
                dve.wait_ge(w_hi_ready, k + 1)
                rest_of_weight(k, k)
            for k in range(KT8 // 2):
                dve.wait_ge(x_hi_ready, k + 1)
                rest_of_input(k)
            with dve.Fori(0, DEPTH) as l:
                steps = [0]

                def link(ins):
                    steps[0] += 1
                    ins.then_inc(vector_step, 1)
                    dve.wait_ge(vector_step, l * VECTOR_STEPS + steps[0])

                def emptied_by(ins, step, i, j=0):
                    ins.then_inc(emptied[FILL[step, i, j][0]], 1)
                    wait_emptied(dve, l, step, i, j)

                def rotate(src, psum, cos, sin, scratch):
                    dve.tensor_tensor(scratch, psum, sin, ALU.mult)
                    return dve.tensor_tensor(src, src, cos, ALU.mult)

                def rest_next(step, i, which=None):
                    for n, d in enumerate(SPLIT_AT.get((step, i), [])):
                        if which is not None and n != which:
                            continue
                        following, d, slot, _, _ = split_weight(d)
                        dve.wait_ge(w_hi_ready, (l + following) * SPLITS + d + 1)
                        rest_of_weight(slot, d)

                for step, i in ORDER:
                    if step not in ("scores", "merge", "norm"):
                        rest_next(step, i)
                    if step == "dense" and i >= AZ:
                        dve.wait_ge(sigmoids, l * SIGMOIDS + SIGMOIDS_BEFORE[step, i])
                        emptied_by(dve.tensor_tensor(h[:, i, :], h[:, i, :], bank[FILL[step, i, 0][0]][:, 0:T],
                                                     ALU.mult), step, i)
                    if step == "cmp_k":
                        dve.wait_ge(x_hi_ready, (l + 1) * (KT8 // 2))
                        dve.memset(zf[:, 0:NB * GP * 32], 0.0).then_inc(q_pad_clear, 1)
                        dve.wait_ge(q_pad_clear, l + 1)
                        dve.wait_ge(roped, (l + 1) * len(ROPED))
                        for g2 in range(2):
                            rows = slice(g2 * HD, g2 * HD + HD)
                            for gp in range(GP):
                                for q in range(2):
                                    at = q * 16 + gp * 8 + g2
                                    ins = dve.tensor_copy(
                                        q_pad[rows, 4 * q:4 * q + 4, gp, at:at + 7:2],
                                        h[rows, Q + gp * R:Q + gp * R + R, SEQ + 4 * q:SEQ + 4 * q + 4
                                          ].rearrange("p r b -> p b r"))
                        ins.then_inc(q_pad_ready, 1)
                        dve.wait_ge(q_pad_ready, l + 1)
                        wait_emptied(dve, l, "dense", NG)
                        for q in range(2):
                            ins = dve.tensor_tensor(
                                gate_d[0:48, q:NB:2, :],
                                h[0:48, NG, SEQ + 4 * q:SEQ + 4 * q + 4].unsqueeze(2).to_broadcast([48, 4, HEADS]),
                                c("gate_head")[0:48, :].unsqueeze(1).to_broadcast([48, 4, HEADS]), ALU.mult)
                        ins.then_inc(gate_d_ready, 1)
                        dve.wait_ge(gate_d_ready, l + 1)
                    if step == "rope":
                        wait_filled(dve, l, step, i)
                        emptied_by(dve.tensor_tensor(tmp[:, 0, 0:T], bank[MI][:, 0:T], c("rope_s"), ALU.mult), step, i)
                        link(dve.tensor_tensor(h[:, i, :], h[:, i, :], c("rope_c"), ALU.mult))
                        wait_emptied(dve, l, step, i)
                        dve.tensor_tensor(h[:, i, :], h[:, i, :], tmp[:, 0, 0:T], ALU.add).then_inc(roped, 1)
                        dve.wait_ge(roped, l * len(ROPED) + ROPED.index(i) + 1)
                    elif step == "v_new_in":
                        for n in (VW, VW + 1):
                            wait_emptied(dve, l, "dense", n)
                        dve.tensor_copy(v_new_c[:, :, :, :], h[:, VS:VS + 4, SEQ:T].rearrange(
                            "p (a g) b -> p g a b", a=2)).then_inc(v_new_ready, 1)
                        dve.wait_ge(v_new_ready, l + 1)
                    elif step == "v_new":
                        wait_filled(dve, l, step, i)
                        emptied_by(dve.tensor_copy(v_new[:, :], bank[SB][0:2 * NB, 0:2 * P]), step, i)
                    elif step == "gates":
                        wait_filled(dve, l, step, i)
                        link(dve.tensor_copy(gate[:, 0:96].rearrange("p (q n) -> p q n", q=2),
                                             bank[MI][:, 0:2 * P].rearrange("p (q n) -> p q n", q=2)[:, :, 0:48]))
                        emptied_by(dve.tensor_copy(gate[:, 96:99], bank[MI][:, 2 * P:2 * P + 3]), step, i)
                    elif step == "cmp_swap":
                        if i == 0:
                            dve.wait_ge(params_loaded, (l + 1) * 16)
                        own = (cache_a, cache_b)[i][:, CMP_CACHED:CMP_CACHED + CMP_OWN].rearrange(
                            "p (u g c s) -> p u g c s", u=2, g=4, c=CT)
                        wait_filled(dve, l, step, i)
                        for gp in range(GP):
                            for j in range(2):
                                rows = slice(j * HD, j * HD + HD)
                                dve.tensor_copy(own[rows, 0, 2 * gp + j, :, :],
                                                h[rows, (KC, VC)[i] + gp, 0:SEQ].rearrange(
                                                    "p (c j s) -> p j c s", c=CT, j=2)[:, j])
                                ins = dve.tensor_copy(own[rows, 0, 2 * gp + 1 - j, :, :],
                                                      bank[MI][rows, gp * SEQ:(gp + 1) * SEQ].rearrange(
                                                          "p (c j s) -> p j c s", c=CT, j=2)[:, j])
                        emptied_by(ins, step, i)
                        dve.tensor_copy(own[:, 1, :, 0:2, :], pr(("pe_k", "pe_v")[i]).rearrange(
                            "p (c s) -> p c s", c=2).unsqueeze(1).to_broadcast([P, 4, 2, KT8])
                            ).then_inc(cmp_in_ready, 1)
                        dve.wait_ge(cmp_in_ready, 2 * l + 1 + i)
                    elif step == "cmp_sum":
                        which = i
                        b = FILL[step, i, 0][0]
                        wait_filled(dve, l, step, i)
                        link(dve.tensor_copy(bias[:, which:which + 1], bank[b][:, 18 * NC:18 * NC + 1]))
                        out = (vc_all if which else kc_all)[:, :, :, 0:NC].rearrange("p g s c -> p s g c")
                        src = bank[b][:, 0:18 * NC].rearrange("p (s g c) -> p s g c", g=GP, c=NC)
                        for gp in range(GP):
                            ins = dve.tensor_scalar(out[:, :, gp, :], src[:, :, gp, :], bias[:, which:which + 1], None,
                                                    ALU.add)
                            if gp == 0:
                                link(ins)
                        emptied_by(ins, step, i)
                        if which:
                            dve.tensor_copy(vc_rep[:, :, :, :], vc_all[:, :, NB, :].unsqueeze(2).to_broadcast(
                                [P, GP, 8, CT])).then_inc(cmp_out_ready, 1)
                            dve.wait_ge(cmp_out_ready, l + 1)
                    elif step == "cmp_rope":
                        wait_filled(dve, l, step, i)
                        flat = kc_all[:, :, :, :].rearrange("p g s c -> p (g s) c")
                        rot = tmp[:, 0, :].rearrange("p (n c) -> p n c", c=CT)
                        emptied_by(dve.tensor_tensor(rot, bank[MI][:, 0:288].rearrange("p (n c) -> p n c", c=CT),
                                                     c("cmp_s").unsqueeze(1).to_broadcast([P, 18, CT]), ALU.mult),
                                   step, i)
                        link(dve.tensor_tensor(flat, flat, c("cmp_c").unsqueeze(1).to_broadcast([P, 18, CT]),
                                               ALU.mult))
                        wait_emptied(dve, l, step, i)
                        link(dve.tensor_tensor(flat, flat, rot, ALU.add))
                        for g2 in range(2):
                            rows = slice(g2 * HD, g2 * HD + HD)
                            ins = dve.tensor_copy(kc_bd[rows, :, g2, :], kc_all[rows, :, NB, :])
                        ins.then_inc(kc_ready, 1)
                        dve.wait_ge(kc_ready, l + 1)
                    elif step == "cmp_vrows":
                        wait_filled(dve, l, step, i)
                        for gp in range(GP):
                            dve.tensor_tensor(vc_bd[:, gp, :, :],
                                              bank[SB][:, gp * P:gp * P + P].unsqueeze(1).to_broadcast([P, R, P]),
                                              c("own_head").rearrange("p (r n) -> p r n", r=R), ALU.mult)
                        emptied_by(dve.tensor_copy(vc_one[:, :, :].rearrange("p g n -> p (g n)"),
                                                   bank[SB][:, 2 * P:4 * P]), step, i)
                    elif step == "cmp_scores":
                        wait_filled(dve, l, step, i)
                        mask = c("cmp_mask").rearrange("p (q c) -> p q c", q=2)
                        for qi in range(2):
                            ins = dve.tensor_tensor(cs[:, qi * 16:qi * 16 + 16, :], bank[SA][:, qi * 256:qi * 256 + 256]
                                                    .rearrange("p (n c) -> p n c", c=CT),
                                                    mask[:, qi, :].unsqueeze(1).to_broadcast([P, 16, CT]), ALU.add)
                            if qi == 0:
                                link(ins)
                        emptied_by(ins, step, i)
                        wait_emptied(dve, l, step, i)
                        link(dve.tensor_reduce(c_max[:, :], cs[:, :, :], AX_X, ALU.max))
                        link(dve.tensor_scalar(c_max[:, :], c_max[:, :], FLOOR, None, ALU.max))
                        dve.tensor_tensor(cs[:, :, :], cs[:, :, :], c_max[:, :].unsqueeze(2).to_broadcast([P, 32, CT]),
                                          ALU.subtract).then_inc(cmp_shifted, 1)
                        dve.wait_ge(cmp_shifted, l + 1)
                    elif step == "cmp_soft":
                        dve.wait_ge(cmp_exped, l + 1)
                        link(dve.tensor_reduce(c_sum[:, :], cs[:, :, :], AX_X, ALU.add))
                        link(dve.tensor_scalar(c_sum[:, :], c_sum[:, :], 1e-30, None, ALU.max))
                        link(dve.reciprocal(c_sum[:, :], c_sum[:, :]))
                        wait_emptied(dve, l, "gates", 0)
                        link(dve.tensor_tensor(c_sum[:, :].rearrange("p (q n) -> p q n", q=2),
                                               c_sum[:, :].rearrange("p (q n) -> p q n", q=2),
                                               gate[:, 0:96].rearrange("p (q n) -> p q n", q=2)[:, :, 0:16], ALU.mult))
                        dve.tensor_tensor(cs[:, :, :], cs[:, :, :], c_sum[:, :].unsqueeze(2).to_broadcast([P, 32, CT]),
                                          ALU.mult).then_inc(cmp_probs, 1)
                        dve.wait_ge(cmp_probs, l + 1)
                    elif step == "scores":
                        for j, n in enumerate((2 * P, P)):
                            wait_filled(dve, l, step, i, j)
                            link(dve.tensor_reduce(u_fac[:, i % 2, 2 * j:2 * j + 2],
                                                   bank[(SA, SB)[j]][:, 0:2 * n].rearrange("p (a n) -> p a n", a=2),
                                                   AX_X, ALU.max))
                        dve.tensor_scalar(u_max[:, i % 2, :], u_fac[:, i % 2, :], -QK, None, ALU.mult
                                          ).then_inc(max_ready, 1)
                        dve.wait_ge(max_ready, l * HEADS + i + 1)
                    elif step == "exp":
                        rest_next("scores", i)
                    elif step == "scale":
                        if i == HEADS // 2:
                            wait_slot(dve, l, "cmp_k", 0)
                            dve.tensor_copy(k_one[:, :, :, PAST], h[:, KS:KS + 2, SEQ:T].rearrange("p g b -> p b g")
                                            ).then_inc(k_new_ready, 1)
                            dve.wait_ge(k_new_ready, 2 * l + 1)
                        wait_emptied(dve, l, "scores", i, 0)
                        wait_emptied(dve, l, "scores", i, 1)
                        fac = u_fac[:, i % 2, :]
                        link(dve.tensor_scalar(fac, u_sum[:, i % 2, :], 1e-30, None, ALU.max))
                        link(dve.reciprocal(fac, fac))
                        link(dve.tensor_tensor(fac.rearrange("p (q a) -> p q a", q=2),
                                               fac.rearrange("p (q a) -> p q a", q=2),
                                               gate[:, 0:96].rearrange("p (q a n) -> p q a n", q=2, a=3)[:, :, 1:3, i],
                                               ALU.mult))
                        at = 0
                        for j, n in enumerate((256, 256, 128, 128)):
                            ins = dve.tensor_scalar(probs[:, i % 2, at:at + n], probs[:, i % 2, at:at + n],
                                                    u_fac[:, i % 2, j:j + 1], None, ALU.mult)
                            at += n
                        ins.then_inc(probs_ready, 1)
                        dve.wait_ge(probs_ready, l * HEADS + i + 1)
                    elif step == "turn":
                        wait_filled(dve, l, step, i, 1)
                        if i >= 2:
                            if i % 2:
                                wait_filled(dve, l, "pv", i - 2)
                            else:
                                dve.wait_ge(pv_even, l * 8 + i // 2)
                        emptied_by(dve.tensor_copy(probs_t[:, i % 2, 1, :], bank[PT1][:, 0:384]), step, i, 1)
                    elif step == "pool" and i == 0:
                        for n in (PU + 2, PU + 3):
                            wait_emptied(dve, l, "dense", n)
                        dve.memset(pu_ext[:, :, 0:HIST], 0.0)
                        dve.tensor_copy(pu_ext[:, :, HIST:NE], h[:, PU:PU + 4, 0:SEQ])
                        dve.tensor_copy(pu_one[:, :, :, 0:HIST], pr("pool_hist").rearrange(
                            "p (g b t) -> p g b t", g=4, b=NB))
                        dve.tensor_copy(pu_one[:, :, :, HIST], h[:, PU:PU + 4, SEQ:T]).then_inc(state_ready, 1)
                        dve.wait_ge(state_ready, 2 * l + 1)
                    elif step == "pool" and i <= 3:
                        for k in ((0,), (1,), (2, 3))[i - 1]:
                            src, to = (sum_a, sum_b)[(k - 1) % 2] if k else pu_ext, (sum_a, sum_b)[k % 2]
                            shift = 2 ** k
                            first = 2 * shift - 1
                            link(dve.tensor_tensor(to[:, k:4, first:NE], src[:, k:4, first:NE],
                                                   src[:, k:4, first - shift:NE - shift], ALU.add))
                    elif step == "pool":
                        k = i - 4
                        w = WINDOWS[k]
                        sums = (sum_a, sum_b)[k % 2]
                        link(dve.scalar_tensor_tensor(out=h[:, PU + k, 0:SEQ], in0=sums[:, k, HIST:NE],
                                                      scalar=1.0 / w, in1=pu_ext[:, k, HIST:NE], op0=ALU.mult,
                                                      op1=ALU.subtract))
                        dve.tensor_tensor(tmp[:, 0, k * CT:k * CT + CT], sums[:, k, HIST:HIST + CT],
                                          c("inv_count")[:, k * CT:k * CT + CT], ALU.mult)
                        link(dve.tensor_reduce(pu_sum[:, k, :], pu_one[:, k, :, HIST + 1 - w:HIST + 1], AX_X,
                                               ALU.add))
                        dve.tensor_tensor(h[:, PU + k, 0:CT], tmp[:, 0, k * CT:k * CT + CT],
                                          pu_ext[:, k, HIST:HIST + CT], ALU.subtract)
                        dve.scalar_tensor_tensor(out=h[:, PU + k, SEQ:T], in0=pu_sum[:, k, :], scalar=1.0 / w,
                                                 in1=pu_one[:, k, :, HIST], op0=ALU.mult, op1=ALU.subtract
                                                 ).then_inc(pooled, 1)
                        dve.wait_ge(pooled, 4 * l + k + 1)
                    elif step == "conv" and i == 0:
                        for n in (CX + 2, CX + 3):
                            wait_emptied(dve, l, "dense", n)
                        dve.wait_ge(state_staged, 2 * l + 1)
                        dve.memset(hc_ext[:, :, 0:2], 0.0)
                        dve.tensor_tensor(hc_ext[:, :, 2:2 + SEQ], h[:, CC:CC + 4, 0:SEQ], h[:, CX:CX + 4, 0:SEQ],
                                          ALU.mult)
                        dve.tensor_copy(hc_one[:, :, 0:2, :], pr("conv_hist").rearrange("p (g j b) -> p g j b",
                                                                                       g=4, j=2))
                        dve.tensor_tensor(hc_one[:, :, 2, :], h[:, CC:CC + 4, SEQ:T], h[:, CX:CX + 4, SEQ:T],
                                          ALU.mult).then_inc(state_ready, 1)
                        dve.wait_ge(state_ready, 2 * l + 2)
                    elif step == "conv" and i <= 3:
                        j = i - 1
                        for k in range(4):
                            w = pr("conv_w", k * 3 + j, 1)
                            for dst, src in ((h[:, CC + k, 0:SEQ], hc_ext[:, k, j:j + SEQ]),
                                             (h[:, CC + k, SEQ:T], hc_one[:, k, j, :])):
                                if j == 0:
                                    ins = dve.tensor_scalar(dst, src, w, None, ALU.mult)
                                else:
                                    ins = dve.scalar_tensor_tensor(out=dst, in0=src, scalar=w, in1=dst,
                                                                   op0=ALU.mult, op1=ALU.add)
                        link(ins)
                    elif step == "conv":
                        dve.tensor_tensor(h[:, CB:CB + 4, :], h[:, CB:CB + 4, :], h[:, CC:CC + 4, :], ALU.mult
                                          ).then_inc(convolved, 1)
                        dve.wait_ge(convolved, l + 1)
                    elif step == "one_cmp_scores":
                        wait_filled(dve, l, step, i)
                        link(dve.tensor_reduce(one_max[:, 2:3], bank[SB][:, 0:NC], AX_X, ALU.max))
                        dve.tensor_scalar(one_max[:, 2:3], one_max[:, 2:3], -QK, None, ALU.mult
                                          ).then_inc(one_max_ready, 1)
                        dve.wait_ge(one_max_ready, 3 * l + 1)
                        wait_emptied(dve, l, step, i)
                        link(dve.tensor_scalar(one_sum[:, 2:3], one_sum[:, 2:3], 1e-30, None, ALU.max))
                        link(dve.reciprocal(one_sum[:, 2:3], one_sum[:, 2:3]))
                        link(dve.tensor_tensor(one_sum[:, 2:3], one_sum[:, 2:3], gate[:, 96:97], ALU.mult))
                        link(dve.tensor_scalar(p_cmp[:, :], p_cmp[:, :], one_sum[:, 2:3], None, ALU.mult))
                        link(dve.tensor_tensor(p_cmp_x[:, :, :], p_cmp[:, :].unsqueeze(1).to_broadcast([P, NB, CT]),
                                               c("own_row").unsqueeze(2).to_broadcast([P, NB, CT]), ALU.mult))
                    elif step == "one_scores":
                        src = bank[(SA, PT0)[i]]
                        wait_filled(dve, l, step, i)
                        link(dve.tensor_reduce(one_max[:, i:i + 1], src[:, 0:KEYS], AX_X, ALU.max))
                        dve.tensor_scalar(one_max[:, i:i + 1], one_max[:, i:i + 1], -QK, None, ALU.mult
                                          ).then_inc(one_max_ready, 1)
                        dve.wait_ge(one_max_ready, 3 * l + 2 + i)
                        if i == 0:
                            dve.tensor_copy(k_one[:, :, :, PAST], h[:, KW:KW + 2, SEQ:T].rearrange("p g b -> p b g")
                                            ).then_inc(k_new_ready, 1)
                            dve.wait_ge(k_new_ready, 2 * l + 2)
                        wait_emptied(dve, l, step, i)
                        link(dve.tensor_scalar(one_sum[:, i:i + 1], one_sum[:, i:i + 1], 1e-30, None, ALU.max))
                        link(dve.reciprocal(one_sum[:, i:i + 1], one_sum[:, i:i + 1]))
                        link(dve.tensor_tensor(one_sum[:, i:i + 1], one_sum[:, i:i + 1], gate[:, 97 + i:98 + i],
                                               ALU.mult))
                        link(dve.tensor_scalar(p_one[:, i, :], p_one[:, i, :], one_sum[:, i:i + 1], None, ALU.mult))
                        dve.tensor_scalar(p_tail[:, i, :], c("own_row"), p_one[:, i, PAST:KEYS], None, ALU.mult
                                          ).then_inc(one_probs, 1)
                        dve.wait_ge(one_probs, 2 * l + i + 1)
                    elif step == "one_cmp_turn":
                        wait_filled(dve, l, step, i)
                        link(dve.tensor_copy(p_cmp_t[:, :], bank[MI][:, 0:P]))
                        emptied_by(dve.tensor_copy(p_tail_t[:, :], bank[MI][0:2 * NB, P:2 * P]), step, i)
                    elif step == "one_out":
                        wait_filled(dve, l, step, i)
                        for g2 in range(2):
                            rows = slice(g2 * HD, g2 * HD + HD)
                            for gp in range(GP):
                                src = bank[MI][rows, gp * HD:gp * HD + HD].rearrange(
                                    "p (b q r a) -> p a r q b", b=4, q=2, a=2)[:, g2]
                                dst = h[rows, Q + gp * R:Q + gp * R + R, SEQ:T].rearrange(
                                    "p r (q b) -> p r q b", q=2)
                                ins = dve.tensor_copy(dst, src)
                                if (g2, gp) != (1, GP - 1):
                                    link(ins)
                        emptied_by(ins, step, i)
                    elif step == "silu":
                        dve.wait_ge(sigmoids, l * SIGMOIDS + SIGMOIDS_BEFORE[step, i])
                        tiles = h[:, PZ + 4 * i:PZ + 4 * i + 4, :]
                        link(dve.tensor_tensor(tiles, z[:, 4 * i:4 * i + 4, :], tiles, ALU.mult))
                    elif step == "mix":
                        wait_filled(dve, l, step, i)
                        emptied_by(dve.scalar_tensor_tensor(out=h[:, PU + i, :], in0=bank[FILL[step, i, 0][0]][:, 0:T],
                                                            scalar=pr("pool_scale", i, 1), in1=h[:, PZ + i, :],
                                                            op0=ALU.mult, op1=ALU.mult), step, i)
                        if i == 3:
                            dve.sem_inc(y_ready, 1)
                    elif step == "y":
                        src, _, tiles = Y_PARTS[i]
                        gates = CZ if i == 0 else AZ + 2 * (i - 2)
                        if i == 2:
                            wait_emptied(dve, l, "pv", HEADS - 1)
                        ins = dve.tensor_tensor(h[:, src:src + tiles, :], h[:, src:src + tiles, :],
                                                h[:, gates:gates + tiles, :], ALU.mult)
                        ins.then_inc(y_ready, 1)
                        dve.wait_ge(y_ready, len(Y_PARTS) * l + i + 1)
                    elif step == "y_rest":
                        lo, hi, tiles = Y_PARTS[i]
                        dve.wait_ge(y_hi_ready, len(Y_PARTS) * l + i + 1)
                        dve.tensor_tensor(h_r[:, lo:lo + tiles, :], h[:, lo:lo + tiles, :],
                                          h_r[:, hi:hi + tiles, :].bitcast(F32), ALU.subtract).then_inc(y_split, 1)
                    elif step == "merge":
                        rest_next(step, i, 0)
                        for j in range(3):
                            wait_emptied(dve, l, "gate", 3 * i + j)
                        wait_slot(dve, l, step, i, 0)
                        banks = [bank[FILL[step, i, j][0]] for j in range(3)]
                        emptied_by(dve.tensor_tensor(m[:, i, :], g[:, i % GATE_RING, 0, :], banks[0][:, 0:T], ALU.mult),
                                   step, i, 0)
                        emptied_by(dve.tensor_tensor(tmp[:, 0, 0:T], g[:, i % GATE_RING, 1, :], banks[1][:, 0:T], ALU.mult),
                                   step, i, 1)
                        wait_emptied(dve, l, step, i, 0)
                        wait_emptied(dve, l, step, i, 1)
                        link(dve.tensor_tensor(m[:, i, :], m[:, i, :], tmp[:, 0, 0:T], ALU.add))
                        rest_next(step, i, 1)
                        wait_slot(dve, l, step, i, 1)
                        emptied_by(dve.tensor_tensor(tmp[:, 1, 0:T], g[:, i % GATE_RING, 2, :], banks[2][:, 0:T], ALU.mult),
                                   step, i, 2)
                        wait_emptied(dve, l, step, i, 2)
                        dve.tensor_tensor(m[:, i, :], m[:, i, :], tmp[:, 1, 0:T], ALU.add).then_inc(merged, 1)
                        dve.wait_ge(merged, l * KT8 + i + 1)
                        dve.wait_ge(m_hi_ready, l * KT8 + i + 1)
                        dve.tensor_tensor(m_lo[:, i, :], m[:, i, :], h_r[:, M_HI + i, :].bitcast(F32), ALU.subtract
                                          ).then_inc(m_split, 1)
                    elif step == "out":
                        dve.tensor_tensor(z[:, i, :], x_hi[:, i, :].bitcast(F32), x_lo[:, i, :].bitcast(F32),
                                          ALU.add).then_inc(residual, 1)
                        dve.wait_ge(residual, l * KT8 + i + 1)
                        wait_slot(dve, l, step, i)
                        emptied_by(dve.scalar_tensor_tensor(out=z[:, i, :], in0=z[:, i, :], scalar=ALPHA,
                                                            in1=bank[FILL[step, i, 0][0]][:, 0:T],
                                                            op0=ALU.mult, op1=ALU.add), step, i)
                    elif step == "norm":
                        dve.wait_ge(mean_ready, l + 1)
                        wait_emptied(dve, l, "out", KT8 - 1)
                        wait_emptied(dve, l, "out", KT8 - 2)
                        for k in range(4):
                            part = z[:, 2 * k:2 * k + 2, :]
                            dve.tensor_tensor(part, part, bank[SA][:, 0:T].unsqueeze(1).to_broadcast([P, 2, T]),
                                              ALU.subtract).then_inc(centered, 1)
                            dve.wait_ge(centered, l * 4 + k + 1)
                        rest_next(step, i)
                        dve.wait_ge(std_ready, l + 1)
                        link(dve.reciprocal(rstd[:, :], rstd[:, :]))
                        dve.wait_ge(state_stored, (l + 1) * 16)
                        for k in range(4):
                            for n in (2 * k, 2 * k + 1):
                                ins = dve.scalar_tensor_tensor(out=z[:, n, :], in0=z[:, n, :],
                                                               scalar=pr("ln_g", n, 1), in1=rstd[:, :],
                                                               op0=ALU.mult, op1=ALU.mult)
                            ins.then_inc(scaled, 1)
                        dve.wait_ge(scaled, (l + 1) * 4)
                        for k in range(4):
                            dve.wait_ge(x_hi_ready, (l + 1) * 4 + k + 1)
                            for n in (2 * k, 2 * k + 1):
                                ins = dve.scalar_tensor_tensor(out=x_lo[:, n, :], in0=z[:, n, :],
                                                               scalar=pr("ln_b", n, 1),
                                                               in1=x_hi[:, n, :].bitcast(F32),
                                                               op0=ALU.add, op1=ALU.subtract)
                            ins.then_inc(x_ready, 1)
                        dve.wait_ge(x_ready, (l + 2) * 4)
                assert steps[0] == VECTOR_STEPS, f"VECTOR_STEPS is {steps[0]}"
            for n in range(KT8 // 2, KT8):
                ins = dve.tensor_scalar(m[:, n, :], z[:, n, :], pr("ln_b", n, 1), None, ALU.add)
                if n % 2:
                    ins.then_inc(output_ready[1], 1)


def _constants():
    t = {k: np.zeros((P, n), np.float32) for k, (_, n) in CST.items()}
    half = 8
    inv = (1.0 / (500000.0 ** (np.arange(0, 16, 2, dtype=np.float32) / 16))).astype(np.float32)
    pos = np.concatenate([np.arange(SEQ), np.full(NB, PAST)]).astype(np.float32)
    cpos = (np.arange(NC) * CT + TAPS - 1).astype(np.float32)
    for cos, sin, at in (("rope_c", "rope_s", pos), ("cmp_c", "cmp_s", cpos)):
        ang = (at[None, :] * inv[:, None]).astype(np.float32).astype(np.float64)
        n = len(at)
        t[cos][:, 0:n] = 1.0
        for g2 in range(2):
            a = g2 * HD
            t[cos][a:a + half, 0:n] = np.cos(ang)
            t[cos][a + half:a + 2 * half, 0:n] = np.cos(ang)
            t[sin][a:a + half, 0:n] = -np.sin(ang)
            t[sin][a + half:a + 2 * half, 0:n] = np.sin(ang)
    for g2 in range(2):
        for d in range(half):
            t["perm"][g2 * HD + d, g2 * HD + d + half] = 1.0
            t["perm"][g2 * HD + d + half, g2 * HD + d] = 1.0
    t["ident"] = np.eye(P, dtype=np.float32)
    q = np.arange(P)
    t["causal"] = np.where(q[None, :] <= q[:, None], 0.0, MASKED).astype(np.float32)
    end = np.arange(CT) * CT + TAPS - 1
    for qi in range(2):
        rows = q + (1 - qi) * P
        ok = (end[None, :] <= rows[:, None]) & (np.arange(CT)[None, :] < NC)
        t["cmp_mask"][:, qi * CT:(qi + 1) * CT] = np.where(ok, 0.0, MASKED)
    t["own_row"] = ((q // 32 + 4 * (q // 16 % 2))[:, None] == np.arange(NB)[None, :]).astype(np.float32)
    r_of, g_of = q // 32, q // CT % 2
    for r in range(R):
        t["own_head"][:, r * P:(r + 1) * P] = ((r_of == r)[:, None] & (g_of[:, None] == (q // HD)[None, :]))
    for k, w in enumerate(WINDOWS):
        t["inv_count"][:, k * CT:(k + 1) * CT] = (1.0 / np.minimum(w, np.arange(CT) + 1)).astype(np.float32)
    t["gate_head"] = (q[:, None] % HEADS == np.arange(HEADS)[None, :]).astype(np.float32)
    for gp in range(GP):
        for n in range(2):
            ok = (q // 16 % 2 == n) & (q // 8 % 2 == gp)
            own = (q // 16)[:, None] * 8 + (q % 8)[:, None] == np.arange(HD)[None, :]
            t["own_pick"][:, (2 * gp + n) * HD:(2 * gp + n + 1) * HD] = ok[:, None] & own
    t["gate_type"] = (q[:, None] // HEADS == np.arange(3)[None, :]).astype(np.float32)
    return np.concatenate([t[k] for k in CST], axis=1).astype(np.float32)


def kernel(**inputs):
    import concourse.bacc as _bacc
    from concourse.bass_utils import run_bass_kernel_spmd as _run

    a = {k: np.asarray(v) for k, v in inputs.items()}
    D = DEPTH

    def tiles(w):
        _, kk, n = w.shape
        return w.reshape(D, kk // P, P, n // P, P).transpose(0, 3, 2, 1, 4).reshape(D, n // P, P, kk // P * P)

    sizes = (512, 512, 512, 512, 512, 512, 1024, 256, 256, 256, 256, 256, 256, 48, 1024, 3072)
    at = dict(zip(("pu", "pz", "cb", "cc", "cx", "cz", "q", "kc", "vc", "ks", "vs", "kw", "vw", "ng", "az", "mg"),
                  np.concatenate([[0], np.cumsum(sizes)[:-1]])))
    head = np.arange(HEADS).reshape(GP, 2, R).transpose(0, 2, 1).reshape(-1)
    by_head = (head[:, None] * HD + np.arange(HD)[None, :]).reshape(-1)
    w_in = a["w_in"]

    def part(name, n):
        return w_in[:, :, at[name]:at[name] + n]

    ng = np.zeros((D, D_MODEL, P), np.float32)
    ng[:, :, 0:48] = w_in[:, :, at["ng"] + (head[None, :] * 3 + np.arange(3)[:, None]).reshape(-1)]
    first = tiles(np.concatenate([part("kc", 256), part("vc", 256), part("ks", 256), part("kw", 256),
                                  part("vs", 256), part("vw", 256), w_in[:, :, at["q"] + by_head], ng], axis=2))
    second = tiles(np.concatenate([part("pu", 512), part("cb", 512), part("cc", 512), part("cx", 512),
                                   part("pz", 512), part("cz", 512), w_in[:, :, at["az"] + by_head]], axis=2))
    taps = a["cmp_w"].reshape(D, 2, TAPS, HD, HD).transpose(0, 1, 3, 2, 4)
    cmp = taps.reshape(D, 2, HD, 2, 2, KT8, HD).transpose(0, 1, 4, 2, 5, 3, 6).reshape(D, 2, P, KT8 * P)
    mg = tiles(part("mg", 3072)).reshape(D, 3, KT8, P, 8 * P)
    ab = np.concatenate([tiles(a["proj_a"]), tiles(a["proj_b"])], axis=3)
    pc = tiles(a["proj_c"][:, by_head, :])
    out_w = tiles(a["w_out"])
    dense = np.concatenate([first, second], axis=1)
    rows = {"dense": lambda i: [dense[:, i]], "cmp_k": lambda i: [cmp[:, 0]],
            "cmp_v": lambda i: [cmp[:, 1]], "gate": lambda i: [mg[:, i % 3, i // 3]],
            "merge": lambda i: [ab[:, i], pc[:, i]], "out": lambda i: [out_w[:, i]]}
    weights = np.stack([row for step, i in ORDER if step in rows for row in rows[step](i)], axis=1)
    weights = np.concatenate([weights.reshape(D * SLOTS, P, KT8 * P), weights[0, 0:2]], axis=0)

    def by_part(v, n):
        return v.reshape(D, n, P).transpose(0, 2, 1)

    pe = a["cmp_pe"].reshape(D, 2, 2, 2, KT8, HD).transpose(0, 1, 3, 5, 2, 4).reshape(D, 2, P, CT)
    params = np.concatenate([
        by_part(a["pool_scale"], 4),
        a["conv_w"].reshape(D, 3, 4, P).transpose(0, 3, 2, 1).reshape(D, P, 12),
        by_part(a["ln_g"], 8), by_part(a["ln_b"], 8), pe[:, 0], pe[:, 1],
        a["state_pool"].reshape(D, NB, HIST, 4, P).transpose(0, 4, 3, 1, 2).reshape(D, P, -1),
        a["state_conv"].reshape(D, NB, 2, 4, P).transpose(0, 4, 3, 2, 1).reshape(D, P, -1),
        a["pool_w"].transpose(0, 2, 1, 3).reshape(D, P, 4 * P)], axis=2)
    xs = np.concatenate([a["x_prompt"].reshape(SEQ, D_MODEL), a["x_sample"].reshape(NB, D_MODEL)], axis=0)
    pool_n = a["cache_k_cmp"].shape[1]

    def cache_cols(v):
        return v.reshape(D, pool_n, P, GP, P).transpose(0, 1, 4, 3, 2)

    def cache_chunks(v):
        return v.reshape(D, pool_n, KT8, 2, KT8, 4, HD).transpose(0, 1, 3, 6, 5, 2, 4).reshape(D, pool_n, P, 4 * HD)

    arrays = {
        "x_in": xs.T.reshape(KT8, P, T).transpose(1, 0, 2), "weights": weights, "params": params,
        "consts": _constants(), "pages": a["page_table"].reshape(1, -1).astype(np.int32),
        "kcmp": cache_chunks(a["cache_k_cmp"]), "vcmp": cache_chunks(a["cache_v_cmp"]),
        "ksel": cache_cols(a["cache_k_sel"]), "vsel": a["cache_v_sel"].reshape(D, pool_n, P, 4 * HD),
        "kwin": a["state_k_win"].reshape(D, NB, PAST, GP, P).transpose(0, 4, 1, 3, 2).reshape(D, P, NB * GP, PAST),
        "vwin": a["state_v_win"].reshape(D, NB, 2, P, 4 * HD).transpose(0, 3, 1, 2, 4).reshape(D, P, -1),
    }
    outs = {"y": (P, KT8, T), "kv": (D, P, 12, T), "state": (D, P, N_ST),
            "kwin_out": (D, P, NB * GP, PAST), "vwin_out": (D, P, NB * 4 * HD * 2)}
    nc = _bacc.Bacc("TRN2", target_bir_lowering=False, num_devices=1)
    args = []
    for name in arrays:
        arrays[name] = np.ascontiguousarray(arrays[name])
        args.append(nc.dram_tensor(name + "_dram", arrays[name].shape, mybir.dt.from_np(arrays[name].dtype),
                                   kind="ExternalInput").ap())
    for name, shape in outs.items():
        args.append(nc.dram_tensor(name + "_dram", shape, F32, kind="ExternalOutput").ap())
    trunk(nc, *args)
    got = _run(nc, [{name + "_dram": v for name, v in arrays.items()}], core_ids=[0]).results[0]
    got = {name: got[name + "_dram"] for name in outs}

    y = np.asarray(got["y"]).transpose(2, 1, 0).reshape(T, D_MODEL)
    kv = np.asarray(got["kv"]).reshape(D, P, 6, GP, T).transpose(2, 0, 4, 3, 1).reshape(6, D, T, 4, HD)
    kc, vc, ks, kw, vs, vw = (kv[n] for n in range(6))
    st = np.asarray(got["state"])

    def p_of(v):
        return v[:, 0:SEQ].reshape(D, 1, SEQ, 4, HD)

    def s_of(v):
        return v[:, SEQ:T].reshape(D, NB, 1, 4, HD)

    kwo = np.asarray(got["kwin_out"]).reshape(D, P, NB, GP, PAST).transpose(0, 2, 4, 3, 1).reshape(D, NB, PAST, 4, HD)
    vwo = np.asarray(got["vwin_out"]).reshape(D, P, NB, 2, 4 * HD).transpose(0, 2, 3, 1, 4).reshape(
        D, NB, PAST, 4, HD)
    p_pool = st[:, :, ST_PP:ST_PS].reshape(D, P, 4, HIST).transpose(0, 3, 2, 1).reshape(D, 1, HIST, 512)
    s_pool = st[:, :, ST_PS:ST_CP].reshape(D, P, 4, NB, HIST).transpose(0, 3, 4, 2, 1).reshape(D, NB, HIST, 512)
    p_conv = st[:, :, ST_CP:ST_CS].reshape(D, P, 4, 2).transpose(0, 3, 2, 1).reshape(D, 1, 2, 512)
    s_conv = st[:, :, ST_CS:N_ST].reshape(D, P, 4, 2, NB).transpose(0, 4, 3, 2, 1).reshape(D, NB, 2, 512)
    out = (y[0:SEQ].reshape(1, SEQ, D_MODEL), y[SEQ:T].reshape(NB, 1, D_MODEL),
           p_of(kc), p_of(vc), p_of(ks), p_of(vs), p_of(kw), p_of(vw), p_pool, p_conv,
           s_of(kc), s_of(vc), s_of(ks), s_of(vs),
           np.concatenate([kwo, s_of(kw)], axis=2), np.concatenate([vwo, s_of(vw)], axis=2), s_pool, s_conv)
    return tuple(np.ascontiguousarray(v) for v in out)
```
